# Optimizing a Trainium2 kernel written in Bass

```python
import math
import jax, jax.numpy as jnp
from jax import lax
import numpy as np

D_MODEL = 1024
BATCH = 1
SEQ = 256
DEPTH = 2

GRID_W = 64
CTX_LEN = 256
HEAD_DIM = 64
HA = 4
DA = HEAD_DIM
HB = 8
KVB = 2
GB = HB // KVB
DH = HEAD_DIM
WINDOW = 128
BLOCK = 128
ROPE_BASE = 10000.0
N_EXPERTS = 16
N_GROUPS = 4
EXPERTS_PER_GROUP = N_EXPERTS // N_GROUPS
TOP_K = 2
D_EXPERT = 512
MOE_CHUNK = 128
EPS = 1e-6
NEG = -1e30

D_QA = HA * 2 * DA
D_VA = HA * 2 * DA
D_QB = HB * DH
D_KB = KVB * DH
D_IN = 2 * D_QA + D_VA + D_QB + 2 * D_KB
D_MIX_OUT = HA * 2 * DA + HB * DH
SPLITS = (D_QA, 2 * D_QA, 2 * D_QA + D_VA, 2 * D_QA + D_VA + D_QB, 2 * D_QA + D_VA + D_QB + D_KB)

kernel_name = "hybrid_diffattn_swa_moe_dit_block"

def rmsnorm(x, g):
    xf = x.astype(jnp.float32)
    y = xf * lax.rsqrt(jnp.mean(xf * xf, axis=-1, keepdims=True) + EPS)
    return (y * g.astype(jnp.float32)).astype(x.dtype)

def axial_rope_tables(n):
    rows = n // GRID_W
    row = jnp.broadcast_to(jnp.arange(rows)[:, None], (rows, GRID_W)).reshape(-1)
    col = jnp.broadcast_to(jnp.arange(GRID_W)[None, :], (rows, GRID_W)).reshape(-1)
    n_freq = HEAD_DIM // 4
    inv = 1.0 / (ROPE_BASE ** (jnp.arange(n_freq, dtype=jnp.float32) / n_freq))
    ang = jnp.stack([row, col], axis=-1).astype(jnp.float32)[:, :, None] * inv
    return jnp.cos(ang), jnp.sin(ang)

def apply_rope(x, cos, sin):
    xs = x.reshape(*x.shape[:-1], 2, 2, HEAD_DIM // 4)
    x1, x2 = xs[..., 0, :], xs[..., 1, :]
    cs = cos[:, None].astype(x.dtype)
    sn = sin[:, None].astype(x.dtype)
    out = jnp.stack([x1 * cs - x2 * sn, x2 * cs + x1 * sn], axis=-2)
    return out.reshape(x.shape)

def split_heads(p):
    B, n, _ = p.shape
    qa, ka, va, qb, kb, vb = jnp.split(p, list(SPLITS), axis=-1)
    qa = qa.reshape(B, n, HA, 2, DA)
    ka = ka.reshape(B, n, HA, 2, DA)
    return (qa[..., 0, :], qa[..., 1, :], ka[..., 0, :], ka[..., 1, :],
            va.reshape(B, n, HA, 2 * DA), qb.reshape(B, n, HB, DH),
            kb.reshape(B, n, KVB, DH), vb.reshape(B, n, KVB, DH))

def diff_mix(q1, q2, k1, k2, v, lam):
    scale = DA ** -0.5
    s1 = jnp.einsum('bqhd,bkhd->bhqk', q1, k1).astype(jnp.float32) * scale
    s2 = jnp.einsum('bqhd,bkhd->bhqk', q2, k2).astype(jnp.float32) * scale
    a = (jax.nn.softmax(s1, axis=-1) - lam * jax.nn.softmax(s2, axis=-1)).astype(v.dtype)
    return jnp.einsum('bhqk,bkhe->bqhe', a, v)

def sink_attend(q, k, v, bias, sink):
    B, Q = q.shape[0], q.shape[1]
    qg = q.reshape(B, Q, KVB, GB, DH)
    s = jnp.einsum('bqhgd,bkhd->bhgqk', qg, k).astype(jnp.float32) * (DH ** -0.5)
    if bias is not None:
        s = s + bias
    sk = jnp.broadcast_to(sink.astype(jnp.float32).reshape(1, KVB, GB, 1, 1), s.shape[:-1] + (1,))
    p = jax.nn.softmax(jnp.concatenate([s, sk], axis=-1), axis=-1)[..., :-1]
    o = jnp.einsum('bhgqk,bkhd->bqhgd', p.astype(v.dtype), v)
    return o.reshape(B, Q, HB * DH)

def latent_mixers(h, ctx_kv, w_in_l, lam, lam_init, subln_l, sink_l, cos, sin):
    B, n, _ = h.shape
    nblk = n // BLOCK
    cka1, cka2, cva, ckb, cvb = ctx_kv
    qa1, qa2, ka1, ka2, va, qb, kb, vb = split_heads(h @ w_in_l)
    qa1, qa2, ka1, ka2, qb, kb = (apply_rope(t, cos, sin) for t in (qa1, qa2, ka1, ka2, qb, kb))

    def to_blocks(t):
        return jnp.moveaxis(t.reshape(B, nblk, BLOCK, *t.shape[2:]), 1, 0)

    def from_blocks(t):
        return jnp.moveaxis(t, 0, 1).reshape(B, n, -1)

    k1 = jnp.concatenate([cka1, ka1], axis=1)
    k2 = jnp.concatenate([cka2, ka2], axis=1)
    v_a = jnp.concatenate([cva, va], axis=1)
    oa = lax.map(lambda qs: diff_mix(qs[0], qs[1], k1, k2, v_a, lam), (to_blocks(qa1), to_blocks(qa2)))
    oa = from_blocks(oa).reshape(B, n, HA, 2 * DA)
    oa = rmsnorm(oa, subln_l) * (1.0 - lam_init)

    def windows(t):
        tp = jnp.pad(t, ((0, 0), (BLOCK, BLOCK), (0, 0), (0, 0))).reshape(B, nblk + 2, BLOCK, KVB, DH)
        return jnp.moveaxis(jnp.concatenate([tp[:, :-2], tp[:, 1:-1], tp[:, 2:]], axis=2), 1, 0)

    q_off = jnp.arange(BLOCK)
    k_off = jnp.arange(3 * BLOCK) - BLOCK
    ctx_bias = jnp.zeros((BLOCK, ckb.shape[1]), jnp.float32)

    def win_block(args):
        qblk, kw, vw, i = args
        qpos = i * BLOCK + q_off
        kpos = i * BLOCK + k_off
        valid = ((jnp.abs(qpos[:, None] - kpos[None, :]) <= WINDOW)
                 & (kpos >= 0)[None, :] & (kpos < n)[None, :])
        bias = jnp.concatenate([jnp.where(valid, 0.0, NEG).astype(jnp.float32), ctx_bias], axis=-1)
        k = jnp.concatenate([kw, ckb], axis=1)
        v = jnp.concatenate([vw, cvb], axis=1)
        return sink_attend(qblk, k, v, bias, sink_l)

    ob = lax.map(win_block, (to_blocks(qb), windows(kb), windows(vb), jnp.arange(nblk)))
    ob = from_blocks(ob)
    return jnp.concatenate([oa.reshape(B, n, HA * 2 * DA), ob], axis=-1)

def route(h_flat, w_router, b_router):
    s = jax.nn.sigmoid((h_flat @ w_router).astype(jnp.float32))
    sb = s + b_router.astype(jnp.float32)
    gscore = lax.top_k(sb.reshape(-1, N_GROUPS, EXPERTS_PER_GROUP), TOP_K)[0].sum(-1)
    gsel = jnp.argmax(gscore, axis=-1)
    in_group = (jnp.arange(N_EXPERTS) // EXPERTS_PER_GROUP)[None, :] == gsel[:, None]
    _, idx = lax.top_k(jnp.where(in_group, sb, -jnp.inf), TOP_K)
    w = jnp.take_along_axis(s, idx, axis=-1)
    w = w / jnp.sum(w, axis=-1, keepdims=True)
    return jnp.sum(jax.nn.one_hot(idx, N_EXPERTS, dtype=jnp.float32) * w[..., None], axis=1)

def moe(h, w_router, b_router, w1_l, w3_l, w2_l):
    shp = h.shape
    hf = h.reshape(-1, D_MODEL)
    comb = route(hf, w_router, b_router).astype(h.dtype)

    def chunk(args):
        xc, gc = args
        a = jnp.einsum('td,edf->tef', xc, w1_l)
        b = jnp.einsum('td,edf->tef', xc, w3_l)
        u = jax.nn.silu(a) * b * gc[..., None]
        return jnp.einsum('tef,efd->td', u, w2_l)

    y = lax.map(chunk, (hf.reshape(-1, MOE_CHUNK, D_MODEL), comb.reshape(-1, MOE_CHUNK, N_EXPERTS)))
    return y.reshape(shp)

def setup_inputs(seed: int = 0) -> dict:
    key = jax.random.key(seed)
    ks = jax.random.split(key, 20)

    def nrm(k, shape, s):
        return jax.random.normal(k, shape, jnp.float32) * s

    return {
        "x": nrm(ks[0], (BATCH, SEQ, D_MODEL), 1.0),
        "c": nrm(ks[1], (BATCH, D_MODEL), 1.0),
        "ctx": nrm(ks[2], (BATCH, CTX_LEN, D_MODEL), 1.0),
        "c_ctx": nrm(ks[3], (D_MODEL,), 1.0),
        "w_ada": nrm(ks[4], (DEPTH, D_MODEL, 6 * D_MODEL), 0.5 * D_MODEL ** -0.5),
        "b_ada": nrm(ks[5], (DEPTH, 6 * D_MODEL), 0.02),
        "norm_attn": 1.0 + nrm(ks[6], (DEPTH, D_MODEL), 0.05),
        "norm_ffn": 1.0 + nrm(ks[7], (DEPTH, D_MODEL), 0.05),
        "w_in": nrm(ks[8], (DEPTH, D_MODEL, D_IN), D_MODEL ** -0.5),
        "w_out": nrm(ks[9], (DEPTH, D_MIX_OUT, D_MODEL), D_MIX_OUT ** -0.5),
        "lambda_qk": nrm(ks[10], (DEPTH, 4, DA), 0.1),
        "subln": 1.0 + nrm(ks[11], (DEPTH, 2 * DA), 0.05),
        "sink": nrm(ks[12], (DEPTH, HB), 0.5),
        "w_router": nrm(ks[13], (D_MODEL, N_EXPERTS), D_MODEL ** -0.5),
        "b_router": nrm(ks[14], (N_EXPERTS,), 0.01),
        "w1": nrm(ks[15], (DEPTH, N_EXPERTS, D_MODEL, D_EXPERT), D_MODEL ** -0.5),
        "w3": nrm(ks[16], (DEPTH, N_EXPERTS, D_MODEL, D_EXPERT), D_MODEL ** -0.5),
        "w2": nrm(ks[17], (DEPTH, N_EXPERTS, D_EXPERT, D_MODEL), D_EXPERT ** -0.5),
        "norm_final": 1.0 + nrm(ks[18], (D_MODEL,), 0.05),
    }

def reference(x, c, ctx, c_ctx, w_ada, b_ada, norm_attn, norm_ffn, w_in, w_out, lambda_qk, subln,
              sink, w_router, b_router, w1, w3, w2, norm_final):
    B, n, _ = x.shape
    cos, sin = axial_rope_tables(n)
    h_c = ctx
    for l in range(DEPTH):
        last = l == DEPTH - 1
        mod = (jax.nn.silu(c) @ w_ada[l] + b_ada[l])[:, None, :]
        mod_c = (jax.nn.silu(c_ctx) @ w_ada[l] + b_ada[l])[None, None, :]
        sh_a, sc_a, g_a, sh_f, sc_f, g_f = jnp.split(mod, 6, axis=-1)
        csh_a, csc_a, cg_a, csh_f, csc_f, cg_f = jnp.split(mod_c, 6, axis=-1)
        lam_init = 0.8 - 0.6 * math.exp(-0.3 * l)
        lq1, lk1, lq2, lk2 = (lambda_qk[l, i].astype(jnp.float32) for i in range(4))
        lam = jnp.exp(jnp.sum(lq1 * lk1)) - jnp.exp(jnp.sum(lq2 * lk2)) + lam_init

        hc = rmsnorm(h_c, norm_attn[l]) * (1 + csc_a) + csh_a
        cqa1, cqa2, cka1, cka2, cva, cqb, ckb, cvb = split_heads(hc @ w_in[l])

        hx = rmsnorm(x, norm_attn[l]) * (1 + sc_a) + sh_a
        mix = latent_mixers(hx, (cka1, cka2, cva, ckb, cvb), w_in[l], lam, lam_init, subln[l], sink[l], cos, sin)
        x = x + g_a * (mix @ w_out[l])
        hx = rmsnorm(x, norm_ffn[l]) * (1 + sc_f) + sh_f
        x = x + g_f * moe(hx, w_router, b_router, w1[l], w3[l], w2[l])

        if not last:
            oa_c = rmsnorm(diff_mix(cqa1, cqa2, cka1, cka2, cva, lam), subln[l]) * (1.0 - lam_init)
            ob_c = sink_attend(cqb, ckb, cvb, None, sink[l])
            mix_c = jnp.concatenate([oa_c.reshape(B, -1, HA * 2 * DA), ob_c], axis=-1)
            h_c = h_c + cg_a * (mix_c @ w_out[l])
            hc = rmsnorm(h_c, norm_ffn[l]) * (1 + csc_f) + csh_f
            h_c = h_c + cg_f * moe(hc, w_router, b_router, w1[l], w3[l], w2[l])
    return rmsnorm(x, norm_final)


_drawn_inputs = setup_inputs


def setup_inputs(seed=0):
    import zlib

    import numpy as np

    out = dict(_drawn_inputs(seed))
    spreads = {}
    factors = {'lambda_qk': 3.661, 'sink': 24.006, 'subln': 2.9}
    for name, (base, spread) in spreads.items():
        noise = np.random.default_rng([zlib.crc32(name.encode()), seed]).standard_normal(out[name].shape)
        drawn = base * np.exp(spread * noise) if base else spread * noise
        out[name] = __import__('jax').numpy.asarray(drawn.astype(out[name].dtype))
    for name, factor in factors.items():
        out[name] = (out[name] * factor).astype(out[name].dtype)
    return out
```

```python
import math
from contextlib import ExitStack

import numpy as np
import concourse.bass as bass
from concourse import mybir

P = 128
DM, SEQ, CTX, DEPTH = 1024, 256, 256, 2
GRID_W = 64
HA, HB, KVB, DH = 4, 8, 2, 64
NE, NG, EPG, TOPK, DE = 16, 4, 4, 2, 512
EPS, NEG = 1e-6, -1e30
ROPE_BASE = 10000.0
KC = DM // P
TT = (SEQ + CTX) // P
LT = SEQ // P
TOK = SEQ + CTX
D_IN = 2304
N_ADA = 6 * DM // 512
TILE = 64
MAXT = TOK // TILE
SLOTCOLS = 4096
SCALE = DH ** -0.5

C_ID, C_TRI, C_MB, C_ROPE = 0, 128, 256, 512
C_DEC, C_DECG, C_EB, C_TOK, C_H, C_THR = 768, 784, 788, 804, 808, 809
C_BEF = C_THR + MAXT - 1
C_ALL = C_BEF + NE * NE


def constants():
    c = np.zeros((P, C_ALL), np.float32)
    r = np.arange(P)
    c[:, C_ID:C_ID + P] = np.eye(P)
    c[:, C_TRI:C_TRI + P] = r[:, None] < r[None, :]
    c[:, C_MB:C_MB + P] = np.where(r[None, :] <= r[:, None], 0.0, NEG)
    c[:, C_MB + P:C_MB + 2 * P] = np.where(r[None, :] >= r[:, None], 0.0, NEG)
    n_freq = DH // 4
    inv = (1.0 / (ROPE_BASE ** (np.arange(n_freq, dtype=np.float32) / np.float32(n_freq)))).astype(np.float32)
    pos = np.arange(SEQ)
    ang = np.stack([pos // GRID_W, pos % GRID_W], -1).astype(np.float32)[:, :, None] * inv
    cos, sin = np.cos(ang), np.sin(ang)
    full_cos = np.stack([cos, cos], 2).reshape(LT, P, DH)
    full_sin = np.stack([-sin, sin], 2).reshape(LT, P, DH)
    for t in range(LT):
        c[:, C_ROPE + 128 * t:C_ROPE + 128 * t + 64] = full_cos[t]
        c[:, C_ROPE + 128 * t + 64:C_ROPE + 128 * t + 128] = full_sin[t]
    c[:, C_DEC:C_DEC + NE] = EPG - np.arange(NE) % EPG
    c[:, C_DECG:C_DECG + NG] = NG - np.arange(NG)
    c[:, C_EB:C_EB + NE] = np.arange(NE) * TOK
    c[:, C_TOK:C_TOK + TT] = r[:, None] + P * np.arange(TT)[None, :]
    c[:, C_H] = r // 64
    c[:, C_THR:C_BEF] = TILE * np.arange(1, MAXT)
    c[:, C_BEF:C_ALL] = (np.arange(NE)[None, :] < np.arange(NE)[:, None]).reshape(-1)
    return c


class Chain:

    def __init__(self, eng, sem):
        self.eng, self.sem, self.n = eng, sem, 0

    def step(self, ins):
        ins.then_inc(self.sem, 1)
        self.n += 1
        self.eng.wait_ge(self.sem, self.n)


def build(nc, a):
    f32, bf16, i32 = mybir.dt.float32, mybir.dt.bfloat16, mybir.dt.int32
    ALU, ACT, AX = mybir.AluOpType, mybir.ActivationFunctionType, mybir.AxisListType
    ds = bass.ds

    mod_d = nc.dram_tensor("mod_d", [DEPTH, 2, 6 * DM], f32).ap()
    h_d = [nc.dram_tensor(f"h_d{l}", [TOK, DM], f32).ap() for l in range(DEPTH)]
    list_d = [nc.dram_tensor(f"list_d{l}", [NE * TOK, 1], f32).ap() for l in range(DEPTH)]
    y_d = [nc.dram_tensor(f"y_d{l}", [TOPK * P * (TT if l == 0 else LT) + TOK, DM], f32).ap() for l in range(DEPTH)]

    qtiles = [list(range(TT)), list(range(LT))]
    UNITS = ["ka", "va", "kvb", "qa", "qb"]
    UCOL = {"qa": (0, 512), "ka": (512, 512), "va": (1024, 512), "qb": (1536, 512), "kvb": (2048, 256)}
    PROJ = [(l, u, t) for l in range(DEPTH) for u in UNITS
            for t in (range(TT) if u in ("ka", "va", "kvb") else qtiles[l])]
    by_dve = lambda u, t: t < LT and u != "va"
    POST = {True: [s for s in PROJ if by_dve(s[1], s[2])], False: [s for s in PROJ if not by_dve(s[1], s[2])]}
    TR = [s for s in PROJ if s[1] != "va"]
    ATT = [(l, qt, kind, j) for l in range(DEPTH) for qt in qtiles[l] for kind in ("diff", "gqa") for j in (0, 1)]
    WOUT = [(l, t, n) for l in range(DEPTH) for t in qtiles[l] for n in (0, 1)]
    ADA = [(l, n) for l in range(DEPTH) for n in range(N_ADA)]
    first_ada = 4
    heads_in = {"diff": 2, "gqa": 4}

    att0 = [n for n, u in enumerate(ATT) if u[0] == 0]
    rest = list(range(first_ada, len(ADA)))
    ada_at = {n: [] for n in range(len(ATT))}
    for i, x in enumerate(rest):
        ada_at[att0[i * len(att0) // len(rest)]].append(x)

    TU = ["c"]
    for l in range(DEPTH):
        TU += [("mod", l)] + [("hT", l, k) for k in range(KC)]
        TU += [("tr",) + s for s in TR if s[0] == l]
        units = [n for n, u in enumerate(ATT) if u[0] == l]
        for i, n in enumerate(units):
            TU += [("att", n, c) for c in range(heads_in[ATT[n][2]])]
            if i % 4 == 0 and i:
                TU += [("mix", l, ATT[n][1] - 1, h) for h in (0, 1)]
        TU += [("mix", l, qtiles[l][-1], h) for h in (0, 1)]
        TU += [("rt", l, t, h) for t in qtiles[l] for h in (0, 1)]
        TU += [("list", l)]
    tix = {key: i for i, key in enumerate(TU)}

    RS, col = {}, 0
    rs_order = []
    for l in range(DEPTH):
        evs = [("attn", l, TT, DM)] + [("sub", l, qt, HA, 128) for qt in qtiles[l]] + \
              [("ffn", l, t, 1, DM) for t in qtiles[l]]
        if l == DEPTH - 1:
            evs += [("fin", LT, DM)]
        for e in evs:
            RS[e[:-2]] = (col, e[-2], e[-1], len(rs_order))
            rs_order.append(e[:-2])
            col += e[-2]
    n_rs = col

    with ExitStack() as ctx:
        def sb(name, shape, dt=f32):
            return ctx.enter_context(nc.sbuf_tensor(name, shape, dt))

        def sem(name):
            return ctx.enter_context(nc.semaphore(name))

        ring = sb("ring", [P, 6, SLOTCOLS])
        X = sb("X", [P, TT, DM])
        hT = sb("hT", [P, KC, TOK])
        R2 = sb("R2", [P, 9728])
        R3 = sb("R3", [P, 5120])
        modrow = sb("modrow", [P, DEPTH * N_ADA, 128])
        cst = sb("cst", [P, C_ALL])
        wr = sb("wr", [P, KC, NE])
        tmp = sb("tmp", [P, 512])
        subb = sb("subb", [P, DEPTH, 128])
        modT = sb("modT", [40, 128])
        mc = sb("mc", [P, 40])
        Ac = sb("Ac", [P, 2, KC])
        cs = sb("cs", [P, KC, 2])
        craw = sb("craw", [P, 16])
        cth = sb("cth", [P, 16])
        ssq = sb("ssq", [P, n_rs])
        rstd = sb("rstd", [P, n_rs])
        sinkb = sb("sinkb", [P, DEPTH, HB])
        nsink = sb("nsink", [P, DEPTH, HB])
        broutb = sb("broutb", [P, NE])
        mhalf = sb("mhalf", [P, 4])
        nlam = sb("nlam", [P, DEPTH])
        lsum = sb("lsum", [P, 2 * DEPTH])
        lexp = sb("lexp", [P, 2 * DEPTH])
        rm = sb("rm", [P, 4])
        negm = sb("negm", [P, 4])
        sdif = sb("sdif", [P, 4])
        sexp = sb("sexp", [P, 2, 4])
        sums = sb("sums", [P, 2, 4])
        rec = sb("rec", [P, 2, 4])
        gate = sb("gate", [P, 2, TT])
        slot_ix = sb("slot_ix", [P, DEPTH, 2, TT], i32)
        row_ix = sb("row_ix", [P, DEPTH, 2, TT], i32)
        ntile = sb("ntile", [P, DEPTH, NE], i32)
        first_row = sb("first_row", [P, DEPTH, NE], i32)
        ix1 = sb("ix1", [P, 1], i32)

        kaT = R2[:, 0:2048].rearrange("p (c t) -> p c t", c=4)
        qaT = R2[:, 2048:4096].rearrange("p (c t) -> p c t", c=4)
        qbT = R2[:, 4096:6144].rearrange("p (c t) -> p c t", c=4)
        kbT = R2[:, 6144:7168].rearrange("p (c t) -> p c t", c=2)
        Va = R2[:, 7168:9216].rearrange("p (t n) -> p t n", t=TT)
        Vb = R2[:, 9216:9728].rearrange("p (t n) -> p t n", t=TT)
        xn = R2[:, 2048:6144].rearrange("p (t n) -> p t n", t=TT)
        gA = R2[:, 0:2048].rearrange("p (s n) -> p s n", s=2)
        gF = R2[:, 2048:4096].rearrange("p (s n) -> p s n", s=2)
        Af = R2[:, 4096:6144].rearrange("p (s n) -> p s n", s=2)
        Bf = R2[:, 6144:8192].rearrange("p (s n) -> p s n", s=2)
        nfb = R2[:, 8192:9216]
        yk = R2[:, 4096:8192].rearrange("p (b k n) -> p b k n", b=2, k=2)
        rope_t1, rope_t2 = R3[:, 0:512], R3[:, 512:1024]
        stage = R3[:, 1024:2048].rearrange("p (b n) -> p b n", b=2)
        Pm = R3[:, 0:2048].rearrange("p (b n) -> p b n", b=4)
        PT = R3[:, 2048:4096].rearrange("p (b k q) -> p b k q", b=4, k=4)
        mix = R3[:, 4096:5120]
        hTs = R3[:, 0:1024].rearrange("p (k t) -> p k t", k=KC)
        junk = R3[:, 1024:2048]
        hb = R3[:, 2560:4608].rearrange("p (b n) -> p b n", b=2)
        lamb = R3[:, 0:512].rearrange("p (l i d) -> p l i d", l=DEPTH, i=4)
        lprod = R3[:, 512:768].rearrange("p (l i d) -> p l i d", l=DEPTH, i=2)
        crow = R3[0:16, 768:896]
        zlist = R3[:, 896:960]
        lst = R3[:, 2048:2176].rearrange("p (h s) -> p h s", h=2)
        xg, xT = R3[:, 0:512], R3[:, 512:1024].rearrange("p (j t) -> p j t", j=4)
        th, t2, u_s = R3[:, 1024:1280], R3[:, 1280:1536], R3[:, 1536:1792]
        uT = R3[:, 1792:2048].rearrange("p (c t) -> p c t", c=2)
        y_s = R3[:, 2048:2560]
        g_ix = R3[:, 4608:4736].bitcast(i32)
        tri_b = R3[:, 4736:4800].bitcast(bf16)
        one_b = R3[:, 4800:4864].bitcast(bf16)
        mask_b = R3[:, 4864:4896].bitcast(bf16)
        ident = cst[:, C_ID:C_ID + P]

        S = ctx.enter_context(nc.psum_tensor("S", [P, 4, 512], f32))
        T = [ctx.enter_context(nc.psum_tensor(f"T{i}", [P, 512], f32)) for i in range(2)]
        O = ctx.enter_context(nc.psum_tensor("O", [P, 512], f32))
        AUX = ctx.enter_context(nc.psum_tensor("AUX", [P, 512], f32))

        slot_full = [sem(f"slot_full{i}") for i in range(6)]
        names = """consts_in x_in small_in router_in bias_in clear_done bank_clear zero_list list_zeroed c_ready
            ada_done ada_out mod_stored0 mod_stored1 mod_stored2 modT_in coeff_ready proj_done post_dve post_act t_full t_free_act
            t_free_dve act_ssq dve_ssq rstd_ready xn_ready scores_done negm_ready exps_done norm_done
            pv_done o_out mix_ready wout_done wout_out ga_in ab_in gf_in nfin_in ab_ready h_ready h_stored0 h_stored1
            logits_done sig_done mask_ready ranks_done counts_done slots_ready list_scattered list_in
            gix_ready ix_ready x_gathered xtr_done xT_ready up1_done up3_done tanh_done t2_done ua_done ub_done
            uta_done utb_done ea_done eb_done down_done y_out y_stored expert_done y_gathered0 y_gathered1 comb_done
            dve_self act_self pool_self lam_dot lam_exp fin_ready out_stored""".split()
        s = {n: sem(n) for n in names}
        t_free = [s["t_free_act"], s["t_free_dve"]]

        loads, where, last, count = [], {}, {}, [0] * 6

        def load(key, slot, src):
            count[slot] += 16
            loads.append((key, slot, src, last.get(slot)))
            where[key] = (slot, count[slot])

        def cols(w, c0, n):
            return w[:, c0:c0 + n].rearrange("(k p) n -> p k n", p=P)

        def load_ada(x, slot):
            l, n = ADA[x]
            load(("ada", x), slot, cols(a["w_ada"][l], 512 * n, 512))
            last[slot] = (s["ada_done"], x + 1)

        def load_in(l, u, slot):
            load(("in", l, u), slot, cols(a["w_in"][l], *UCOL[u]))
            t_last = max(i for i, st in enumerate(PROJ) if st[:2] == (l, u))
            last[slot] = (s["proj_done"], t_last + 1)

        def load_out(l, n, slot):
            load(("out", l, n), slot, cols(a["w_out"][l], 512 * n, 512))
            last[slot] = (s["wout_done"], 1 + max(i for i, st in enumerate(WOUT) if st[0] == l))

        def expert_src(l, e, part):
            w = a[("w1", "w3", "w2")[part]]
            if isinstance(e, int):
                one = w[l, e]
            else:
                one = w[l, ds(e, 1)].rearrange("a k n -> (a k) n")
            return one.rearrange("(k p) n -> p k n", p=P)

        def load_expert(l, e, part):
            load(("e", l, e, part), 3 * (e % 2) + part, expert_src(l, e, part))

        for x in range(first_ada):
            load_ada(x, x)
        for u, slot in zip(UNITS, (4, 5, 0, 1, 2)):
            load_in(0, u, slot)
        for i, x in enumerate(rest):
            load_ada(x, 3 + i % 3)
            if i == 2:
                for part in range(3):
                    load_expert(0, 0, part)
        for n in (0, 1):
            load_out(0, n, 3 + (len(rest) + n) % 3)
        loads.append("rows0")
        for part in range(3):
            load_expert(0, 1, part)
        loads.append("experts0")
        for i in range(6):
            count[i] += 16 * (NE // 2 - 1)
            last[i] = (s["expert_done"], NE - 1 if i < 3 else NE)
        for u, slot in zip(UNITS, (0, 1, 2, 3, 4)):
            load_in(1, u, slot)
        load_out(1, 0, 5)
        for part in range(3):
            load_expert(1, 0, part)
        load_out(1, 1, 4)
        load_expert(1, 1, 0)
        loads.append("rows1")
        for part in (1, 2):
            load_expert(1, 1, part)
        loads.append("experts1")

        def slot_view(slot, k):
            return ring[:, slot, :].rearrange("p (k n) -> p k n", k=k)

        block = ctx.enter_context(nc.Block())

        @block.sync
        def _(sp):
            def rows(l):
                streams = (0, 1) if l == 0 else (0,)
                sp.wait_ge(s["mod_stored1" if l == 0 else "mod_stored2"], 16 * 4)
                n_att = 1 + max(n for n, u in enumerate(ATT) if u[0] == l)
                sp.wait_ge(s["pv_done"], n_att)
                for i in streams:
                    sp.dma_start(gA[:, i, :], mod_d[l, i, 2 * DM:3 * DM].partition_broadcast(P)).then_inc(s["ga_in"], 16)
                for i in streams:
                    sp.dma_start(Af[:, i, :], mod_d[l, i, 4 * DM:5 * DM].partition_broadcast(P)).then_inc(s["ab_in"], 16)
                    sp.dma_start(Bf[:, i, :], mod_d[l, i, 3 * DM:4 * DM].partition_broadcast(P)).then_inc(s["ab_in"], 16)
                sp.dma_start(nfb, a["norm_ffn"][l].partition_broadcast(P)).then_inc(s["ab_in"], 16)
                for i in streams:
                    sp.dma_start(gF[:, i, :], mod_d[l, i, 5 * DM:6 * DM].partition_broadcast(P)).then_inc(s["gf_in"], 16)

            for item in loads:
                if item in ("rows0", "rows1"):
                    rows(int(item[-1]))
                elif item in ("experts0", "experts1"):
                    l = int(item[-1])
                    with sp.Fori(1, NE // 2) as pair:
                        for half in range(2):
                            sp.wait_ge(s["expert_done"], 2 * pair + (NE * l + half - 1))
                            for part in range(3):
                                slot = 3 * half + part
                                dst = slot_view(slot, 4 if part == 2 else 8)
                                sp.dma_start(dst, expert_src(l, 2 * pair + half, part)).then_inc(slot_full[slot], 16)
                else:
                    key, slot, src, free = item
                    if free is not None:
                        sp.wait_ge(*free)
                    k, n = src.shape[1], src.shape[2]
                    dst = ring[:, slot, 0:k * n].rearrange("p (k n) -> p k n", k=k)
                    sp.dma_start(dst, src).then_inc(slot_full[slot], 16)
            sp.wait_ge(s["ab_ready"], 2)
            sp.dma_start(nfb, a["norm_final"].partition_broadcast(P)).then_inc(s["nfin_in"], 16)
            for t in range(LT):
                sp.wait_ge(s["fin_ready"], t + 1)
                sp.dma_start(a["out"][0, t * P:(t + 1) * P, :], X[:, t, :]).then_inc(s["out_stored"], 16)
            sp.wait_ge(s["out_stored"], 16 * LT)

        @block.gpsimd
        def _(pool):
            self_ = Chain(pool, s["pool_self"])
            pool.memset(mhalf[:, :], -0.5)
            pool.memset(zlist, 0.0).then_inc(s["zero_list"], 1)
            pool.wait_ge(s["zero_list"], 1)
            for l in range(DEPTH):
                pool.dma_start(list_d[l].rearrange("(p c) o -> p (c o)", p=P), zlist).then_inc(s["list_zeroed"], 16)
            pool.wait_ge(s["clear_done"], 1)
            for l in range(DEPTH):
                src = a["b_ada"][l].rearrange("(n q c) -> q n c", q=4, c=128)
                for q in range(4):
                    for i in range(2):
                        pool.dma_start(modrow[32 * q + i:32 * q + i + 1, l * N_ADA:(l + 1) * N_ADA, :],
                                       src[q:q + 1]).then_inc(s["bias_in"], 16)

            def rsqrt(key):
                c0, w, n, i = RS[key]
                self_.step(pool.tensor_scalar(rstd[:, c0:c0 + w], ssq[:, c0:c0 + w], 1.0 / n, EPS, ALU.mult, ALU.add))
                pool.tensor_tensor(rstd[:, c0:c0 + w], rstd[:, c0:c0 + w], mhalf[:, 0:w], ALU.pow).then_inc(s["rstd_ready"], 1)

            def store_mod(l, n0, n1, stored):
                pool.wait_ge(s["ada_out"], l * N_ADA + n1)
                for q in range(4):
                    dst = mod_d[l].rearrange("i (n q c) -> q i n c", q=4, c=128)[q, :, n0:n1, :]
                    pool.dma_start(dst, modrow[32 * q:32 * q + 2, l * N_ADA + n0:l * N_ADA + n1, :]).then_inc(s[stored], 16)

            def load_modT(l):
                for i in range(2):
                    pool.dma_start(modT[16 * i:16 * i + 16, :],
                                   mod_d[l, i, 0:2 * DM].rearrange("(r c) -> r c", c=128)).then_inc(s["modT_in"], 16)
                pool.dma_start(modT[32:40, :], a["norm_attn"][l].rearrange("(r c) -> r c", c=128)).then_inc(s["modT_in"], 16)

            n_items = pool.alloc_register("pool_items")
            pool.reg_mov(n_items, 0)
            have, stored = pool.alloc_register("pool_have"), pool.alloc_register("pool_stored")
            n_ssq = 0
            for l in range(DEPTH):
                n_ssq += TT
                if l == 0:
                    store_mod(0, 0, first_ada, "mod_stored0")
                    pool.wait_ge(s["mod_stored0"], 16 * 4)
                else:
                    pool.wait_ge(s["mod_stored2"], 16 * 4)
                    pool.wait_ge(s["t_full"], tix[("mod", 0)] + 1)
                load_modT(l)
                pool.wait_ge(s["act_ssq"], n_ssq)
                rsqrt(("attn", l))
                for i, qt in enumerate(qtiles[l]):
                    pool.wait_ge(s["dve_ssq"], 1 + i + (0 if l == 0 else len(qtiles[0])))
                    rsqrt(("sub", l, qt))
                if l == 0:
                    store_mod(0, first_ada, N_ADA, "mod_stored1")
                    store_mod(1, 0, N_ADA, "mod_stored2")
                for t in qtiles[l]:
                    n_ssq += 1
                    pool.wait_ge(s["act_ssq"], n_ssq)
                    rsqrt(("ffn", l, t))
                pool.wait_ge(s["list_zeroed"], 16 * DEPTH)
                pool.wait_ge(s["slots_ready"], l + 1)
                base = 32 * (0 if l == 0 else len(qtiles[0]))
                for t in qtiles[l]:
                    for k in range(2):
                        pool.indirect_dma_start(
                            out=list_d[l], out_offset=bass.IndirectOffsetOnAxis(ap=slot_ix[:, l, k, t:t + 1], axis=0),
                            in_=cst[:, C_TOK + t:C_TOK + t + 1], in_offset=None).then_inc(s["list_scattered"], 16)
                pool.wait_ge(s["list_scattered"], base + 32 * len(qtiles[l]))
                for h in range(2):
                    pool.dma_start(lst[:, h, :], list_d[l].rearrange("(p c) o -> p (c o)", p=P)).then_inc(s["list_in"], 16)
                pool.wait_ge(s["gix_ready"], l + 1)
                for b in range(2):
                    pool.wait_ge(s[f"h_stored{b}"], 8 * (len(qtiles[0]) + (len(qtiles[1]) if l else 0)))
                rows_of_h = h_d[l][0:P * len(qtiles[l]), :].rearrange("t (h d) -> (t h) d", h=2)

                def gather(column, gathers):
                    pool.reg_mov(have, gathers + 1)
                    pool.wait_ge(s["gix_ready"], l + 1)
                    pool.wait_ge(s["xtr_done"], have)
                    pool.tensor_copy(ix1[:, :], g_ix[:, column]).then_inc(s["ix_ready"], 1)
                    pool.wait_ge(s["gix_ready"], l + 1)
                    pool.wait_ge(s["ix_ready"], have)
                    pool.indirect_dma_start(
                        out=xg, out_offset=None, in_=rows_of_h,
                        in_offset=bass.IndirectOffsetOnAxis(ap=ix1[:, 0:1], axis=0)).then_inc(s["x_gathered"], 16)

                with pool.Fori(0, NE) as e:
                    n = pool.value_load(ntile[0:1, l, ds(e, 1)], min_val=1, max_val=MAXT)
                    with pool.Fori(0, n) as t:
                        g = pool.snap(n_items, min_val=0, max_val=64)
                        gather(ds(e * MAXT + t, 1), g + l)
                        pool.reg_add(n_items, n_items, 1)
                g = pool.snap(n_items, min_val=1, max_val=64)
                gather(slice(0, 1), g + l)
                pool.reg_mov(stored, 32 * g)
                pool.wait_ge(s["gix_ready"], l + 1)
                pool.wait_ge(s["y_stored"], stored)
                done = 0 if l == 0 else len(qtiles[0])
                for i, t in enumerate(qtiles[l]):
                    if i >= 2:
                        pool.wait_ge(s["comb_done"], done + i - 1)
                    for k in range(2):
                        pool.indirect_dma_start(
                            out=yk[:, i % 2, k, :], out_offset=None, in_=y_d[l][0:TOPK * P * len(qtiles[l]), :],
                            in_offset=bass.IndirectOffsetOnAxis(ap=row_ix[:, l, k, t:t + 1], axis=0)
                        ).then_inc(s[f"y_gathered{i % 2}"], 16)
            n_ssq += LT
            pool.wait_ge(s["act_ssq"], n_ssq)
            rsqrt(("fin",))

        @block.scalar
        def _(act):
            act.dma_start(cst[:, :], a["consts"]).then_inc(s["consts_in"], 16)
            act.dma_start(crow[0:8, :], a["c"][0].rearrange("(r c) -> r c", c=128)).then_inc(s["consts_in"], 16)
            act.dma_start(crow[8:16, :], a["c_ctx"].rearrange("(r c) -> r c", c=128)).then_inc(s["consts_in"], 16)
            for t in range(TT):
                src = a["x"] if t < LT else a["ctx"]
                act.dma_start(X[:, t, :], src[0, (t % LT) * P:(t % LT + 1) * P, :]).then_inc(s["x_in"], 16)
            act.dma_start(lamb.rearrange("p l i d -> p (l i d)"),
                          a["lambda_qk"].rearrange("l i d -> (l i d)").partition_broadcast(P)).then_inc(s["small_in"], 16)
            act.dma_start(sinkb[:, :, :].rearrange("p l h -> p (l h)"),
                          a["sink"].rearrange("l h -> (l h)").partition_broadcast(P)).then_inc(s["small_in"], 16)
            act.dma_start(subb[:, :, :].rearrange("p l d -> p (l d)"),
                          a["subln"].rearrange("l d -> (l d)").partition_broadcast(P)).then_inc(s["small_in"], 16)
            act.dma_start(broutb[:, :], a["b_router"].partition_broadcast(P)).then_inc(s["small_in"], 16)
            act.dma_start(wr[:, :, :], a["w_router"].rearrange("(k p) n -> p k n", p=P)).then_inc(s["router_in"], 16)

            def full(key):
                act.wait_ge(s["t_full"], tix[key] + 1)
                return T[0]

            def mine(key):
                return tix[key] % 2 == 0

            def copy(out, in_):
                return act.activation(out, in_, ACT.Copy)

            full("c")
            copy(craw[:, :], T[0][:, 0:16])
            act.activation(cth[:, :], T[0][:, 0:16], ACT.Tanh, scale=0.5).then_inc(s["t_free_act"], 1)
            act.wait_ge(s["lam_dot"], 1)
            act.activation(lexp[:, :], lsum[:, :], ACT.Exp).then_inc(s["lam_exp"], 1)

            squares = [0]

            def square_sum(t, key, c):
                c0 = RS[key][0]
                if squares[0]:
                    act.wait_ge(s["act_ssq"], squares[0])
                squares[0] += 1
                act.activation(junk, X[:, t, :], ACT.Square, accum_out=ssq[:, c0 + c:c0 + c + 1]).then_inc(s["act_ssq"], 1)

            n_items = act.alloc_register("act_items")
            act.reg_mov(n_items, 0)
            for l in range(DEPTH):
                if l == 0:
                    act.wait_ge(s["x_in"], 16 * TT)
                for t in range(TT):
                    if l and t < TT:
                        act.wait_ge(s["comb_done"], t + 1)
                    square_sum(t, ("attn", l), t)
                if mine(("mod", l)):
                    full(("mod", l))
                    copy(mc[:, :], T[0][:, 0:40]).then_inc(s["t_free_act"], 1)
                act.wait_ge(s["coeff_ready"], l + 1)
                for k in range(KC):
                    if mine(("hT", l, k)):
                        full(("hT", l, k))
                        for i in range(2):
                            ins = act.activation(hT[:, k, i * 256:(i + 1) * 256], T[0][:, i * 256:(i + 1) * 256],
                                                 ACT.Identity, bias=mc[:, 16 * i + k:16 * i + k + 1],
                                                 scale=Ac[:, i, k:k + 1])
                        ins.then_inc(s["t_free_act"], 1)

                def post(i):
                    _, u, t = PROJ[i]
                    if by_dve(u, t):
                        return
                    act.wait_ge(s["proj_done"], i + 1)
                    if u == "va":
                        copy(Va[:, t, :], S[:, i % 4, :]).then_inc(s["post_act"], 1)
                        return
                    j = TR.index(PROJ[i])
                    if j >= 2:
                        act.wait_ge(s["t_full"], tix[("tr",) + TR[j - 2]] + 1)
                    if u == "kvb":
                        src = S[:, i % 4, 0:128].rearrange("p (v o d) -> p v o d", v=2, o=1).to_broadcast([P, 2, 2, 64])
                        copy(stage[:, j % 2, 0:256].rearrange("p (v o d) -> p v o d", v=2, o=2), src)
                        copy(Vb[:, t, :], S[:, i % 4, 128:256]).then_inc(s["post_act"], 1)
                    else:
                        copy(stage[:, j % 2, :], S[:, i % 4, :]).then_inc(s["post_act"], 1)

                def take(key, dst, src_cols, c):
                    full(key)
                    src = T[0][:, 0:src_cols].rearrange("p (c t) -> p c t", c=c)
                    copy(dst, src).then_inc(s["t_free_act"], 1)

                idx = [i for i, st in enumerate(PROJ) if st[0] == l]
                for i in idx + [None]:
                    if i is not None:
                        post(i)
                    prev = (i - 1) if i is not None else idx[-1]
                    if prev >= idx[0] and PROJ[prev][1] != "va" and mine(("tr",) + PROJ[prev]):
                        _, u, t = PROJ[prev]
                        dst = {"ka": kaT, "qa": qaT, "qb": qbT, "kvb": kbT}[u]
                        c = 2 if u == "kvb" else 4
                        take(("tr",) + PROJ[prev], dst[:, :, t * P:(t + 1) * P], c * P, c)

                units = [n for n, u in enumerate(ATT) if u[0] == l]
                for i, n in enumerate(units):
                    _, qt, kind, j = ATT[n]
                    k0 = 0 if qt < LT else SEQ
                    act.wait_ge(s["negm_ready"], n + 1)
                    if i:
                        act.wait_ge(s["t_full"], tix[("att", n - 1, heads_in[ATT[n - 1][2]] - 1)] + 1)
                    else:
                        act.wait_ge(s["t_full"], max(tix[("tr",) + st] for st in TR if st[0] == l) + 1)
                    if kind == "gqa":
                        act.activation(sexp[:, n % 2, :], sdif[:, :], ACT.Exp)
                    for b in range(4):
                        ins = act.activation(Pm[:, b, 0:TOK - k0], S[:, b, 0:TOK - k0], ACT.Exp, bias=negm[:, b:b + 1],
                                             scale=SCALE, accum_out=sums[:, n % 2, b:b + 1])
                    ins.then_inc(s["exps_done"], 1)
                    nk = (TOK - k0) // P
                    for c in range(heads_in[kind]):
                        if mine(("att", n, c)):
                            take(("att", n, c), PT[:, c, 0:nk, :], nk * P, nk)
                    done = [qt - 1] if i % 4 == 0 and i else []
                    if i == len(units) - 1:
                        done.append(qt)
                    for q in done:
                        for h in (0, 1):
                            if mine(("mix", l, q, h)):
                                take(("mix", l, q, h), hT[:, 4 * h:4 * h + 4, q * P:(q + 1) * P], 512, 4)

                base = 0 if l == 0 else len(qtiles[0])
                w0 = WOUT.index((l, 0, 0))
                for i, t in enumerate(qtiles[l]):
                    act.wait_ge(s["wout_out"], w0 + 2 * i + 2)
                    square_sum(t, ("ffn", l, t), 0)
                    act.wait_ge(s["h_ready"], base + i + 1)
                    act.dma_start(h_d[l][t * P:(t + 1) * P, :], hb[:, i % 2, :]).then_inc(s[f"h_stored{i % 2}"], 16)
                    for h in (0, 1):
                        if mine(("rt", l, t, h)):
                            take(("rt", l, t, h), hTs[:, 4 * h:4 * h + 4, :], 512, 4)
                nt = len(qtiles[l])
                act.wait_ge(s["logits_done"], base + nt)
                act.activation(junk[:, 0:nt * NE], AUX[:, 0:nt * NE], ACT.Tanh, scale=0.5).then_inc(s["sig_done"], 1)
                if mine(("list", l)):
                    full(("list", l))
                    act.activation(g_ix, T[0][:, 0:P], ACT.Identity, bias=cst[:, C_H:C_H + 1],
                                   scale=2.0).then_inc(s["t_free_act"], 1)

                g = act.snap(n_items, min_val=0, max_val=64)
                act.wait_ge(s["xtr_done"], g + (l + 2))
                copy(xT, O[:, :].rearrange("p (j t) -> p j t", j=4)).then_inc(s["xT_ready"], 1)
                if l == 0:
                    copy(sexp[:, 0, 0:1], sexp[:, 0, 0:1]).then_inc(s["y_out"], 1)
                with act.Fori(0, NE) as e:
                    n = act.value_load(ntile[0:1, l, ds(e, 1)], min_val=1, max_val=MAXT)
                    row0 = act.value_load(first_row[0:1, l, ds(e, 1)], min_val=0, max_val=TOPK * P * nt)
                    with act.Fori(0, n) as t:
                        g = act.snap(n_items, min_val=0, max_val=64)
                        act.wait_ge(s["up1_done"], g + 1)
                        act.activation(th, S[:, 0, 0:256], ACT.Tanh, scale=0.5).then_inc(s["tanh_done"], 1)
                        act.wait_ge(s["xtr_done"], g + (l + 3))
                        copy(xT, O[:, :].rearrange("p (j t) -> p j t", j=4)).then_inc(s["xT_ready"], 1)
                        act.wait_ge(s["down_done"], g + 1)
                        copy(y_s, S[:, 3, :]).then_inc(s["y_out"], 1)
                        act.wait_ge(s["y_out"], g + 2)
                        for h in range(2):
                            dst = y_d[l][ds(row0 + t * TILE, TILE), 512 * h:512 * h + 512]
                            act.dma_start(dst, y_s[64 * h:64 * h + 64, :]).then_inc(s["y_stored"], 16)
                        act.wait_ge(s["y_stored"], 32 * g + 32)
                        act.reg_add(n_items, n_items, 1)
            base = len(qtiles[0])
            for t in range(LT):
                act.wait_ge(s["comb_done"], base + t + 1)
                square_sum(t, ("fin",), t)

        @block.vector
        def _(dve):
            ch = Chain(dve, s["dve_self"])

            def full(key):
                dve.wait_ge(s["t_full"], tix[key] + 1)
                return T[1]

            def mine(key):
                return tix[key] % 2 == 1

            def bc(ap, shape):
                return ap.to_broadcast(shape)

            dve.memset(modrow[:, :, :], 0.0).then_inc(s["clear_done"], 1)
            dve.memset(AUX[:, :], 0.0).then_inc(s["bank_clear"], 1)
            dve.wait_ge(s["consts_in"], 48)
            dve.wait_ge(s["small_in"], 64)
            ch.step(dve.tensor_tensor(lprod, lamb[:, :, 0::2, :], lamb[:, :, 1::2, :], ALU.mult))
            dve.tensor_reduce(lsum[:, :].rearrange("p (l i) -> p l i", l=DEPTH), lprod, AX.X, ALU.add).then_inc(s["lam_dot"], 1)
            dve.tensor_scalar(nsink[:, :, :], sinkb[:, :, :], -1.0, None, ALU.mult)
            for l in range(DEPTH):
                lam_init = 0.8 - 0.6 * math.exp(-0.3 * l)
                dve.tensor_scalar(subb[:, l, :], subb[:, l, :], 1.0 - lam_init, None, ALU.mult)
            dve.wait_ge(s["lam_exp"], 1)
            for l in range(DEPTH):
                lam_init = 0.8 - 0.6 * math.exp(-0.3 * l)
                ch.step(dve.tensor_tensor(nlam[:, l:l + 1], lexp[:, 2 * l + 1:2 * l + 2], lexp[:, 2 * l:2 * l + 1], ALU.subtract))
                ch.step(dve.tensor_scalar(nlam[:, l:l + 1], nlam[:, l:l + 1], -lam_init, None, ALU.add))
            dve.wait_ge(s["t_free_act"], 1)
            ch.step(dve.scalar_tensor_tensor(cth[:, :], cth[:, :], 1.0, craw[:, :], ALU.add, ALU.mult))
            dve.tensor_scalar(cs[:, :, :], cth[:, :].rearrange("p (i k) -> p k i", i=2), 0.5, None, ALU.mult).then_inc(s["c_ready"], 1)

            def ada_out(x):
                dve.wait_ge(s["ada_done"], x + 1)
                dve.tensor_tensor(modrow[:, x, :], modrow[:, x, :], AUX[:, 0:128], ALU.add).then_inc(s["ada_out"], 1)

            dve.wait_ge(s["bias_in"], 16 * 8 * DEPTH)
            for x in range(first_ada):
                ada_out(x)

            n_items = dve.alloc_register("dve_items")
            dve.reg_mov(n_items, 0)
            for l in range(DEPTH):
                base = 0 if l == 0 else len(qtiles[0])
                nt = len(qtiles[l])
                if mine(("mod", l)):
                    full(("mod", l))
                    dve.tensor_copy(mc[:, :], T[1][:, 0:40]).then_inc(s["t_free_dve"], 1)
                dve.wait_ge(t_free[tix[("mod", l)] % 2], tix[("mod", l)] // 2 + 1)
                for i in range(2):
                    ins = dve.scalar_tensor_tensor(Ac[:, i, :], mc[:, 16 * i + 8:16 * i + 16], 1.0, mc[:, 32:40], ALU.add, ALU.mult)
                ins.then_inc(s["coeff_ready"], 1)
                c0, _, _, ev = RS[("attn", l)]
                dve.wait_ge(s["rstd_ready"], ev + 1)
                for t in range(TT):
                    dve.tensor_scalar(xn[:, t, :], X[:, t, :], rstd[:, c0 + t:c0 + t + 1], None, ALU.mult).then_inc(s["xn_ready"], 1)
                dve.wait_ge(s["coeff_ready"], l + 1)
                for k in range(KC):
                    if mine(("hT", l, k)):
                        full(("hT", l, k))
                        for i in range(2):
                            ins = dve.tensor_scalar(hT[:, k, i * 256:(i + 1) * 256], T[1][:, i * 256:(i + 1) * 256],
                                                    Ac[:, i, k:k + 1], mc[:, 16 * i + k:16 * i + k + 1], ALU.mult, ALU.add)
                        ins.then_inc(s["t_free_dve"], 1)

                def rope(src, heads, t, outs):
                    n = heads * 64
                    v = lambda ap: ap[:, 0:n].rearrange("p (h x b f) -> p h x b f", h=heads, x=2, b=2)
                    tab = cst[:, C_ROPE + 128 * t:C_ROPE + 128 * t + 128]
                    cosv = tab[:, 0:64].rearrange("p (o d) -> p o d", o=1)
                    sinv = tab[:, 64:128].rearrange("p (o x b f) -> p o x b f", o=1, x=2, b=2)
                    dve.tensor_tensor(rope_t1[:, 0:n].rearrange("p (h d) -> p h d", h=heads),
                                      src[:, 0:n].rearrange("p (h d) -> p h d", h=heads), bc(cosv, [P, heads, 64]), ALU.mult)
                    for b in range(2):
                        ins = dve.tensor_tensor(v(rope_t2)[:, :, :, b, :], v(src)[:, :, :, 1 - b, :],
                                                bc(sinv[:, :, :, b, :], [P, heads, 2, 16]), ALU.mult)
                    ch.step(ins)
                    for out in outs:
                        ins = dve.tensor_tensor(out, rope_t1[:, 0:n].rearrange("p (h d) -> p h d", h=heads),
                                                rope_t2[:, 0:n].rearrange("p (h d) -> p h d", h=heads), ALU.add)
                    return ins

                def post(i):
                    _, u, t = PROJ[i]
                    if not by_dve(u, t):
                        return
                    dve.wait_ge(s["proj_done"], i + 1)
                    j = TR.index(PROJ[i])
                    if j >= 2:
                        dve.wait_ge(s["t_full"], tix[("tr",) + TR[j - 2]] + 1)
                    src = S[:, i % 4, :]
                    if u == "kvb":
                        dve.tensor_copy(Vb[:, t, :], src[:, 128:256])
                        st = stage[:, j % 2, 0:256].rearrange("p (v o d) -> p v o d", v=2, o=2)
                        ch.step(rope(src, 2, t, [st[:, :, 0, :], st[:, :, 1, :]]))
                    else:
                        ch.step(rope(src, 8, t, [stage[:, j % 2, :].rearrange("p (h d) -> p h d", h=8)]))
                    dve.tensor_scalar(sdif[:, 0:1], nlam[:, 0:1], 1.0, None, ALU.mult).then_inc(s["post_dve"], 1)

                def take(key, dst, src_cols, c):
                    full(key)
                    dve.tensor_copy(dst, T[1][:, 0:src_cols].rearrange("p (c t) -> p c t", c=c)).then_inc(s["t_free_dve"], 1)

                idx = [i for i, st in enumerate(PROJ) if st[0] == l]
                for i in idx + [None]:
                    if i is not None:
                        post(i)
                    prev = (i - 1) if i is not None else idx[-1]
                    if prev >= idx[0] and PROJ[prev][1] != "va" and mine(("tr",) + PROJ[prev]):
                        _, u, t = PROJ[prev]
                        dst = {"ka": kaT, "qa": qaT, "qb": qbT, "kvb": kbT}[u]
                        c = 2 if u == "kvb" else 4
                        take(("tr",) + PROJ[prev], dst[:, :, t * P:(t + 1) * P], c * P, c)

                units = [n for n, u in enumerate(ATT) if u[0] == l]

                def row_max(n):
                    _, qt, kind, j = ATT[n]
                    k0 = 0 if qt < LT else SEQ
                    dve.wait_ge(s["scores_done"], n + 1)
                    ch.step(dve.tensor_reduce(rm[:, :], S[:, :, 0:TOK - k0], AX.X, ALU.max))
                    if kind == "diff":
                        dve.tensor_scalar(negm[:, :], rm[:, :], -SCALE, None, ALU.mult).then_inc(s["negm_ready"], 1)
                    else:
                        ch.step(dve.scalar_tensor_tensor(negm[:, :], rm[:, :], -SCALE, nsink[:, l, 4 * j:4 * j + 4], ALU.mult, ALU.min))
                        dve.tensor_tensor(sdif[:, :], negm[:, :], sinkb[:, l, 4 * j:4 * j + 4], ALU.add).then_inc(s["negm_ready"], 1)

                row_max(units[0])
                for i, n in enumerate(units):
                    _, qt, kind, j = ATT[n]
                    nkey = TOK if qt < LT else CTX
                    dve.wait_ge(s["exps_done"], n + 1)
                    sm, rc = sums[:, n % 2, :], rec[:, n % 2, :]
                    if kind == "gqa":
                        ch.step(dve.tensor_tensor(sm, sm, sexp[:, n % 2, :], ALU.add))
                    ch.step(dve.reciprocal(rc, sm))
                    if kind == "diff":
                        ch.step(dve.tensor_scalar(rec[:, n % 2, 1::2], rec[:, n % 2, 1::2], nlam[:, l:l + 1], None, ALU.mult))
                        for h in range(2):
                            ch.step(dve.tensor_scalar(Pm[:, 2 * h, 0:nkey], Pm[:, 2 * h, 0:nkey], rc[:, 2 * h:2 * h + 1], None, ALU.mult))
                            dve.scalar_tensor_tensor(Pm[:, 2 * h, 0:nkey], Pm[:, 2 * h + 1, 0:nkey], rc[:, 2 * h + 1:2 * h + 2],
                                                     Pm[:, 2 * h, 0:nkey], ALU.mult, ALU.add).then_inc(s["norm_done"], 1)
                    if i + 1 < len(units):
                        row_max(n + 1)
                    nk = nkey // P
                    for x in ada_at[n]:
                        ada_out(x)
                    for c in range(heads_in[kind]):
                        if mine(("att", n, c)):
                            take(("att", n, c), PT[:, c, 0:nk, :], nk * P, nk)
                    dve.wait_ge(s["pv_done"], n + 1)
                    if kind == "diff":
                        if j == 0 and i:
                            dve.wait_ge(s["t_full"], tix[("mix", l, qt - 1, 1)] + 1)
                        dve.tensor_copy(mix[:, 256 * j:256 * j + 256], O[:, 0:256]).then_inc(s["o_out"], 1)
                        if j == 1:
                            dve.wait_ge(s["o_out"], n + 1)
                            ch.step(dve.tensor_tensor(tmp[:, :], mix[:, 0:512], mix[:, 0:512], ALU.mult))
                            c0 = RS[("sub", l, qt)][0]
                            dve.tensor_reduce(ssq[:, c0:c0 + HA], tmp[:, :].rearrange("p (h d) -> p h d", h=HA), AX.X,
                                              ALU.add).then_inc(s["dve_ssq"], 1)
                    else:
                        dve.tensor_tensor(mix[:, 512 + 256 * j:768 + 256 * j].rearrange("p (h d) -> p h d", h=4),
                                          O[:, 0:256].rearrange("p (h d) -> p h d", h=4),
                                          bc(rc.rearrange("p (h o) -> p h o", o=1), [P, 4, 64]), ALU.mult).then_inc(s["o_out"], 1)
                        if j == 1:
                            c0, _, _, ev = RS[("sub", l, qt)]
                            dve.wait_ge(s["rstd_ready"], ev + 1)
                            mv = mix[:, 0:512].rearrange("p (h d) -> p h d", h=HA)
                            ch.step(dve.tensor_tensor(mv, mv, bc(rstd[:, c0:c0 + HA].rearrange("p (h o) -> p h o", o=1), [P, HA, 128]), ALU.mult))
                            dve.tensor_tensor(mv, mv, bc(subb[:, l, :].rearrange("p (o d) -> p o d", o=1), [P, HA, 128]),
                                              ALU.mult).then_inc(s["mix_ready"], 1)
                    done = [qt - 1] if i % 4 == 0 and i else []
                    if i == len(units) - 1:
                        done.append(qt)
                    for q in done:
                        for h in (0, 1):
                            if mine(("mix", l, q, h)):
                                take(("mix", l, q, h), hT[:, 4 * h:4 * h + 4, q * P:(q + 1) * P], 512, 4)

                streams = 2 if l == 0 else 1
                dve.wait_ge(s["ga_in"], 32 if l == 0 else 48)
                w0 = WOUT.index((l, 0, 0))

                def residual(t):
                    for n in range(2):
                        w = WOUT.index((l, t, n))
                        if w:
                            dve.wait_ge(s["wout_out"], w)
                        dve.wait_ge(s["wout_done"], w + 1)
                        ch.step(dve.tensor_tensor(tmp[:, :], S[:, w % 4, :], gA[:, t // LT, n * 512:(n + 1) * 512], ALU.mult))
                        xs = X[:, t, n * 512:(n + 1) * 512]
                        dve.tensor_tensor(xs, xs, tmp[:, :], ALU.add).then_inc(s["wout_out"], 1)

                def ffn_input(i, t):
                    c0, _, _, ev = RS[("ffn", l, t)]
                    dve.wait_ge(s["rstd_ready"], ev + 1)
                    if i >= 2:
                        dve.wait_ge(s[f"h_stored{i % 2}"], 16 * (base // 2 + i // 2))
                        dve.wait_ge(s["t_full"], tix[("rt", l, t - 2, 1)] + 1)
                    ch.step(dve.scalar_tensor_tensor(hb[:, i % 2, :], X[:, t, :], rstd[:, c0:c0 + 1], Af[:, t // LT, :], ALU.mult, ALU.mult))
                    dve.tensor_tensor(hb[:, i % 2, :], hb[:, i % 2, :], Bf[:, t // LT, :], ALU.add).then_inc(s["h_ready"], 1)

                def take_rt(t):
                    for h in (0, 1):
                        if mine(("rt", l, t, h)):
                            take(("rt", l, t, h), hTs[:, 4 * h:4 * h + 4, :], 512, 4)

                residual(0)
                dve.wait_ge(s["ab_in"], 80 if l == 0 else 80 + 48)
                for i in range(streams):
                    ins = dve.scalar_tensor_tensor(Af[:, i, :], Af[:, i, :], 1.0, nfb, ALU.add, ALU.mult)
                    if i < streams - 1:
                        ch.step(ins)
                ins.then_inc(s["ab_ready"], 1)
                dve.wait_ge(s["ab_ready"], l + 1)
                for i, t in enumerate(qtiles[l]):
                    if i + 1 < nt:
                        residual(t + 1)
                    ffn_input(i, t)
                    take_rt(t)

                W = nt * NE
                R = [junk[:, 64 * i:64 * i + W] for i in range(14)]
                g4 = lambda ap: ap.rearrange("p (a e) -> p a e", e=EPG)
                G = [junk[:, 896 + 16 * i:896 + 16 * i + nt * NG] for i in range(8)]
                ch.step(dve.tensor_copy(tri_b, cst[:, C_TRI:C_TRI + P]))
                ch.step(dve.memset(one_b, 1.0))
                dve.wait_ge(s["sig_done"], l + 1)
                sg, sbv, e1, k1, o1, s2 = R[1], R[2], R[3], R[4], R[5], R[6]
                A4 = [P, nt * NG, EPG]
                dec = bc(cst[:, C_DEC:C_DEC + EPG].rearrange("p (o e) -> p o e", o=1), A4)
                up = lambda ap: bc(ap.rearrange("p (a o) -> p a o", o=1), A4)
                ch.step(dve.tensor_scalar(sg, R[0], 0.5, 0.5, ALU.mult, ALU.add))
                ch.step(dve.tensor_tensor(sbv.rearrange("p (t e) -> p t e", e=NE), sg.rearrange("p (t e) -> p t e", e=NE),
                                          bc(broutb[:, :].rearrange("p (o e) -> p o e", o=1), [P, nt, NE]), ALU.add))

                def best(vals, top, onehot, dec_, up_, view, top_view):
                    ch.step(dve.tensor_reduce(top, view(vals), AX.X, ALU.max))
                    ch.step(dve.tensor_tensor(view(e1), view(vals), up_(top), ALU.is_equal))
                    ch.step(dve.tensor_tensor(view(e1), view(e1), dec_, ALU.mult))
                    ch.step(dve.tensor_reduce(top_view, view(e1), AX.X, ALU.max))
                    ch.step(dve.tensor_tensor(view(onehot), view(e1), up_(top_view), ALU.is_equal))

                best(sbv, G[0], o1, dec, up, g4, G[1])
                ch.step(dve.scalar_tensor_tensor(s2, o1, -3e38, sbv, ALU.mult, ALU.add))
                o2 = k1
                best(s2, G[2], o2, dec, up, g4, G[3])
                ch.step(dve.tensor_tensor(G[4], G[0], G[2], ALU.add))
                tg = lambda ap: ap.rearrange("p (t g) -> p t g", g=NG)
                G3 = [P, nt, NG]
                upg = lambda ap: bc(ap.rearrange("p (t o) -> p t o", o=1), G3)
                gm, gk = G[5][:, 0:nt], G[6][:, 0:nt]
                decg = bc(cst[:, C_DECG:C_DECG + NG].rearrange("p (o g) -> p o g", o=1), G3)
                ch.step(dve.tensor_reduce(gm, tg(G[4]), AX.X, ALU.max))
                ch.step(dve.tensor_tensor(tg(G[1]), tg(G[4]), upg(gm), ALU.is_equal))
                ch.step(dve.tensor_tensor(tg(G[1]), tg(G[1]), decg, ALU.mult))
                ch.step(dve.tensor_reduce(gk, tg(G[1]), AX.X, ALU.max))
                ch.step(dve.tensor_tensor(tg(G[1]), tg(G[1]), upg(gk), ALU.is_equal))
                ch.step(dve.tensor_tensor(g4(o1), g4(o1), up(G[1]), ALU.mult))
                ch.step(dve.tensor_tensor(g4(o2), g4(o2), up(G[1]), ALU.mult))
                dve.tensor_tensor(mask_b[:, 0:W], o1, o2, ALU.add).then_inc(s["mask_ready"], 1)
                te = lambda ap: ap.rearrange("p (t e) -> p t e", e=NE)
                for k, oh in enumerate((o1, o2)):
                    ch.step(dve.tensor_tensor(R[7 + k], sg, oh, ALU.mult))
                    ch.step(dve.tensor_reduce(gate[:, k, 0:nt], te(R[7 + k]), AX.X, ALU.add))
                den = G[7][:, 0:nt]
                ch.step(dve.tensor_tensor(den, gate[:, 0, 0:nt], gate[:, 1, 0:nt], ALU.add))
                ch.step(dve.reciprocal(den, den))
                for k in range(2):
                    ch.step(dve.tensor_tensor(gate[:, k, 0:nt], gate[:, k, 0:nt], den, ALU.mult))
                dve.wait_ge(s["ranks_done"], l + 1)
                cnt = AUX[:, 256:256 + NE]
                before = tmp[:, 0:NE * NE].rearrange("p (e f) -> p e f", e=NE)
                ch.step(dve.tensor_tensor(before, bc(cnt.rearrange("p (o f) -> p o f", o=1), [P, NE, NE]),
                                          cst[:, C_BEF:C_ALL].rearrange("p (e f) -> p e f", e=NE), ALU.mult))
                ch.step(dve.tensor_reduce(R[13][:, 0:NE], before, AX.X, ALU.add))
                ch.step(dve.tensor_copy(first_row[:, l, :], R[13][:, 0:NE]))
                rank = AUX[:, 128:128 + W].rearrange("p (t e) -> p t e", e=NE)
                for start, place in ((cst[:, C_EB:C_EB + NE], slot_ix), (R[13][:, 0:NE], row_ix)):
                    ch.step(dve.tensor_tensor(te(R[9]), rank, bc(start.rearrange("p (o e) -> p o e", o=1), [P, nt, NE]), ALU.add))
                    for k, oh in enumerate((o1, o2)):
                        ch.step(dve.tensor_tensor(R[10 + k], R[9], oh, ALU.mult))
                        ch.step(dve.tensor_reduce(G[k][:, 0:nt], te(R[10 + k]), AX.X, ALU.add))
                        ch.step(dve.tensor_copy(place[:, l, k, 0:nt], G[k][:, 0:nt]))
                big = tmp[:, 0:NE * (MAXT - 1)].rearrange("p (e j) -> p e j", e=NE)
                ch.step(dve.tensor_tensor(big, bc(cnt.rearrange("p (e o) -> p e o", o=1), [P, NE, MAXT - 1]),
                                          bc(cst[:, C_THR:C_BEF].rearrange("p (o j) -> p o j", o=1), [P, NE, MAXT - 1]), ALU.is_gt))
                ch.step(dve.tensor_reduce(R[12][:, 0:NE], big, AX.X, ALU.add))
                dve.tensor_scalar(ntile[:, l, :], R[12][:, 0:NE], 1.0, None, ALU.add).then_inc(s["slots_ready"], 1)
                if mine(("list", l)):
                    full(("list", l))
                    dve.tensor_scalar(g_ix, T[1][:, 0:P], 2.0, cst[:, C_H:C_H + 1], ALU.mult, ALU.add).then_inc(s["t_free_dve"], 1)
                dve.wait_ge(t_free[tix[("list", l)] % 2], tix[("list", l)] // 2 + 1)
                dve.tensor_copy(tmp[:, 0:1], cst[:, C_H:C_H + 1]).then_inc(s["gix_ready"], 1)
                dve.wait_ge(s["slots_ready"], l + 1)

                with dve.Fori(0, NE) as e:
                    n = dve.value_load(ntile[0:1, l, ds(e, 1)], min_val=1, max_val=MAXT)
                    with dve.Fori(0, n) as t:
                        g = dve.snap(n_items, min_val=0, max_val=64)
                        dve.wait_ge(s["tanh_done"], g + 1)
                        dve.scalar_tensor_tensor(t2, th, 1.0, S[:, 0, 0:256], ALU.add, ALU.mult).then_inc(s["t2_done"], 1)
                        dve.wait_ge(s["t2_done"], g + 1)
                        dve.wait_ge(s["up3_done"], g + 1)
                        for c, name in enumerate(("ua_done", "ub_done")):
                            dve.scalar_tensor_tensor(u_s[:, 128 * c:128 * c + 128], t2[:, 128 * c:128 * c + 128], 0.5,
                                                     S[:, 1, 128 * c:128 * c + 128], ALU.mult, ALU.mult).then_inc(s[name], 1)
                        dve.wait_ge(s["uta_done"], g + 1)
                        dve.tensor_copy(uT[:, 0, :], S[:, 2, 0:128]).then_inc(s["ea_done"], 1)
                        dve.wait_ge(s["utb_done"], g + 1)
                        dve.tensor_copy(uT[:, 1, :], S[:, 2, 128:256]).then_inc(s["eb_done"], 1)
                        dve.reg_add(n_items, n_items, 1)

                dve.wait_ge(s["gf_in"], 32 if l == 0 else 48)
                for i, t in enumerate(qtiles[l]):
                    dve.wait_ge(s[f"y_gathered{i % 2}"], 32 * (base // 2 + i // 2 + 1))
                    y0, y1 = yk[:, i % 2, 0, :], yk[:, i % 2, 1, :]
                    ch.step(dve.tensor_scalar(y0, y0, gate[:, 0, t:t + 1], None, ALU.mult))
                    ch.step(dve.scalar_tensor_tensor(y0, y1, gate[:, 1, t:t + 1], y0, ALU.mult, ALU.add))
                    ch.step(dve.tensor_tensor(y0, y0, gF[:, t // LT, :], ALU.mult))
                    dve.tensor_tensor(X[:, t, :], X[:, t, :], y0, ALU.add).then_inc(s["comb_done"], 1)
            c0, _, _, ev = RS[("fin",)]
            dve.wait_ge(s["rstd_ready"], ev + 1)
            dve.wait_ge(s["nfin_in"], 16)
            for t in range(LT):
                dve.scalar_tensor_tensor(X[:, t, :], X[:, t, :], rstd[:, c0 + t:c0 + t + 1], nfb, ALU.mult, ALU.mult).then_inc(s["fin_ready"], 1)

        @block.tensor
        def _(pe):
            def weights(key):
                slot, n = where[key]
                pe.wait_ge(slot_full[slot], n)
                return slot

            def bank(key):
                k = tix[key]
                if k >= 2:
                    pe.wait_ge(t_free[k % 2], k // 2)
                return T[k % 2]

            def taken(key):
                k = tix[key]
                pe.wait_ge(t_free[k % 2], k // 2 + 1)

            def transposes(key, srcs):
                b, at = bank(key), 0
                for src in srcs:
                    rows = src.shape[0]
                    ins = pe.transpose(b[0:src.shape[1], at:at + rows], src, cst[0:rows, C_ID:C_ID + rows])
                    at += rows
                ins.then_inc(s["t_full"], 1)

            pe.wait_ge(s["consts_in"], 48)
            transposes("c", [crow])
            pe.wait_ge(s["c_ready"], 1)
            pe.wait_ge(s["bank_clear"], 1)

            def ada(x):
                slot = weights(("ada", x))
                if x:
                    pe.wait_ge(s["ada_out"], x)
                w = slot_view(slot, KC)
                for k in range(KC):
                    for q in range(4):
                        ins = pe.matmul(AUX[32 * q:32 * q + 2, 0:128], cs[:, k, :], w[:, k, 128 * q:128 * q + 128],
                                        start=(k == 0), stop=(k == KC - 1))
                ins.then_inc(s["ada_done"], 1)

            for x in range(first_ada):
                ada(x)

            n_items = pe.alloc_register("pe_items")
            pe.reg_mov(n_items, 0)
            loaded, last_x, last_y = (pe.alloc_register(f"pe_{n}") for n in ("loaded", "last_x", "last_y"))
            for l in range(DEPTH):
                nt = len(qtiles[l])
                base = 0 if l == 0 else len(qtiles[0])
                pe.wait_ge(s["modT_in"], 48 * (l + 1))
                transposes(("mod", l), [modT[:, :]])
                pe.wait_ge(s["xn_ready"], TT * (l + 1))
                for k in range(KC):
                    transposes(("hT", l, k), [xn[:, t, k * P:(k + 1) * P] for t in range(TT)])
                taken(("hT", l, KC - 2))
                taken(("hT", l, KC - 1))

                def posted(i):
                    eng = by_dve(*PROJ[i][1:])
                    pe.wait_ge(s["post_dve" if eng else "post_act"], POST[eng].index(PROJ[i]) + 1)

                def tr(st):
                    posted(PROJ.index(st))
                    j = TR.index(st)
                    n = 2 if st[1] == "kvb" else 4
                    transposes(("tr",) + st, [stage[:, j % 2, c * P:(c + 1) * P] for c in range(n)])

                idx = [i for i, st in enumerate(PROJ) if st[0] == l]
                for i in idx:
                    _, u, t = PROJ[i]
                    slot = weights(("in", l, u))
                    width = UCOL[u][1]
                    w = ring[:, slot, 0:KC * width].rearrange("p (k n) -> p k n", k=KC)
                    if i - 4 >= idx[0]:
                        posted(i - 4)
                    for k in range(KC):
                        ins = pe.matmul(S[:, i % 4, 0:width], hT[:, k, t * P:(t + 1) * P], w[:, k, :],
                                        start=(k == 0), stop=(k == KC - 1))
                    ins.then_inc(s["proj_done"], 1)
                    if i > idx[0] and PROJ[i - 1][1] != "va":
                        tr(PROJ[i - 1])
                tr(PROJ[idx[-1]])

                trs = sorted(tix[("tr",) + st] for st in TR if st[0] == l)[-2:]
                for k in trs:
                    pe.wait_ge(t_free[k % 2], k // 2 + 1)
                for eng in (True, False):
                    pe.wait_ge(s["post_dve" if eng else "post_act"], len([st for st in POST[eng] if st[0] <= l]))
                units = [n for n, u in enumerate(ATT) if u[0] == l]

                def scores(n):
                    _, qt, kind, j = ATT[n]
                    k0 = 0 if qt < LT else SEQ
                    nkey = TOK - k0
                    q = slice(qt * P, (qt + 1) * P)
                    for b in range(4):
                        r = slice(64 * (b % 2), 64 * (b % 2) + 64)
                        biased = kind == "gqa" and qt < LT
                        if kind == "diff":
                            c = 2 * j + b // 2
                            lhs, rhs = qaT[r, c, q], kaT[r, c, k0:TOK]
                        else:
                            lhs, rhs = qbT[r, 2 * j + b // 2, q], kbT[r, j, k0:TOK]
                        ins = pe.matmul(S[:, b, 0:nkey], lhs, rhs, start=True, stop=not biased)
                    if biased:
                        blk = (1 - qt) * P
                        for b in range(4):
                            ins = pe.matmul(S[:, b, blk:blk + P], ident, cst[:, C_MB + P * qt:C_MB + P * qt + P],
                                            start=False, stop=True)
                    ins.then_inc(s["scores_done"], 1)

                def heads(n):
                    _, qt, kind, j = ATT[n]
                    t0 = 0 if qt < LT else LT
                    nk = TT - t0
                    nh = heads_in[kind]

                    def flip(c):
                        if kind == "diff":
                            pe.wait_ge(s["norm_done"], 2 * diffs[n] + c + 1)
                        else:
                            pe.wait_ge(s["exps_done"], n + 1)
                        row = 2 * c if kind == "diff" else c
                        transposes(("att", n, c), [Pm[:, row, kb * P:(kb + 1) * P] for kb in range(nk)])

                    def product(c):
                        taken(("att", n, c))
                        if c == 0 and n:
                            pe.wait_ge(s["o_out"], n)
                        for kb in range(nk):
                            if kind == "diff":
                                h = 2 * j + c
                                out, v = O[:, 128 * c:128 * c + 128], Va[:, t0 + kb, 128 * h:128 * h + 128]
                            else:
                                out, v = O[:, 64 * c:64 * c + 64], Vb[:, t0 + kb, 64 * j:64 * j + 64]
                            ins = pe.matmul(out, PT[:, c, kb, :], v, start=(kb == 0), stop=(kb == nk - 1))
                        return ins

                    flip(0)
                    for c in range(nh):
                        if c + 1 < nh:
                            flip(c + 1)
                        ins = product(c)
                    ins.then_inc(s["pv_done"], 1)

                diffs, d = {}, 0
                for n, u in enumerate(ATT):
                    diffs[n] = d
                    d += u[2] == "diff"

                def mixT(qt):
                    pe.wait_ge(s["mix_ready"], base + qt + 1)
                    for h in (0, 1):
                        transposes(("mix", l, qt, h), [mix[:, (4 * h + c) * P:(4 * h + c + 1) * P] for c in range(4)])

                scores(units[0])
                for i, n in enumerate(units):
                    if i + 1 < len(units):
                        pe.wait_ge(s["exps_done"], n + 1)
                        scores(n + 1)
                    for x in ada_at[n]:
                        ada(x)
                    heads(n)
                    if i % 4 == 0 and i:
                        mixT(ATT[n][1] - 1)
                mixT(qtiles[l][-1])

                slots = [weights(("out", l, n)) for n in (0, 1)]

                def out_proj(t):
                    for n in range(2):
                        w = WOUT.index((l, t, n))
                        if t == qtiles[l][0] and n == 0:
                            pe.wait_ge(s["exps_done"], units[-1] + 1)
                        if w - 4 >= WOUT.index((l, 0, 0)):
                            pe.wait_ge(s["wout_out"], w - 3)
                        if n == 0:
                            taken(("mix", l, t, 0))
                            taken(("mix", l, t, 1))
                        wv = slot_view(slots[n], KC)
                        for k in range(KC):
                            ins = pe.matmul(S[:, w % 4, :], hT[:, k, t * P:(t + 1) * P], wv[:, k, :],
                                            start=(k == 0), stop=(k == KC - 1))
                        ins.then_inc(s["wout_done"], 1)

                def logits(i, t):
                    pe.wait_ge(s["h_ready"], base + i + 1)
                    for h in (0, 1):
                        transposes(("rt", l, t, h), [hb[:, i % 2, (4 * h + c) * P:(4 * h + c + 1) * P] for c in range(4)])
                    for h in (0, 1):
                        taken(("rt", l, t, h))
                    for k in range(KC):
                        ins = pe.matmul(AUX[:, t * NE:(t + 1) * NE], hTs[:, k, :], wr[:, k, :], start=(k == 0), stop=(k == KC - 1))
                    ins.then_inc(s["logits_done"], 1)

                if l == 0:
                    pe.wait_ge(s["ada_out"], len(ADA))
                    pe.wait_ge(s["router_in"], 16)
                out_proj(0)
                for i, t in enumerate(qtiles[l]):
                    if i + 1 < nt:
                        out_proj(t + 1)
                    logits(i, t)

                pe.wait_ge(s["mask_ready"], l + 1)
                pe.wait_ge(s["sig_done"], l + 1)
                for t in range(nt):
                    for p_ in range(t + 1):
                        pe.matmul(AUX[:, 128 + t * NE:128 + (t + 1) * NE], tri_b if p_ == t else one_b,
                                  mask_b[:, p_ * NE:(p_ + 1) * NE], start=(p_ == 0), stop=(p_ == t))
                for p_ in range(nt):
                    ins = pe.matmul(AUX[:, 256:256 + NE], one_b, mask_b[:, p_ * NE:(p_ + 1) * NE],
                                    start=(p_ == 0), stop=(p_ == nt - 1))
                ins.then_inc(s["ranks_done"], 1)
                pe.wait_ge(s["list_in"], 32 * (l + 1))
                transposes(("list", l), [lst.rearrange("p h s -> p (h s)")])

                if l == 0:
                    pe.matmul(O[:, 0:16], one_b, mask_b[:, 0:16], start=True, stop=True).then_inc(s["xtr_done"], 1)

                def token_T(gathers):
                    pe.wait_ge(s["x_gathered"], 16 * gathers + 16)
                    for j in range(4):
                        ins = pe.transpose(O[:, j * P:(j + 1) * P], xg[:, j * P:(j + 1) * P], ident)
                    ins.then_inc(s["xtr_done"], 1)

                g = pe.snap(n_items, min_val=0, max_val=64)
                if l:
                    pe.wait_ge(s["xT_ready"], g + l)
                token_T(g + l)
                pe.wait_ge(s["slots_ready"], l + 1)
                with pe.Fori(0, NE // 2) as pair:
                    for half in range(2):
                        n = pe.value_load(ntile[0:1, l, ds(2 * pair + half, 1)], min_val=1, max_val=MAXT)
                        part = [slot_view(3 * half + i, 4 if i == 2 else 8) for i in range(3)]
                        full0 = [where[("e", l, half, i)][1] for i in range(3)]
                        pe.reg_mov(loaded, 16 * pair + full0[0])
                        pe.wait_ge(s["slots_ready"], l + 1)
                        pe.wait_ge(slot_full[3 * half], loaded)
                        with pe.Fori(0, n) as t:
                            g = pe.snap(n_items, min_val=0, max_val=64)
                            pe.wait_ge(s["xT_ready"], g + (l + 1))
                            for i, done in ((0, "up1_done"), (1, "up3_done")):
                                if i == 1:
                                    pe.wait_ge(slot_full[3 * half + 1], 16 * pair + full0[1])
                                for k in range(KC):
                                    for h in range(2):
                                        ins = pe.matmul(S[64 * h:64 * h + 64, i, 0:256],
                                                        xT[:, k % 4, 64 * (k // 4):64 * (k // 4) + 64],
                                                        part[i][:, k, h * 256:h * 256 + 256], start=(k == 0), stop=(k == KC - 1))
                                ins.then_inc(s[done], 1)
                            token_T(g + (l + 1))
                            for c, (have, done) in enumerate((("ua_done", "uta_done"), ("ub_done", "utb_done"))):
                                pe.wait_ge(s[have], g + 1)
                                if c == 1:
                                    pe.wait_ge(s["ea_done"], g + 1)
                                pe.transpose(S[:, 2, c * P:(c + 1) * P], u_s[:, c * P:(c + 1) * P], ident).then_inc(s[done], 1)
                                if c == 0:
                                    pe.wait_ge(s["ea_done"], g + 1)
                                    pe.wait_ge(s["y_out"], g + 1)
                                    pe.wait_ge(slot_full[3 * half + 2], 16 * pair + full0[2])
                                else:
                                    pe.wait_ge(s["eb_done"], g + 1)
                                for hf in range(2):
                                    for h in range(2):
                                        ins = pe.matmul(S[64 * h:64 * h + 64, 3, :], uT[:, c, 64 * hf:64 * hf + 64],
                                                        part[2][:, 2 * hf + c, h * 512:h * 512 + 512],
                                                        start=(c == 0 and hf == 0), stop=(c == 1 and hf == 1))
                            ins.then_inc(s["down_done"], 1)
                            pe.reg_add(n_items, n_items, 1)
                        pe.drain().then_inc(s["expert_done"], 1)
                g = pe.snap(n_items, min_val=1, max_val=64)
                pe.reg_mov(last_x, g + (l + 1))
                pe.reg_mov(last_y, g + 1)
                pe.wait_ge(s["slots_ready"], l + 1)
                pe.wait_ge(s["xT_ready"], last_x)
                pe.wait_ge(s["y_out"], last_y)


_INS = ["x", "c", "ctx", "c_ctx", "w_ada", "b_ada", "norm_attn", "norm_ffn", "w_in", "w_out", "lambda_qk",
        "subln", "sink", "w_router", "b_router", "w1", "w3", "w2", "norm_final"]


def kernel(**inputs):
    import concourse.bacc as bacc
    from concourse.bass_utils import run_bass_kernel_spmd

    nc = bacc.Bacc("TRN2", target_bir_lowering=False, num_devices=1)
    arrays = {f"in_{n}": np.ascontiguousarray(inputs[n]) for n in _INS}
    arrays["in_consts"] = constants()
    aps = {n[3:]: nc.dram_tensor(n, v.shape, mybir.dt.from_np(v.dtype), kind="ExternalInput").ap()
           for n, v in arrays.items()}
    aps["out"] = nc.dram_tensor("out", (1, SEQ, DM), mybir.dt.float32, kind="ExternalOutput").ap()
    build(nc, aps)
    r = run_bass_kernel_spmd(nc, [arrays], core_ids=[0])
    return r.results[0]["out"]
```

```python
import math
from contextlib import ExitStack

import numpy as np
import concourse.bass as bass
from concourse import mybir

P = 128
DM, SEQ, CTX, DEPTH = 1024, 256, 256, 2
GRID_W = 64
HA, HB, KVB, DH = 4, 8, 2, 64
NE, NG, EPG, TOPK, DE = 16, 4, 4, 2, 512
EPS, NEG = 1e-6, -1e30
ROPE_BASE = 10000.0
KC = DM // P
TT = (SEQ + CTX) // P
LT = SEQ // P
TOK = SEQ + CTX
D_IN = 2304
N_ADA = 6 * DM // 512
TILE = 64
MAXT = TOK // TILE
SLOTCOLS = 4096
SCALE = DH ** -0.5

C_ID, C_TRI, C_MB, C_ROPE = 0, 128, 256, 512
C_DEC, C_DECG, C_EB, C_TOK, C_H, C_THR = 768, 784, 788, 804, 808, 809
C_BEF = C_THR + MAXT - 1
C_ALL = C_BEF + NE * NE


def constants():
    c = np.zeros((P, C_ALL), np.float32)
    r = np.arange(P)
    c[:, C_ID:C_ID + P] = np.eye(P)
    c[:, C_TRI:C_TRI + P] = r[:, None] < r[None, :]
    c[:, C_MB:C_MB + P] = np.where(r[None, :] <= r[:, None], 0.0, NEG)
    c[:, C_MB + P:C_MB + 2 * P] = np.where(r[None, :] >= r[:, None], 0.0, NEG)
    n_freq = DH // 4
    inv = (1.0 / (ROPE_BASE ** (np.arange(n_freq, dtype=np.float32) / np.float32(n_freq)))).astype(np.float32)
    pos = np.arange(SEQ)
    ang = np.stack([pos // GRID_W, pos % GRID_W], -1).astype(np.float32)[:, :, None] * inv
    cos, sin = np.cos(ang), np.sin(ang)
    full_cos = np.stack([cos, cos], 2).reshape(LT, P, DH)
    full_sin = np.stack([-sin, sin], 2).reshape(LT, P, DH)
    for t in range(LT):
        c[:, C_ROPE + 128 * t:C_ROPE + 128 * t + 64] = full_cos[t]
        c[:, C_ROPE + 128 * t + 64:C_ROPE + 128 * t + 128] = full_sin[t]
    c[:, C_DEC:C_DEC + NE] = EPG - np.arange(NE) % EPG
    c[:, C_DECG:C_DECG + NG] = NG - np.arange(NG)
    c[:, C_EB:C_EB + NE] = np.arange(NE) * TOK
    c[:, C_TOK:C_TOK + TT] = r[:, None] + P * np.arange(TT)[None, :]
    c[:, C_H] = r // 64
    c[:, C_THR:C_BEF] = TILE * np.arange(1, MAXT)
    c[:, C_BEF:C_ALL] = (np.arange(NE)[None, :] < np.arange(NE)[:, None]).reshape(-1)
    return c


class Chain:

    def __init__(self, eng, sem):
        self.eng, self.sem, self.n = eng, sem, 0

    def step(self, ins):
        ins.then_inc(self.sem, 1)
        self.n += 1
        self.eng.wait_ge(self.sem, self.n)


def build(nc, a):
    f32, bf16, i32 = mybir.dt.float32, mybir.dt.bfloat16, mybir.dt.int32
    ALU, ACT, AX = mybir.AluOpType, mybir.ActivationFunctionType, mybir.AxisListType
    ds = bass.ds

    mod_d = nc.dram_tensor("mod_d", [DEPTH, 2, 6 * DM], f32).ap()
    h_d = [nc.dram_tensor(f"h_d{l}", [TOK, DM], f32).ap() for l in range(DEPTH)]
    list_d = [nc.dram_tensor(f"list_d{l}", [NE * TOK, 1], f32).ap() for l in range(DEPTH)]
    y_d = [nc.dram_tensor(f"y_d{l}", [TOPK * P * (TT if l == 0 else LT) + TOK, DM], f32).ap() for l in range(DEPTH)]

    qtiles = [list(range(TT)), list(range(LT))]
    UNITS = ["ka", "va", "kvb", "qa", "qb"]
    UCOL = {"qa": (0, 512), "ka": (512, 512), "va": (1024, 512), "qb": (1536, 512), "kvb": (2048, 256)}
    PROJ = [(l, u, t) for l in range(DEPTH) for u in UNITS
            for t in (range(TT) if u in ("ka", "va", "kvb") else qtiles[l])]
    by_dve = lambda u, t: t < LT and u != "va"
    POST = {True: [s for s in PROJ if by_dve(s[1], s[2])], False: [s for s in PROJ if not by_dve(s[1], s[2])]}
    TR = [s for s in PROJ if s[1] != "va"]
    ATT = [(l, qt, kind, j) for l in range(DEPTH) for qt in qtiles[l] for kind in ("diff", "gqa") for j in (0, 1)]
    WOUT = [(l, t, n) for l in range(DEPTH) for t in qtiles[l] for n in (0, 1)]
    ADA = [(l, n) for l in range(DEPTH) for n in range(N_ADA)]
    first_ada = 4
    heads_in = {"diff": 2, "gqa": 4}

    att0 = [n for n, u in enumerate(ATT) if u[0] == 0]
    rest = list(range(first_ada, len(ADA)))
    ada_at = {n: [] for n in range(len(ATT))}
    for i, x in enumerate(rest):
        ada_at[att0[i * len(att0) // len(rest)]].append(x)

    TU = ["c"]
    for l in range(DEPTH):
        TU += [("mod", l)] + [("hT", l, k) for k in range(KC)]
        TU += [("tr",) + s for s in TR if s[0] == l]
        units = [n for n, u in enumerate(ATT) if u[0] == l]
        for i, n in enumerate(units):
            TU += [("att", n, c) for c in range(heads_in[ATT[n][2]])]
            if i % 4 == 0 and i:
                TU += [("mix", l, ATT[n][1] - 1, h) for h in (0, 1)]
        TU += [("mix", l, qtiles[l][-1], h) for h in (0, 1)]
        TU += [("rt", l, t, h) for t in qtiles[l] for h in (0, 1)]
        TU += [("list", l)]
    tix = {key: i for i, key in enumerate(TU)}

    RS, col = {}, 0
    rs_order = []
    for l in range(DEPTH):
        evs = [("attn", l, TT, DM)] + [("sub", l, qt, HA, 128) for qt in qtiles[l]] + \
              [("ffn", l, t, 1, DM) for t in qtiles[l]]
        if l == DEPTH - 1:
            evs += [("fin", LT, DM)]
        for e in evs:
            RS[e[:-2]] = (col, e[-2], e[-1], len(rs_order))
            rs_order.append(e[:-2])
            col += e[-2]
    n_rs = col

    with ExitStack() as ctx:
        def sb(name, shape, dt=f32):
            return ctx.enter_context(nc.sbuf_tensor(name, shape, dt))

        def sem(name):
            return ctx.enter_context(nc.semaphore(name))

        ring = sb("ring", [P, 6, SLOTCOLS])
        X = sb("X", [P, TT, DM])
        hT = sb("hT", [P, KC, TOK])
        R2 = sb("R2", [P, 9728])
        R3 = sb("R3", [P, 5120])
        modrow = sb("modrow", [P, DEPTH * N_ADA, 128])
        cst = sb("cst", [P, C_ALL])
        wr = sb("wr", [P, KC, NE])
        tmp = sb("tmp", [P, 512])
        subb = sb("subb", [P, DEPTH, 128])
        mc = sb("mc", [P, 4 * KC])
        ng = sb("ng", [P, DEPTH * KC])
        Ac = sb("Ac", [P, 2, KC])
        cs = sb("cs", [P, KC, 2])
        craw = sb("craw", [P, 16])
        cth = sb("cth", [P, 16])
        ssq = sb("ssq", [P, n_rs])
        rstd = sb("rstd", [P, n_rs])
        sinkb = sb("sinkb", [P, DEPTH, HB])
        nsink = sb("nsink", [P, DEPTH, HB])
        broutb = sb("broutb", [P, NE])
        mhalf = sb("mhalf", [P, 4])
        nlam = sb("nlam", [P, DEPTH])
        lsum = sb("lsum", [P, 2 * DEPTH])
        lexp = sb("lexp", [P, 2 * DEPTH])
        rm = sb("rm", [P, 4])
        negm = sb("negm", [P, 4])
        sdif = sb("sdif", [P, 4])
        sexp = sb("sexp", [P, 2, 4])
        sums = sb("sums", [P, 2, 4])
        rec = sb("rec", [P, 2, 4])
        gate = sb("gate", [P, 2, TT])
        slot_ix = sb("slot_ix", [P, DEPTH, 2, TT], i32)
        row_ix = sb("row_ix", [P, DEPTH, 2, TT], i32)
        ntile = sb("ntile", [P, DEPTH, NE], i32)
        first_row = sb("first_row", [P, DEPTH, NE], i32)
        ix_next = sb("ix_next", [P, 3], i32)

        kaT = R2[:, 0:2048].rearrange("p (c t) -> p c t", c=4)
        qaT = R2[:, 2048:4096].rearrange("p (c t) -> p c t", c=4)
        qbT = R2[:, 4096:6144].rearrange("p (c t) -> p c t", c=4)
        kbT = R2[:, 6144:7168].rearrange("p (c t) -> p c t", c=2)
        Va = R2[:, 7168:9216].rearrange("p (t n) -> p t n", t=TT)
        Vb = R2[:, 9216:9728].rearrange("p (t n) -> p t n", t=TT)
        xn = R2[:, 2048:6144].rearrange("p (t n) -> p t n", t=TT)
        gA = R2[:, 0:2048].rearrange("p (s n) -> p s n", s=2)
        gF = R2[:, 2048:4096].rearrange("p (s n) -> p s n", s=2)
        Af = R2[:, 4096:6144].rearrange("p (s n) -> p s n", s=2)
        Bf = R2[:, 6144:8192].rearrange("p (s n) -> p s n", s=2)
        nfb = R2[:, 8192:9216]
        yk = R2[:, 4096:8192].rearrange("p (b k n) -> p b k n", b=2, k=2)
        rope_t1, rope_t2 = R3[:, 0:512], R3[:, 512:1024]
        stage = R3[:, 1024:2048].rearrange("p (b n) -> p b n", b=2)
        Pm = R3[:, 0:2048].rearrange("p (b n) -> p b n", b=4)
        PT = R3[:, 2048:4096].rearrange("p (b k q) -> p b k q", b=4, k=4)
        mix = R3[:, 4096:5120]
        hTs = R3[:, 0:1024].rearrange("p (k t) -> p k t", k=KC)
        junk = R3[:, 1024:2048]
        hb = R3[:, 2560:4608].rearrange("p (b n) -> p b n", b=2)
        lamb = R3[:, 0:512].rearrange("p (l i d) -> p l i d", l=DEPTH, i=4)
        lprod = R3[:, 512:768].rearrange("p (l i d) -> p l i d", l=DEPTH, i=2)
        crow = R3[0:32, 768:896]
        zlist = R3[:, 896:960]
        lst = R3[:, 2048:2176].rearrange("p (h s) -> p h s", h=2)
        xg = R2[:, 0:1536].rearrange("p (b n) -> p b n", b=3)
        y_s = R2[:, 4096:5120].rearrange("p (b n) -> p b n", b=2)
        xT = R3[:, 0:1536].rearrange("p (b j t) -> p b j t", b=3, j=4)
        th, t2, u_s = R3[:, 1536:1792], R3[:, 1792:2048], R3[:, 2048:2304]
        uT = R3[:, 2304:2560].rearrange("p (c t) -> p c t", c=2)
        g_ix = R3[:, 4608:4744].bitcast(i32)
        tri_b = R3[:, 4744:4808].bitcast(bf16)
        one_b = R3[:, 4808:4872].bitcast(bf16)
        mask_b = R3[:, 4872:4904].bitcast(bf16)
        ident = cst[:, C_ID:C_ID + P]

        S = ctx.enter_context(nc.psum_tensor("S", [P, 4, 512], f32))
        T = [ctx.enter_context(nc.psum_tensor(f"T{i}", [P, 512], f32)) for i in range(2)]
        O = ctx.enter_context(nc.psum_tensor("O", [P, 512], f32))
        AUX = ctx.enter_context(nc.psum_tensor("AUX", [P, 512], f32))

        mc_view = mc[:, :].rearrange("p (i x q) -> p x q i", i=2, x=first_ada)

        def mod_view(bank):
            return bank[:, :].rearrange("p (x q r) -> p x q r", x=first_ada, q=4)[:, :, :, 0:2]

        ut_bank = [S[:, 2, :], AUX]

        slot_full = [sem(f"slot_full{i}") for i in range(6)]
        names = """consts_in x_in small_in router_in bias_in clear_done bank_clear zero_list list_zeroed c_ready
            ada_done ada_out mod_stored1 mod_stored2 coeff_ready proj_done post_dve post_act t_full t_free_act
            t_free_dve act_ssq dve_ssq rstd_ready xn_ready scores_done negm_ready exps_done norm_done
            pv_done places_ready o_out mix_ready wout_done wout_out ga_in ab_in gf_in nfin_in ab_ready h_ready h_stored0 h_stored1
            logits_done sig_done mask_ready ranks_done counts_done slots_ready list_scattered list_in
            gix_ready ix_ready first_gathered0 first_gathered1 more_gathered first_flipped more_flipped
            first_ready more_ready up1_done up3_done tanh_done t2_done ua_done ub_done
            uta_done utb_done ea_done eb_done down_done y_out y_stored expert_done y_gathered0 y_gathered1 comb_done
            dve_self act_self pool_self lam_dot lam_exp fin_ready out_stored""".split()
        s = {n: sem(n) for n in names}
        t_free = [s["t_free_act"], s["t_free_dve"]]

        loads, where, last, count = [], {}, {}, [0] * 6

        def load(key, slot, src):
            count[slot] += 16
            loads.append((key, slot, src, last.get(slot)))
            where[key] = (slot, count[slot])

        def cols(w, c0, n):
            return w[:, c0:c0 + n].rearrange("(k p) n -> p k n", p=P)

        def load_ada(x, slot):
            l, n = ADA[x]
            load(("ada", x), slot, cols(a["w_ada"][l], 512 * n, 512))
            last[slot] = (s["ada_done"], x + 1)

        def load_in(l, u, slot):
            load(("in", l, u), slot, cols(a["w_in"][l], *UCOL[u]))
            t_last = max(i for i, st in enumerate(PROJ) if st[:2] == (l, u))
            last[slot] = (s["proj_done"], t_last + 1)

        def load_out(l, n, slot):
            load(("out", l, n), slot, cols(a["w_out"][l], 512 * n, 512))
            last[slot] = (s["wout_done"], 1 + max(i for i, st in enumerate(WOUT) if st[0] == l))

        def expert_src(l, e, part):
            w = a[("w1", "w3", "w2")[part]]
            if isinstance(e, int):
                one = w[l, e]
            else:
                one = w[l, ds(e, 1)].rearrange("a k n -> (a k) n")
            return one.rearrange("(k p) n -> p k n", p=P)

        def load_expert(l, e, part):
            load(("e", l, e, part), 3 * (e % 2) + part, expert_src(l, e, part))

        for x in range(first_ada):
            load_ada(x, x)
        for u, slot in zip(UNITS, (4, 5, 0, 1, 2)):
            load_in(0, u, slot)
        for i, x in enumerate(rest):
            load_ada(x, 3 + i % 3)
            if i == 2:
                for part in range(3):
                    load_expert(0, 0, part)
        for n in (0, 1):
            load_out(0, n, 3 + (len(rest) + n) % 3)
        loads.append("rows0")
        for part in range(3):
            load_expert(0, 1, part)
        loads.append("experts0")
        for i in range(6):
            count[i] += 16 * (NE // 2 - 1)
            last[i] = (s["expert_done"], NE - 1 if i < 3 else NE)
        for u, slot in zip(UNITS, (0, 1, 2, 3, 4)):
            load_in(1, u, slot)
        load_out(1, 0, 5)
        for part in range(3):
            load_expert(1, 0, part)
        load_out(1, 1, 4)
        load_expert(1, 1, 0)
        loads.append("rows1")
        for part in (1, 2):
            load_expert(1, 1, part)
        loads.append("experts1")

        def slot_view(slot, k):
            return ring[:, slot, :].rearrange("p (k n) -> p k n", k=k)

        block = ctx.enter_context(nc.Block())

        @block.sync
        def _(sp):
            def rows(l):
                streams = (0, 1) if l == 0 else (0,)
                sp.wait_ge(s["mod_stored1" if l == 0 else "mod_stored2"], 16 * 4)
                n_att = 1 + max(n for n, u in enumerate(ATT) if u[0] == l)
                sp.wait_ge(s["pv_done"], n_att)
                for i in streams:
                    sp.dma_start(gA[:, i, :], mod_d[l, i, 2 * DM:3 * DM].partition_broadcast(P)).then_inc(s["ga_in"], 16)
                for i in streams:
                    sp.dma_start(Af[:, i, :], mod_d[l, i, 4 * DM:5 * DM].partition_broadcast(P)).then_inc(s["ab_in"], 16)
                    sp.dma_start(Bf[:, i, :], mod_d[l, i, 3 * DM:4 * DM].partition_broadcast(P)).then_inc(s["ab_in"], 16)
                sp.dma_start(nfb, a["norm_ffn"][l].partition_broadcast(P)).then_inc(s["ab_in"], 16)
                for i in streams:
                    sp.dma_start(gF[:, i, :], mod_d[l, i, 5 * DM:6 * DM].partition_broadcast(P)).then_inc(s["gf_in"], 16)

            n_items = sp.alloc_register("sp_items")
            sp.reg_mov(n_items, 0)
            flying = []
            for item in loads:
                if item in ("rows0", "rows1"):
                    rows(int(item[-1]))
                elif item in ("experts0", "experts1"):
                    l = int(item[-1])
                    flying = []
                    sp.wait_ge(s["slots_ready"], l + 1)
                    with sp.Fori(1, NE // 2) as pair:
                        for half in range(2):
                            n = sp.value_load(ntile[0:1, l, ds(2 * pair + (half - 2), 1)], min_val=1, max_val=MAXT)
                            sp.reg_add(n_items, n_items, n)
                            for part, used in enumerate(("up1_done", "up3_done", "down_done")):
                                slot = 3 * half + part
                                sp.wait_ge(s["slots_ready"], l + 1)
                                sp.wait_ge(s[used], n_items)
                                early = (slot - 2) % 6
                                full = where[("e", l, early // 3, early % 3)][1] - (16 if slot < 2 else 0)
                                sp.wait_ge(slot_full[early], 16 * pair + full)
                                dst = slot_view(slot, 4 if part == 2 else 8)
                                sp.dma_start(dst, expert_src(l, 2 * pair + half, part)).then_inc(slot_full[slot], 16)
                    for half in range(2):
                        n = sp.value_load(ntile[0:1, l, NE - 2 + half:NE - 1 + half], min_val=1, max_val=MAXT)
                        sp.reg_add(n_items, n_items, n)
                    if l == 0:
                        for b in range(2):
                            sp.wait_ge(s[f"y_gathered{b}"], 32)
                else:
                    key, slot, src, free = item
                    if len(flying) >= 2:
                        sp.wait_ge(*flying[-2])
                    flying.append((slot_full[slot], where[key][1]))
                    if free is not None:
                        sp.wait_ge(*free)
                    k, n = src.shape[1], src.shape[2]
                    dst = ring[:, slot, 0:k * n].rearrange("p (k n) -> p k n", k=k)
                    sp.dma_start(dst, src).then_inc(slot_full[slot], 16)
            sp.wait_ge(s["ab_ready"], 2)
            sp.dma_start(nfb, a["norm_final"].partition_broadcast(P)).then_inc(s["nfin_in"], 16)
            for t in range(LT):
                sp.wait_ge(s["fin_ready"], t + 1)
                sp.dma_start(a["out"][0, t * P:(t + 1) * P, :], X[:, t, :]).then_inc(s["out_stored"], 16)
            sp.wait_ge(s["out_stored"], 16 * LT)

        @block.gpsimd
        def _(pool):
            self_ = Chain(pool, s["pool_self"])
            pool.memset(mhalf[:, :], -0.5)
            pool.memset(zlist, 0.0).then_inc(s["zero_list"], 1)
            pool.wait_ge(s["zero_list"], 1)
            pool.wait_ge(s["clear_done"], 1)
            src = a["b_ada"].rearrange("l (n q c) -> q (l n) c", q=4, c=128)
            for q in range(4):
                pool.dma_start(modrow[32 * q:32 * q + 2, :, :], src[q].partition_broadcast(2)).then_inc(s["bias_in"], 16)
            for l in range(DEPTH):
                pool.dma_start(list_d[l].rearrange("(p c) o -> p (c o)", p=P), zlist).then_inc(s["list_zeroed"], 16)

            def rsqrt(key):
                c0, w, n, i = RS[key]
                self_.step(pool.tensor_scalar(rstd[:, c0:c0 + w], ssq[:, c0:c0 + w], 1.0 / n, EPS, ALU.mult, ALU.add))
                pool.tensor_tensor(rstd[:, c0:c0 + w], rstd[:, c0:c0 + w], mhalf[:, 0:w], ALU.pow).then_inc(s["rstd_ready"], 1)

            def store_mod(l, n0, n1, stored):
                pool.wait_ge(s["ada_out"], l * N_ADA + n1)
                for q in range(4):
                    dst = mod_d[l].rearrange("i (n q c) -> q i n c", q=4, c=128)[q, :, n0:n1, :]
                    pool.dma_start(dst, modrow[32 * q:32 * q + 2, l * N_ADA + n0:l * N_ADA + n1, :]).then_inc(s[stored], 16)

            n_items = pool.alloc_register("pool_items")
            pool.reg_mov(n_items, 0)
            have, stored, n_gathers, n_more = (pool.alloc_register(f"pool_{n}") for n in ("have", "stored", "gathers", "more"))
            pool.reg_mov(n_gathers, 0)
            pool.reg_mov(n_more, 0)
            tiles = pool.alloc_register("pool_tiles")
            n_ssq = 0
            for l in range(DEPTH):
                n_ssq += TT
                pool.wait_ge(s["act_ssq"], n_ssq)
                rsqrt(("attn", l))
                for i, qt in enumerate(qtiles[l]):
                    pool.wait_ge(s["dve_ssq"], 1 + i + (0 if l == 0 else len(qtiles[0])))
                    rsqrt(("sub", l, qt))
                if l == 0:
                    store_mod(0, first_ada, N_ADA, "mod_stored1")
                    store_mod(1, first_ada, N_ADA, "mod_stored2")
                for t in qtiles[l]:
                    n_ssq += 1
                    pool.wait_ge(s["act_ssq"], n_ssq)
                    rsqrt(("ffn", l, t))
                pool.wait_ge(s["list_zeroed"], 16 * DEPTH)
                pool.wait_ge(s["places_ready"], l + 1)
                base = 32 * (0 if l == 0 else len(qtiles[0]))
                for t in qtiles[l]:
                    for k in range(2):
                        pool.indirect_dma_start(
                            out=list_d[l], out_offset=bass.IndirectOffsetOnAxis(ap=slot_ix[:, l, k, t:t + 1], axis=0),
                            in_=cst[:, C_TOK + t:C_TOK + t + 1], in_offset=None).then_inc(s["list_scattered"], 16)
                pool.wait_ge(s["list_scattered"], base + 32 * len(qtiles[l]))
                for h in range(2):
                    pool.dma_start(lst[:, h, :], list_d[l].rearrange("(p c) o -> p (c o)", p=P)).then_inc(s["list_in"], 16)
                pool.wait_ge(s["gix_ready"], l + 1)
                for b in range(2):
                    pool.wait_ge(s[f"h_stored{b}"], 8 * (len(qtiles[0]) + (len(qtiles[1]) if l else 0)))
                rows_of_h = h_d[l][0:P * len(qtiles[l]), :].rearrange("t (h d) -> (t h) d", h=2)

                def gather(column, buf, free, count):
                    pool.reg_add(n_gathers, n_gathers, 1)
                    pool.wait_ge(s["gix_ready"], l + 1)
                    pool.wait_ge(s[free], count)
                    pool.tensor_copy(ix_next[:, buf:buf + 1], g_ix[:, column]).then_inc(s["ix_ready"], 1)
                    pool.wait_ge(s["gix_ready"], l + 1)
                    pool.wait_ge(s["ix_ready"], n_gathers)
                    pool.indirect_dma_start(
                        out=xg[:, buf, :], out_offset=None, in_=rows_of_h,
                        in_offset=bass.IndirectOffsetOnAxis(ap=ix_next[:, buf:buf + 1], axis=0)
                    ).then_inc(s[("first_gathered0", "first_gathered1", "more_gathered")[buf]], 16)

                firsts = (NE + 1) * l
                pool.reg_mov(have, firsts)
                gather(slice(0, 1), 0, "first_flipped", have)
                with pool.Fori(0, NE // 2) as pair:
                    for half in range(2):
                        pool.reg_mov(have, 2 * pair + (half + firsts))
                        gather(ds((2 * pair + (half + 1)) * MAXT, 1), 1 - half, "first_flipped", have)
                        n = pool.value_load(ntile[0:1, l, ds(2 * pair + half, 1)], min_val=1, max_val=MAXT)
                        pool.reg_add(n_items, n_items, 1)
                        pool.reg_mov(tiles, n)
                        with pool.If_ne(tiles, 1), pool.Fori(1, n) as t:
                            gather(ds((2 * pair + half) * MAXT + t, 1), 2, "more_flipped", n_more)
                            pool.reg_add(n_more, n_more, 1)
                            pool.reg_add(n_items, n_items, 1)
                g = pool.snap(n_items, min_val=1, max_val=64)
                pool.reg_mov(stored, 32 * g)
                pool.wait_ge(s["gix_ready"], l + 1)
                pool.wait_ge(s["y_stored"], stored)
                done = 0 if l == 0 else len(qtiles[0])
                for i, t in enumerate(qtiles[l]):
                    if i >= 2:
                        pool.wait_ge(s["comb_done"], done + i - 1)
                    for k in range(2):
                        pool.indirect_dma_start(
                            out=yk[:, i % 2, k, :], out_offset=None, in_=y_d[l][0:TOPK * P * len(qtiles[l]), :],
                            in_offset=bass.IndirectOffsetOnAxis(ap=row_ix[:, l, k, t:t + 1], axis=0)
                        ).then_inc(s[f"y_gathered{i % 2}"], 16)
            n_ssq += LT
            pool.wait_ge(s["act_ssq"], n_ssq)
            rsqrt(("fin",))

        @block.scalar
        def _(act):
            act.dma_start(cst[:, :], a["consts"]).then_inc(s["consts_in"], 16)
            act.dma_start(crow[0:8, :], a["c"][0].rearrange("(r c) -> r c", c=128)).then_inc(s["consts_in"], 16)
            act.dma_start(crow[8:16, :], a["c_ctx"].rearrange("(r c) -> r c", c=128)).then_inc(s["consts_in"], 16)
            act.dma_start(crow[16:32, :], a["norm_attn"].rearrange("l (r c) -> (l r) c", c=128)).then_inc(s["consts_in"], 16)
            for t in range(TT):
                src = a["x"] if t < LT else a["ctx"]
                act.dma_start(X[:, t, :], src[0, (t % LT) * P:(t % LT + 1) * P, :]).then_inc(s["x_in"], 16)
            act.dma_start(lamb.rearrange("p l i d -> p (l i d)"),
                          a["lambda_qk"].rearrange("l i d -> (l i d)").partition_broadcast(P)).then_inc(s["small_in"], 16)
            act.dma_start(sinkb[:, :, :].rearrange("p l h -> p (l h)"),
                          a["sink"].rearrange("l h -> (l h)").partition_broadcast(P)).then_inc(s["small_in"], 16)
            act.dma_start(subb[:, :, :].rearrange("p l d -> p (l d)"),
                          a["subln"].rearrange("l d -> (l d)").partition_broadcast(P)).then_inc(s["small_in"], 16)
            act.dma_start(broutb[:, :], a["b_router"].partition_broadcast(P)).then_inc(s["small_in"], 16)
            act.dma_start(wr[:, :, :], a["w_router"].rearrange("(k p) n -> p k n", p=P)).then_inc(s["router_in"], 16)

            def full(key):
                act.wait_ge(s["t_full"], tix[key] + 1)
                return T[0]

            def mine(key):
                return tix[key] % 2 == 0

            def copy(out, in_):
                return act.activation(out, in_, ACT.Copy)

            full("c")
            copy(craw[:, :], T[0][:, 0:16])
            copy(ng[:, :], T[0][:, 16:32])
            act.activation(cth[:, :], T[0][:, 0:16], ACT.Tanh, scale=0.5).then_inc(s["t_free_act"], 1)

            squares = [0]

            def square_sum(t, key, c):
                c0 = RS[key][0]
                if squares[0]:
                    act.wait_ge(s["act_ssq"], squares[0])
                squares[0] += 1
                act.activation(junk, X[:, t, :], ACT.Square, accum_out=ssq[:, c0 + c:c0 + c + 1]).then_inc(s["act_ssq"], 1)

            n_items, n_more = act.alloc_register("act_items"), act.alloc_register("act_more")
            act.reg_mov(n_items, 0)
            act.reg_mov(n_more, 0)
            tiles = act.alloc_register("act_tiles")
            for l in range(DEPTH):
                if l == 0:
                    act.wait_ge(s["x_in"], 16 * TT)
                for t in range(TT):
                    if l and t < TT:
                        act.wait_ge(s["comb_done"], t + 1)
                    square_sum(t, ("attn", l), t)
                if mine(("mod", l)):
                    full(("mod", l))
                    copy(mc_view, mod_view(T[0])).then_inc(s["t_free_act"], 1)
                act.wait_ge(s["coeff_ready"], l + 1)
                for k in range(KC):
                    if mine(("hT", l, k)):
                        full(("hT", l, k))
                        for i in range(2):
                            ins = act.activation(hT[:, k, i * 256:(i + 1) * 256], T[0][:, i * 256:(i + 1) * 256],
                                                 ACT.Identity, bias=mc[:, 16 * i + k:16 * i + k + 1],
                                                 scale=Ac[:, i, k:k + 1])
                        ins.then_inc(s["t_free_act"], 1)
                if l == 0:
                    act.wait_ge(s["lam_dot"], 1)
                    act.activation(lexp[:, :], lsum[:, :], ACT.Exp).then_inc(s["lam_exp"], 1)

                def post(i):
                    _, u, t = PROJ[i]
                    if by_dve(u, t):
                        return
                    act.wait_ge(s["proj_done"], i + 1)
                    if u == "va":
                        copy(Va[:, t, :], S[:, i % 4, :]).then_inc(s["post_act"], 1)
                        return
                    j = TR.index(PROJ[i])
                    if j >= 2:
                        act.wait_ge(s["t_full"], tix[("tr",) + TR[j - 2]] + 1)
                    if u == "kvb":
                        src = S[:, i % 4, 0:128].rearrange("p (v o d) -> p v o d", v=2, o=1).to_broadcast([P, 2, 2, 64])
                        copy(stage[:, j % 2, 0:256].rearrange("p (v o d) -> p v o d", v=2, o=2), src)
                        copy(Vb[:, t, :], S[:, i % 4, 128:256]).then_inc(s["post_act"], 1)
                    else:
                        copy(stage[:, j % 2, :], S[:, i % 4, :]).then_inc(s["post_act"], 1)

                def take(key, dst, src_cols, c):
                    full(key)
                    src = T[0][:, 0:src_cols].rearrange("p (c t) -> p c t", c=c)
                    copy(dst, src).then_inc(s["t_free_act"], 1)

                idx = [i for i, st in enumerate(PROJ) if st[0] == l]
                for i in idx + [None]:
                    if i is not None:
                        post(i)
                    prev = (i - 1) if i is not None else idx[-1]
                    if prev >= idx[0] and PROJ[prev][1] != "va" and mine(("tr",) + PROJ[prev]):
                        _, u, t = PROJ[prev]
                        dst = {"ka": kaT, "qa": qaT, "qb": qbT, "kvb": kbT}[u]
                        c = 2 if u == "kvb" else 4
                        take(("tr",) + PROJ[prev], dst[:, :, t * P:(t + 1) * P], c * P, c)

                units = [n for n, u in enumerate(ATT) if u[0] == l]
                for i, n in enumerate(units):
                    _, qt, kind, j = ATT[n]
                    k0 = 0 if qt < LT else SEQ
                    act.wait_ge(s["negm_ready"], n + 1)
                    if i:
                        act.wait_ge(s["t_full"], tix[("att", n - 1, heads_in[ATT[n - 1][2]] - 1)] + 1)
                    else:
                        act.wait_ge(s["t_full"], max(tix[("tr",) + st] for st in TR if st[0] == l) + 1)
                    if kind == "gqa":
                        act.activation(sexp[:, n % 2, :], sdif[:, :], ACT.Exp)
                    for b in range(4):
                        ins = act.activation(Pm[:, b, 0:TOK - k0], S[:, b, 0:TOK - k0], ACT.Exp, bias=negm[:, b:b + 1],
                                             scale=SCALE, accum_out=sums[:, n % 2, b:b + 1])
                    ins.then_inc(s["exps_done"], 1)
                    nk = (TOK - k0) // P
                    for c in range(heads_in[kind]):
                        if mine(("att", n, c)):
                            take(("att", n, c), PT[:, c, 0:nk, :], nk * P, nk)
                    done = [qt - 1] if i % 4 == 0 and i else []
                    if i == len(units) - 1:
                        done.append(qt)
                    for q in done:
                        for h in (0, 1):
                            if mine(("mix", l, q, h)):
                                take(("mix", l, q, h), hT[:, 4 * h:4 * h + 4, q * P:(q + 1) * P], 512, 4)

                base = 0 if l == 0 else len(qtiles[0])
                w0 = WOUT.index((l, 0, 0))
                for i, t in enumerate(qtiles[l]):
                    act.wait_ge(s["wout_out"], w0 + 2 * i + 2)
                    square_sum(t, ("ffn", l, t), 0)
                    act.wait_ge(s["h_ready"], base + i + 1)
                    act.dma_start(h_d[l][t * P:(t + 1) * P, :], hb[:, i % 2, :]).then_inc(s[f"h_stored{i % 2}"], 16)
                    for h in (0, 1):
                        if mine(("rt", l, t, h)):
                            take(("rt", l, t, h), hTs[:, 4 * h:4 * h + 4, :], 512, 4)
                nt = len(qtiles[l])
                act.wait_ge(s["logits_done"], base + nt)
                act.activation(junk[:, 0:nt * NE], AUX[:, 0:nt * NE], ACT.Tanh, scale=0.5).then_inc(s["sig_done"], 1)
                if mine(("list", l)):
                    full(("list", l))
                    act.activation(g_ix[:, P:P + MAXT], T[0][:, 0:MAXT], ACT.Identity, bias=cst[:, C_H:C_H + 1], scale=2.0)
                    act.activation(g_ix[:, 0:P], T[0][:, 0:P], ACT.Identity, bias=cst[:, C_H:C_H + 1],
                                   scale=2.0).then_inc(s["t_free_act"], 1)

                firsts = (NE + 1) * l

                def take_tokens(buf, flipped, count, ready):
                    act.wait_ge(s[flipped], count)
                    copy(xT[:, buf], O[:, :].rearrange("p (j t) -> p j t", j=4)).then_inc(s[ready], 1)

                def item(half, row, first, have):
                    g = act.snap(n_items, min_val=0, max_val=64)
                    act.wait_ge(s["up1_done"], g + 1)
                    act.activation(th, S[:, 0, 0:256], ACT.Tanh, scale=0.5).then_inc(s["tanh_done"], 1)
                    if first:
                        take_tokens(1 - half, "first_flipped", have, "first_ready")
                    act.wait_ge(s["down_done"], g + 1)
                    if not first:
                        act.wait_ge(s["y_stored"], 32 * g)
                    copy(y_s[:, half, :], S[:, 3, :]).then_inc(s["y_out"], 1)
                    act.wait_ge(s["y_stored"], 32 * g)
                    act.wait_ge(s["y_out"], g + 2)
                    for h in range(2):
                        dst = y_d[l][ds(row, TILE), 512 * h:512 * h + 512]
                        act.dma_start(dst, y_s[64 * h:64 * h + 64, half, :]).then_inc(s["y_stored"], 16)
                    act.reg_add(n_items, n_items, 1)

                take_tokens(0, "first_flipped", firsts + 1, "first_ready")
                if l == 0:
                    copy(sexp[:, 0, 0:1], sexp[:, 0, 0:1]).then_inc(s["y_out"], 1)
                with act.Fori(0, NE // 2) as pair:
                    for half in range(2):
                        n = act.value_load(ntile[0:1, l, ds(2 * pair + half, 1)], min_val=1, max_val=MAXT)
                        row0 = act.value_load(first_row[0:1, l, ds(2 * pair + half, 1)], min_val=0, max_val=TOPK * P * nt)
                        item(half, row0, True, 2 * pair + (firsts + half + 2))
                        act.reg_mov(tiles, n)
                        with act.If_ne(tiles, 1), act.Fori(1, n) as t:
                            act.reg_add(n_more, n_more, 1)
                            take_tokens(2, "more_flipped", n_more, "more_ready")
                            item(half, row0 + t * TILE, False, None)
            base = len(qtiles[0])
            for t in range(LT):
                act.wait_ge(s["comb_done"], base + t + 1)
                square_sum(t, ("fin",), t)

        @block.vector
        def _(dve):
            ch = Chain(dve, s["dve_self"])

            def full(key):
                dve.wait_ge(s["t_full"], tix[key] + 1)
                return T[1]

            def mine(key):
                return tix[key] % 2 == 1

            def bc(ap, shape):
                return ap.to_broadcast(shape)

            dve.memset(modrow[:, :, :], 0.0).then_inc(s["clear_done"], 1)
            dve.memset(AUX[:, :], 0.0).then_inc(s["bank_clear"], 1)
            dve.wait_ge(s["consts_in"], 64)
            dve.wait_ge(s["t_free_act"], 1)
            ch.step(dve.scalar_tensor_tensor(cth[:, :], cth[:, :], 1.0, craw[:, :], ALU.add, ALU.mult))
            dve.tensor_scalar(cs[:, :, :], cth[:, :].rearrange("p (i k) -> p k i", i=2), 0.5, None, ALU.mult).then_inc(s["c_ready"], 1)

            def ada_out(x):
                dve.wait_ge(s["ada_done"], x + 1)
                dve.tensor_tensor(modrow[:, x, :], modrow[:, x, :], AUX[:, 0:128], ALU.add).then_inc(s["ada_out"], 1)

            dve.wait_ge(s["bias_in"], 16 * 4)
            for x in range(2):
                ada_out(x)

            n_items = dve.alloc_register("dve_items")
            dve.reg_mov(n_items, 0)
            for l in range(DEPTH):
                base = 0 if l == 0 else len(qtiles[0])
                nt = len(qtiles[l])
                c0, _, _, ev = RS[("attn", l)]
                dve.wait_ge(s["rstd_ready"], ev + 1)
                for t in range(TT):
                    dve.tensor_scalar(xn[:, t, :], X[:, t, :], rstd[:, c0 + t:c0 + t + 1], None, ALU.mult).then_inc(s["xn_ready"], 1)
                if l == 0:
                    for x in range(2, first_ada):
                        ada_out(x)
                if mine(("mod", l)):
                    full(("mod", l))
                    dve.tensor_copy(mc_view, mod_view(T[1])).then_inc(s["t_free_dve"], 1)
                dve.wait_ge(t_free[tix[("mod", l)] % 2], tix[("mod", l)] // 2 + 1)
                for i in range(2):
                    ins = dve.scalar_tensor_tensor(Ac[:, i, :], mc[:, 16 * i + 8:16 * i + 16], 1.0, ng[:, KC * l:KC * l + KC], ALU.add, ALU.mult)
                ins.then_inc(s["coeff_ready"], 1)
                dve.wait_ge(s["coeff_ready"], l + 1)
                for k in range(KC):
                    if mine(("hT", l, k)):
                        full(("hT", l, k))
                        for i in range(2):
                            ins = dve.tensor_scalar(hT[:, k, i * 256:(i + 1) * 256], T[1][:, i * 256:(i + 1) * 256],
                                                    Ac[:, i, k:k + 1], mc[:, 16 * i + k:16 * i + k + 1], ALU.mult, ALU.add)
                        ins.then_inc(s["t_free_dve"], 1)
                if l == 0:
                    dve.wait_ge(s["list_zeroed"], 16 * DEPTH)
                    dve.wait_ge(s["small_in"], 64)
                    ch.step(dve.tensor_tensor(lprod, lamb[:, :, 0::2, :], lamb[:, :, 1::2, :], ALU.mult))
                    dve.tensor_reduce(lsum[:, :].rearrange("p (l i) -> p l i", l=DEPTH), lprod, AX.X, ALU.add).then_inc(s["lam_dot"], 1)
                    dve.tensor_scalar(nsink[:, :, :], sinkb[:, :, :], -1.0, None, ALU.mult)
                    for m in range(DEPTH):
                        lam_init = 0.8 - 0.6 * math.exp(-0.3 * m)
                        dve.tensor_scalar(subb[:, m, :], subb[:, m, :], 1.0 - lam_init, None, ALU.mult)
                    dve.wait_ge(s["lam_exp"], 1)
                    for m in range(DEPTH):
                        lam_init = 0.8 - 0.6 * math.exp(-0.3 * m)
                        ch.step(dve.tensor_tensor(nlam[:, m:m + 1], lexp[:, 2 * m + 1:2 * m + 2], lexp[:, 2 * m:2 * m + 1], ALU.subtract))
                        ch.step(dve.tensor_scalar(nlam[:, m:m + 1], nlam[:, m:m + 1], -lam_init, None, ALU.add))

                def rope(src, heads, t, outs):
                    n = heads * 64
                    v = lambda ap: ap[:, 0:n].rearrange("p (h x b f) -> p h x b f", h=heads, x=2, b=2)
                    tab = cst[:, C_ROPE + 128 * t:C_ROPE + 128 * t + 128]
                    cosv = tab[:, 0:64].rearrange("p (o d) -> p o d", o=1)
                    sinv = tab[:, 64:128].rearrange("p (o x b f) -> p o x b f", o=1, x=2, b=2)
                    dve.tensor_tensor(rope_t1[:, 0:n].rearrange("p (h d) -> p h d", h=heads),
                                      src[:, 0:n].rearrange("p (h d) -> p h d", h=heads), bc(cosv, [P, heads, 64]), ALU.mult)
                    for b in range(2):
                        ins = dve.tensor_tensor(v(rope_t2)[:, :, :, b, :], v(src)[:, :, :, 1 - b, :],
                                                bc(sinv[:, :, :, b, :], [P, heads, 2, 16]), ALU.mult)
                    ch.step(ins)
                    for out in outs:
                        ins = dve.tensor_tensor(out, rope_t1[:, 0:n].rearrange("p (h d) -> p h d", h=heads),
                                                rope_t2[:, 0:n].rearrange("p (h d) -> p h d", h=heads), ALU.add)
                    return ins

                def post(i):
                    _, u, t = PROJ[i]
                    if not by_dve(u, t):
                        return
                    dve.wait_ge(s["proj_done"], i + 1)
                    j = TR.index(PROJ[i])
                    if j >= 2:
                        dve.wait_ge(s["t_full"], tix[("tr",) + TR[j - 2]] + 1)
                    src = S[:, i % 4, :]
                    if u == "kvb":
                        dve.tensor_copy(Vb[:, t, :], src[:, 128:256])
                        st = stage[:, j % 2, 0:256].rearrange("p (v o d) -> p v o d", v=2, o=2)
                        ch.step(rope(src, 2, t, [st[:, :, 0, :], st[:, :, 1, :]]))
                    else:
                        ch.step(rope(src, 8, t, [stage[:, j % 2, :].rearrange("p (h d) -> p h d", h=8)]))
                    dve.tensor_scalar(sdif[:, 0:1], nlam[:, 0:1], 1.0, None, ALU.mult).then_inc(s["post_dve"], 1)

                def take(key, dst, src_cols, c):
                    full(key)
                    dve.tensor_copy(dst, T[1][:, 0:src_cols].rearrange("p (c t) -> p c t", c=c)).then_inc(s["t_free_dve"], 1)

                idx = [i for i, st in enumerate(PROJ) if st[0] == l]
                for i in idx + [None]:
                    if i is not None:
                        post(i)
                    prev = (i - 1) if i is not None else idx[-1]
                    if prev >= idx[0] and PROJ[prev][1] != "va" and mine(("tr",) + PROJ[prev]):
                        _, u, t = PROJ[prev]
                        dst = {"ka": kaT, "qa": qaT, "qb": qbT, "kvb": kbT}[u]
                        c = 2 if u == "kvb" else 4
                        take(("tr",) + PROJ[prev], dst[:, :, t * P:(t + 1) * P], c * P, c)

                units = [n for n, u in enumerate(ATT) if u[0] == l]

                def row_max(n):
                    _, qt, kind, j = ATT[n]
                    k0 = 0 if qt < LT else SEQ
                    dve.wait_ge(s["scores_done"], n + 1)
                    ch.step(dve.tensor_reduce(rm[:, :], S[:, :, 0:TOK - k0], AX.X, ALU.max))
                    if kind == "diff":
                        dve.tensor_scalar(negm[:, :], rm[:, :], -SCALE, None, ALU.mult).then_inc(s["negm_ready"], 1)
                    else:
                        ch.step(dve.scalar_tensor_tensor(negm[:, :], rm[:, :], -SCALE, nsink[:, l, 4 * j:4 * j + 4], ALU.mult, ALU.min))
                        dve.tensor_tensor(sdif[:, :], negm[:, :], sinkb[:, l, 4 * j:4 * j + 4], ALU.add).then_inc(s["negm_ready"], 1)

                row_max(units[0])
                for i, n in enumerate(units):
                    _, qt, kind, j = ATT[n]
                    nkey = TOK if qt < LT else CTX
                    dve.wait_ge(s["exps_done"], n + 1)
                    sm, rc = sums[:, n % 2, :], rec[:, n % 2, :]
                    if kind == "gqa":
                        ch.step(dve.tensor_tensor(sm, sm, sexp[:, n % 2, :], ALU.add))
                    ch.step(dve.reciprocal(rc, sm))
                    if kind == "diff":
                        ch.step(dve.tensor_scalar(rec[:, n % 2, 1::2], rec[:, n % 2, 1::2], nlam[:, l:l + 1], None, ALU.mult))
                        for h in range(2):
                            ch.step(dve.tensor_scalar(Pm[:, 2 * h, 0:nkey], Pm[:, 2 * h, 0:nkey], rc[:, 2 * h:2 * h + 1], None, ALU.mult))
                            dve.scalar_tensor_tensor(Pm[:, 2 * h, 0:nkey], Pm[:, 2 * h + 1, 0:nkey], rc[:, 2 * h + 1:2 * h + 2],
                                                     Pm[:, 2 * h, 0:nkey], ALU.mult, ALU.add).then_inc(s["norm_done"], 1)
                    if i + 1 < len(units):
                        row_max(n + 1)
                    nk = nkey // P
                    for x in ada_at[n]:
                        ada_out(x)
                    for c in range(heads_in[kind]):
                        if mine(("att", n, c)):
                            take(("att", n, c), PT[:, c, 0:nk, :], nk * P, nk)
                    dve.wait_ge(s["pv_done"], n + 1)
                    if kind == "diff":
                        if j == 0 and i:
                            dve.wait_ge(s["t_full"], tix[("mix", l, qt - 1, 1)] + 1)
                        dve.tensor_copy(mix[:, 256 * j:256 * j + 256], O[:, 0:256]).then_inc(s["o_out"], 1)
                        if j == 1:
                            dve.wait_ge(s["o_out"], n + 1)
                            ch.step(dve.tensor_tensor(tmp[:, :], mix[:, 0:512], mix[:, 0:512], ALU.mult))
                            c0 = RS[("sub", l, qt)][0]
                            dve.tensor_reduce(ssq[:, c0:c0 + HA], tmp[:, :].rearrange("p (h d) -> p h d", h=HA), AX.X,
                                              ALU.add).then_inc(s["dve_ssq"], 1)
                    else:
                        dve.tensor_tensor(mix[:, 512 + 256 * j:768 + 256 * j].rearrange("p (h d) -> p h d", h=4),
                                          O[:, 0:256].rearrange("p (h d) -> p h d", h=4),
                                          bc(rc.rearrange("p (h o) -> p h o", o=1), [P, 4, 64]), ALU.mult).then_inc(s["o_out"], 1)
                        if j == 1:
                            c0, _, _, ev = RS[("sub", l, qt)]
                            dve.wait_ge(s["rstd_ready"], ev + 1)
                            mv = mix[:, 0:512].rearrange("p (h d) -> p h d", h=HA)
                            ch.step(dve.tensor_tensor(mv, mv, bc(rstd[:, c0:c0 + HA].rearrange("p (h o) -> p h o", o=1), [P, HA, 128]), ALU.mult))
                            dve.tensor_tensor(mv, mv, bc(subb[:, l, :].rearrange("p (o d) -> p o d", o=1), [P, HA, 128]),
                                              ALU.mult).then_inc(s["mix_ready"], 1)
                    done = [qt - 1] if i % 4 == 0 and i else []
                    if i == len(units) - 1:
                        done.append(qt)
                    for q in done:
                        for h in (0, 1):
                            if mine(("mix", l, q, h)):
                                take(("mix", l, q, h), hT[:, 4 * h:4 * h + 4, q * P:(q + 1) * P], 512, 4)

                streams = 2 if l == 0 else 1
                dve.wait_ge(s["ga_in"], 32 if l == 0 else 48)
                w0 = WOUT.index((l, 0, 0))

                def residual(t):
                    for n in range(2):
                        w = WOUT.index((l, t, n))
                        if w:
                            dve.wait_ge(s["wout_out"], w)
                        dve.wait_ge(s["wout_done"], w + 1)
                        ch.step(dve.tensor_tensor(tmp[:, :], S[:, w % 4, :], gA[:, t // LT, n * 512:(n + 1) * 512], ALU.mult))
                        xs = X[:, t, n * 512:(n + 1) * 512]
                        dve.tensor_tensor(xs, xs, tmp[:, :], ALU.add).then_inc(s["wout_out"], 1)

                def ffn_input(i, t):
                    c0, _, _, ev = RS[("ffn", l, t)]
                    dve.wait_ge(s["rstd_ready"], ev + 1)
                    if i >= 2:
                        dve.wait_ge(s[f"h_stored{i % 2}"], 16 * (base // 2 + i // 2))
                        dve.wait_ge(s["t_full"], tix[("rt", l, t - 2, 1)] + 1)
                    ch.step(dve.scalar_tensor_tensor(hb[:, i % 2, :], X[:, t, :], rstd[:, c0:c0 + 1], Af[:, t // LT, :], ALU.mult, ALU.mult))
                    dve.tensor_tensor(hb[:, i % 2, :], hb[:, i % 2, :], Bf[:, t // LT, :], ALU.add).then_inc(s["h_ready"], 1)

                def take_rt(t):
                    for h in (0, 1):
                        if mine(("rt", l, t, h)):
                            take(("rt", l, t, h), hTs[:, 4 * h:4 * h + 4, :], 512, 4)

                residual(0)
                dve.wait_ge(s["ab_in"], 80 if l == 0 else 80 + 48)
                for i in range(streams):
                    ins = dve.scalar_tensor_tensor(Af[:, i, :], Af[:, i, :], 1.0, nfb, ALU.add, ALU.mult)
                    if i < streams - 1:
                        ch.step(ins)
                ins.then_inc(s["ab_ready"], 1)
                dve.wait_ge(s["ab_ready"], l + 1)
                for i, t in enumerate(qtiles[l]):
                    ffn_input(i, t)
                    take_rt(t)
                    if i + 1 < nt:
                        residual(t + 1)

                W = nt * NE
                R = [junk[:, 64 * i:64 * i + W] for i in range(14)]
                g4 = lambda ap: ap.rearrange("p (a e) -> p a e", e=EPG)
                G = [junk[:, 896 + 16 * i:896 + 16 * i + nt * NG] for i in range(8)]
                ch.step(dve.tensor_copy(tri_b, cst[:, C_TRI:C_TRI + P]))
                ch.step(dve.memset(one_b, 1.0))
                dve.wait_ge(s["sig_done"], l + 1)
                sg, sbv, e1, k1, o1, s2 = R[1], R[2], R[3], R[4], R[5], R[6]
                A4 = [P, nt * NG, EPG]
                dec = bc(cst[:, C_DEC:C_DEC + EPG].rearrange("p (o e) -> p o e", o=1), A4)
                up = lambda ap: bc(ap.rearrange("p (a o) -> p a o", o=1), A4)
                ch.step(dve.tensor_scalar(sg, R[0], 0.5, 0.5, ALU.mult, ALU.add))
                ch.step(dve.tensor_tensor(sbv.rearrange("p (t e) -> p t e", e=NE), sg.rearrange("p (t e) -> p t e", e=NE),
                                          bc(broutb[:, :].rearrange("p (o e) -> p o e", o=1), [P, nt, NE]), ALU.add))

                def best(vals, top, onehot, dec_, up_, view, top_view):
                    ch.step(dve.tensor_reduce(top, view(vals), AX.X, ALU.max))
                    ch.step(dve.tensor_tensor(view(e1), view(vals), up_(top), ALU.is_equal))
                    ch.step(dve.tensor_tensor(view(e1), view(e1), dec_, ALU.mult))
                    ch.step(dve.tensor_reduce(top_view, view(e1), AX.X, ALU.max))
                    ch.step(dve.tensor_tensor(view(onehot), view(e1), up_(top_view), ALU.is_equal))

                best(sbv, G[0], o1, dec, up, g4, G[1])
                ch.step(dve.scalar_tensor_tensor(s2, o1, -3e38, sbv, ALU.mult, ALU.add))
                o2 = k1
                best(s2, G[2], o2, dec, up, g4, G[3])
                ch.step(dve.tensor_tensor(G[4], G[0], G[2], ALU.add))
                tg = lambda ap: ap.rearrange("p (t g) -> p t g", g=NG)
                G3 = [P, nt, NG]
                upg = lambda ap: bc(ap.rearrange("p (t o) -> p t o", o=1), G3)
                gm, gk = G[5][:, 0:nt], G[6][:, 0:nt]
                decg = bc(cst[:, C_DECG:C_DECG + NG].rearrange("p (o g) -> p o g", o=1), G3)
                ch.step(dve.tensor_reduce(gm, tg(G[4]), AX.X, ALU.max))
                ch.step(dve.tensor_tensor(tg(G[1]), tg(G[4]), upg(gm), ALU.is_equal))
                ch.step(dve.tensor_tensor(tg(G[1]), tg(G[1]), decg, ALU.mult))
                ch.step(dve.tensor_reduce(gk, tg(G[1]), AX.X, ALU.max))
                ch.step(dve.tensor_tensor(tg(G[1]), tg(G[1]), upg(gk), ALU.is_equal))
                ch.step(dve.tensor_tensor(g4(o1), g4(o1), up(G[1]), ALU.mult))
                ch.step(dve.tensor_tensor(g4(o2), g4(o2), up(G[1]), ALU.mult))
                dve.tensor_tensor(mask_b[:, 0:W], o1, o2, ALU.add).then_inc(s["mask_ready"], 1)
                te = lambda ap: ap.rearrange("p (t e) -> p t e", e=NE)
                dve.wait_ge(s["ranks_done"], l + 1)
                cnt = AUX[:, 256:256 + NE]
                rank = AUX[:, 128:128 + W].rearrange("p (t e) -> p t e", e=NE)

                def places(start, out):
                    ch.step(dve.tensor_tensor(te(R[9]), rank, bc(start.rearrange("p (o e) -> p o e", o=1), [P, nt, NE]), ALU.add))
                    for k, oh in enumerate((o1, o2)):
                        ch.step(dve.tensor_tensor(R[10 + k], R[9], oh, ALU.mult))
                    for k in range(2):
                        ch.step(dve.tensor_reduce(G[k][:, 0:nt], te(R[10 + k]), AX.X, ALU.add))
                    for k in range(2):
                        ins = dve.tensor_copy(out[:, l, k, 0:nt], G[k][:, 0:nt])
                    return ins

                places(cst[:, C_EB:C_EB + NE], slot_ix).then_inc(s["places_ready"], 1)
                before = tmp[:, 0:NE * NE].rearrange("p (e f) -> p e f", e=NE)
                ch.step(dve.tensor_tensor(before, bc(cnt.rearrange("p (o f) -> p o f", o=1), [P, NE, NE]),
                                          cst[:, C_BEF:C_ALL].rearrange("p (e f) -> p e f", e=NE), ALU.mult))
                ch.step(dve.tensor_reduce(R[13][:, 0:NE], before, AX.X, ALU.add))
                ch.step(dve.tensor_copy(first_row[:, l, :], R[13][:, 0:NE]))
                dve.wait_ge(s["places_ready"], l + 1)
                ch.step(places(R[13][:, 0:NE], row_ix))
                for k, oh in enumerate((o1, o2)):
                    ch.step(dve.tensor_tensor(R[7 + k], sg, oh, ALU.mult))
                    ch.step(dve.tensor_reduce(gate[:, k, 0:nt], te(R[7 + k]), AX.X, ALU.add))
                den = G[7][:, 0:nt]
                ch.step(dve.tensor_tensor(den, gate[:, 0, 0:nt], gate[:, 1, 0:nt], ALU.add))
                ch.step(dve.reciprocal(den, den))
                for k in range(2):
                    ch.step(dve.tensor_tensor(gate[:, k, 0:nt], gate[:, k, 0:nt], den, ALU.mult))
                big = tmp[:, 0:NE * (MAXT - 1)].rearrange("p (e j) -> p e j", e=NE)
                ch.step(dve.tensor_tensor(big, bc(cnt.rearrange("p (e o) -> p e o", o=1), [P, NE, MAXT - 1]),
                                          bc(cst[:, C_THR:C_BEF].rearrange("p (o j) -> p o j", o=1), [P, NE, MAXT - 1]), ALU.is_gt))
                ch.step(dve.tensor_reduce(R[12][:, 0:NE], big, AX.X, ALU.add))
                dve.tensor_scalar(ntile[:, l, :], R[12][:, 0:NE], 1.0, None, ALU.add).then_inc(s["slots_ready"], 1)
                if mine(("list", l)):
                    full(("list", l))
                    dve.tensor_scalar(g_ix[:, P:P + MAXT], T[1][:, 0:MAXT], 2.0, cst[:, C_H:C_H + 1], ALU.mult, ALU.add)
                    dve.tensor_scalar(g_ix[:, 0:P], T[1][:, 0:P], 2.0, cst[:, C_H:C_H + 1], ALU.mult, ALU.add).then_inc(s["t_free_dve"], 1)
                dve.wait_ge(t_free[tix[("list", l)] % 2], tix[("list", l)] // 2 + 1)
                dve.tensor_copy(tmp[:, 0:1], cst[:, C_H:C_H + 1]).then_inc(s["gix_ready"], 1)
                dve.wait_ge(s["slots_ready"], l + 1)

                with dve.Fori(0, NE) as e:
                    n = dve.value_load(ntile[0:1, l, ds(e, 1)], min_val=1, max_val=MAXT)
                    with dve.Fori(0, n) as t:
                        g = dve.snap(n_items, min_val=0, max_val=64)
                        dve.wait_ge(s["tanh_done"], g + 1)
                        dve.scalar_tensor_tensor(t2, th, 1.0, S[:, 0, 0:256], ALU.add, ALU.mult).then_inc(s["t2_done"], 1)
                        dve.wait_ge(s["t2_done"], g + 1)
                        dve.wait_ge(s["up3_done"], g + 1)
                        for c, name in enumerate(("ua_done", "ub_done")):
                            dve.scalar_tensor_tensor(u_s[:, 128 * c:128 * c + 128], t2[:, 128 * c:128 * c + 128], 0.5,
                                                     S[:, 1, 128 * c:128 * c + 128], ALU.mult, ALU.mult).then_inc(s[name], 1)
                        dve.wait_ge(s["uta_done"], g + 1)
                        dve.tensor_copy(uT[:, 0, :], ut_bank[0][:, 0:P]).then_inc(s["ea_done"], 1)
                        dve.wait_ge(s["utb_done"], g + 1)
                        dve.tensor_copy(uT[:, 1, :], ut_bank[1][:, 0:P]).then_inc(s["eb_done"], 1)
                        dve.reg_add(n_items, n_items, 1)

                dve.wait_ge(s["gf_in"], 32 if l == 0 else 48)
                for i, t in enumerate(qtiles[l]):
                    dve.wait_ge(s[f"y_gathered{i % 2}"], 32 * (base // 2 + i // 2 + 1))
                    y0, y1 = yk[:, i % 2, 0, :], yk[:, i % 2, 1, :]
                    ch.step(dve.tensor_scalar(y0, y0, gate[:, 0, t:t + 1], None, ALU.mult))
                    ch.step(dve.scalar_tensor_tensor(y0, y1, gate[:, 1, t:t + 1], y0, ALU.mult, ALU.add))
                    ch.step(dve.tensor_tensor(y0, y0, gF[:, t // LT, :], ALU.mult))
                    dve.tensor_tensor(X[:, t, :], X[:, t, :], y0, ALU.add).then_inc(s["comb_done"], 1)
            c0, _, _, ev = RS[("fin",)]
            dve.wait_ge(s["rstd_ready"], ev + 1)
            dve.wait_ge(s["nfin_in"], 16)
            for t in range(LT):
                dve.scalar_tensor_tensor(X[:, t, :], X[:, t, :], rstd[:, c0 + t:c0 + t + 1], nfb, ALU.mult, ALU.mult).then_inc(s["fin_ready"], 1)

        @block.tensor
        def _(pe):
            def weights(key):
                slot, n = where[key]
                pe.wait_ge(slot_full[slot], n)
                return slot

            def bank(key):
                k = tix[key]
                if k >= 2:
                    pe.wait_ge(t_free[k % 2], k // 2)
                return T[k % 2]

            def taken(key):
                k = tix[key]
                pe.wait_ge(t_free[k % 2], k // 2 + 1)

            def transposes(key, srcs):
                b, at = bank(key), 0
                for src in srcs:
                    rows = src.shape[0]
                    ins = pe.transpose(b[0:src.shape[1], at:at + rows], src, cst[0:rows, C_ID:C_ID + rows])
                    at += rows
                ins.then_inc(s["t_full"], 1)

            pe.wait_ge(s["consts_in"], 64)
            transposes("c", [crow])
            pe.wait_ge(s["c_ready"], 1)
            pe.wait_ge(s["bank_clear"], 1)

            def ada(x):
                slot = weights(("ada", x))
                if x:
                    pe.wait_ge(s["ada_out"], x)
                w = slot_view(slot, KC)
                for k in range(KC):
                    for q in range(4):
                        ins = pe.matmul(AUX[32 * q:32 * q + 2, 0:128], cs[:, k, :], w[:, k, 128 * q:128 * q + 128],
                                        start=(k == 0), stop=(k == KC - 1))
                ins.then_inc(s["ada_done"], 1)

            for x in range(first_ada):
                ada(x)

            n_items = pe.alloc_register("pe_items")
            pe.reg_mov(n_items, 0)
            n_more, have, emptied, last_y = (pe.alloc_register(f"pe_{n}") for n in ("more", "have", "emptied", "last_y"))
            pe.reg_mov(n_more, 0)
            tiles = pe.alloc_register("pe_tiles")
            for l in range(DEPTH):
                nt = len(qtiles[l])
                base = 0 if l == 0 else len(qtiles[0])
                pe.wait_ge(s["ada_out"], l * N_ADA + first_ada)
                transposes(("mod", l), [modrow[:, l * N_ADA + x, :] for x in range(first_ada)])
                pe.wait_ge(s["xn_ready"], TT * (l + 1))
                for k in range(KC):
                    transposes(("hT", l, k), [xn[:, t, k * P:(k + 1) * P] for t in range(TT)])
                taken(("hT", l, KC - 2))
                taken(("hT", l, KC - 1))

                def posted(i):
                    eng = by_dve(*PROJ[i][1:])
                    pe.wait_ge(s["post_dve" if eng else "post_act"], POST[eng].index(PROJ[i]) + 1)

                def tr(st):
                    posted(PROJ.index(st))
                    j = TR.index(st)
                    n = 2 if st[1] == "kvb" else 4
                    transposes(("tr",) + st, [stage[:, j % 2, c * P:(c + 1) * P] for c in range(n)])

                idx = [i for i, st in enumerate(PROJ) if st[0] == l]
                for i in idx:
                    _, u, t = PROJ[i]
                    slot = weights(("in", l, u))
                    width = UCOL[u][1]
                    w = ring[:, slot, 0:KC * width].rearrange("p (k n) -> p k n", k=KC)
                    if i - 4 >= idx[0]:
                        posted(i - 4)
                    for k in range(KC):
                        ins = pe.matmul(S[:, i % 4, 0:width], hT[:, k, t * P:(t + 1) * P], w[:, k, :],
                                        start=(k == 0), stop=(k == KC - 1))
                    ins.then_inc(s["proj_done"], 1)
                    if i > idx[0] and PROJ[i - 1][1] != "va":
                        tr(PROJ[i - 1])
                tr(PROJ[idx[-1]])

                trs = sorted(tix[("tr",) + st] for st in TR if st[0] == l)[-2:]
                for k in trs:
                    pe.wait_ge(t_free[k % 2], k // 2 + 1)
                for eng in (True, False):
                    pe.wait_ge(s["post_dve" if eng else "post_act"], len([st for st in POST[eng] if st[0] <= l]))
                units = [n for n, u in enumerate(ATT) if u[0] == l]

                def scores(n):
                    _, qt, kind, j = ATT[n]
                    k0 = 0 if qt < LT else SEQ
                    nkey = TOK - k0
                    q = slice(qt * P, (qt + 1) * P)
                    for b in range(4):
                        r = slice(64 * (b % 2), 64 * (b % 2) + 64)
                        biased = kind == "gqa" and qt < LT
                        if kind == "diff":
                            c = 2 * j + b // 2
                            lhs, rhs = qaT[r, c, q], kaT[r, c, k0:TOK]
                        else:
                            lhs, rhs = qbT[r, 2 * j + b // 2, q], kbT[r, j, k0:TOK]
                        ins = pe.matmul(S[:, b, 0:nkey], lhs, rhs, start=True, stop=not biased)
                    if biased:
                        blk = (1 - qt) * P
                        for b in range(4):
                            ins = pe.matmul(S[:, b, blk:blk + P], ident, cst[:, C_MB + P * qt:C_MB + P * qt + P],
                                            start=False, stop=True)
                    ins.then_inc(s["scores_done"], 1)

                def heads(n):
                    _, qt, kind, j = ATT[n]
                    t0 = 0 if qt < LT else LT
                    nk = TT - t0
                    nh = heads_in[kind]

                    def flip(c):
                        if kind == "diff":
                            pe.wait_ge(s["norm_done"], 2 * diffs[n] + c + 1)
                        else:
                            pe.wait_ge(s["exps_done"], n + 1)
                        row = 2 * c if kind == "diff" else c
                        transposes(("att", n, c), [Pm[:, row, kb * P:(kb + 1) * P] for kb in range(nk)])

                    def product(c):
                        taken(("att", n, c))
                        if c == 0 and n:
                            pe.wait_ge(s["o_out"], n)
                        for kb in range(nk):
                            if kind == "diff":
                                h = 2 * j + c
                                out, v = O[:, 128 * c:128 * c + 128], Va[:, t0 + kb, 128 * h:128 * h + 128]
                            else:
                                out, v = O[:, 64 * c:64 * c + 64], Vb[:, t0 + kb, 64 * j:64 * j + 64]
                            ins = pe.matmul(out, PT[:, c, kb, :], v, start=(kb == 0), stop=(kb == nk - 1))
                        return ins

                    flip(0)
                    for c in range(nh):
                        if c + 1 < nh:
                            flip(c + 1)
                        ins = product(c)
                    ins.then_inc(s["pv_done"], 1)

                diffs, d = {}, 0
                for n, u in enumerate(ATT):
                    diffs[n] = d
                    d += u[2] == "diff"

                def mixT(qt):
                    pe.wait_ge(s["mix_ready"], base + qt + 1)
                    for h in (0, 1):
                        transposes(("mix", l, qt, h), [mix[:, (4 * h + c) * P:(4 * h + c + 1) * P] for c in range(4)])

                scores(units[0])
                for i, n in enumerate(units):
                    if i + 1 < len(units):
                        pe.wait_ge(s["exps_done"], n + 1)
                        scores(n + 1)
                    for x in ada_at[n]:
                        ada(x)
                    heads(n)
                    if i % 4 == 0 and i:
                        mixT(ATT[n][1] - 1)
                mixT(qtiles[l][-1])

                slots = [weights(("out", l, n)) for n in (0, 1)]

                def out_proj(t):
                    for n in range(2):
                        w = WOUT.index((l, t, n))
                        if t == qtiles[l][0] and n == 0:
                            pe.wait_ge(s["exps_done"], units[-1] + 1)
                        if w - 4 >= WOUT.index((l, 0, 0)):
                            pe.wait_ge(s["wout_out"], w - 3)
                        if n == 0:
                            taken(("mix", l, t, 0))
                            taken(("mix", l, t, 1))
                        wv = slot_view(slots[n], KC)
                        for k in range(KC):
                            ins = pe.matmul(S[:, w % 4, :], hT[:, k, t * P:(t + 1) * P], wv[:, k, :],
                                            start=(k == 0), stop=(k == KC - 1))
                        ins.then_inc(s["wout_done"], 1)

                def logits(i, t):
                    pe.wait_ge(s["h_ready"], base + i + 1)
                    for h in (0, 1):
                        transposes(("rt", l, t, h), [hb[:, i % 2, (4 * h + c) * P:(4 * h + c + 1) * P] for c in range(4)])
                    for h in (0, 1):
                        taken(("rt", l, t, h))
                    for k in range(KC):
                        ins = pe.matmul(AUX[:, t * NE:(t + 1) * NE], hTs[:, k, :], wr[:, k, :], start=(k == 0), stop=(k == KC - 1))
                    ins.then_inc(s["logits_done"], 1)

                if l == 0:
                    pe.wait_ge(s["ada_out"], len(ADA))
                    pe.wait_ge(s["router_in"], 16)
                out_proj(0)
                for i, t in enumerate(qtiles[l]):
                    if i + 1 < nt:
                        out_proj(t + 1)
                    logits(i, t)

                pe.wait_ge(s["mask_ready"], l + 1)
                pe.wait_ge(s["sig_done"], l + 1)
                for t in range(nt):
                    for p_ in range(t + 1):
                        pe.matmul(AUX[:, 128 + t * NE:128 + (t + 1) * NE], tri_b if p_ == t else one_b,
                                  mask_b[:, p_ * NE:(p_ + 1) * NE], start=(p_ == 0), stop=(p_ == t))
                for p_ in range(nt):
                    ins = pe.matmul(AUX[:, 256:256 + NE], one_b, mask_b[:, p_ * NE:(p_ + 1) * NE],
                                    start=(p_ == 0), stop=(p_ == nt - 1))
                ins.then_inc(s["ranks_done"], 1)
                pe.wait_ge(s["list_in"], 32 * (l + 1))
                transposes(("list", l), [lst.rearrange("p h s -> p (h s)")])

                firsts = (NE + 1) * l

                def flip_tokens(buf, gathered, count, flipped):
                    pe.wait_ge(s[gathered], count)
                    for j in range(4):
                        ins = pe.transpose(O[:, j * P:(j + 1) * P], xg[:, buf, j * P:(j + 1) * P], ident)
                    ins.then_inc(s[flipped], 1)

                def item(half, pair, first):
                    part = [slot_view(3 * half + i, 4 if i == 2 else 8) for i in range(3)]
                    full0 = [where[("e", l, half, i)][1] for i in range(3)]
                    tokens = xT[:, half if first else 2]
                    g = pe.snap(n_items, min_val=0, max_val=64)
                    pe.wait_ge(s["slots_ready"], l + 1)
                    if first:
                        pe.wait_ge(s["first_ready"], have)
                    else:
                        pe.wait_ge(s["more_ready"], n_more)
                    for i, done in ((0, "up1_done"), (1, "up3_done")):
                        if first:
                            pe.wait_ge(slot_full[3 * half + i], 16 * pair + full0[i])
                        for k in range(KC):
                            for h in range(2):
                                ins = pe.matmul(S[64 * h:64 * h + 64, i, 0:256],
                                                tokens[:, k % 4, 64 * (k // 4):64 * (k // 4) + 64],
                                                part[i][:, k, h * 256:h * 256 + 256], start=(k == 0), stop=(k == KC - 1))
                        ins.then_inc(s[done], 1)
                    if first:
                        before = (NE // 2 + 1 if half else NE // 2) * l
                        flip_tokens(1 - half, f"first_gathered{1 - half}", 16 * pair + 16 * (before + 1 + half), "first_flipped")
                    for c, (made, done) in enumerate((("ua_done", "uta_done"), ("ub_done", "utb_done"))):
                        pe.wait_ge(s[made], g + 1)
                        pe.transpose(ut_bank[c][:, 0:P], u_s[:, c * P:(c + 1) * P], ident).then_inc(s[done], 1)
                    pe.wait_ge(s["ea_done"], g + 1)
                    pe.wait_ge(s["y_out"], g + 1)
                    if first:
                        pe.wait_ge(slot_full[3 * half + 2], 16 * pair + full0[2])
                    for c in range(2):
                        if c == 1:
                            pe.wait_ge(s["eb_done"], g + 1)
                        for hf in range(2):
                            for h in range(2):
                                ins = pe.matmul(S[64 * h:64 * h + 64, 3, :], uT[:, c, 64 * hf:64 * hf + 64],
                                                part[2][:, 2 * hf + c, h * 512:h * 512 + 512],
                                                start=(c == 0 and hf == 0), stop=(c == 1 and hf == 1))
                    ins.then_inc(s["down_done"], 1)
                    pe.reg_add(n_items, n_items, 1)

                flip_tokens(0, "first_gathered0", 16 * ((NE // 2 + 1) * l + 1), "first_flipped")
                pe.wait_ge(s["slots_ready"], l + 1)
                with pe.Fori(0, NE // 2) as pair:
                    for half in range(2):
                        n = pe.value_load(ntile[0:1, l, ds(2 * pair + half, 1)], min_val=1, max_val=MAXT)
                        pe.reg_mov(have, 2 * pair + (firsts + half + 1))
                        item(half, pair, True)
                        pe.reg_mov(tiles, n)
                        with pe.If_ne(tiles, 1), pe.Fori(1, n):
                            pe.reg_add(n_more, n_more, 1)
                            pe.reg_mov(have, 16 * pe.snap(n_more, min_val=0, max_val=64))
                            pe.reg_mov(emptied, 2 * pair + (firsts + half + 2))
                            pe.wait_ge(s["slots_ready"], l + 1)
                            pe.wait_ge(s["first_ready"], emptied)
                            flip_tokens(2, "more_gathered", have, "more_flipped")
                            item(half, pair, False)
                        pe.drain().then_inc(s["expert_done"], 1)
                g = pe.snap(n_items, min_val=1, max_val=64)
                pe.reg_mov(last_y, g + 1)
                pe.wait_ge(s["slots_ready"], l + 1)
                pe.wait_ge(s["first_ready"], firsts + NE + 1)
                pe.wait_ge(s["y_out"], last_y)


_INS = ["x", "c", "ctx", "c_ctx", "w_ada", "b_ada", "norm_attn", "norm_ffn", "w_in", "w_out", "lambda_qk",
        "subln", "sink", "w_router", "b_router", "w1", "w3", "w2", "norm_final"]


def kernel(**inputs):
    import concourse.bacc as bacc
    from concourse.bass_utils import run_bass_kernel_spmd

    nc = bacc.Bacc("TRN2", target_bir_lowering=False, num_devices=1)
    arrays = {f"in_{n}": np.ascontiguousarray(inputs[n]) for n in _INS}
    arrays["in_consts"] = constants()
    aps = {n[3:]: nc.dram_tensor(n, v.shape, mybir.dt.from_np(v.dtype), kind="ExternalInput").ap()
           for n, v in arrays.items()}
    aps["out"] = nc.dram_tensor("out", (1, SEQ, DM), mybir.dt.float32, kind="ExternalOutput").ap()
    build(nc, aps)
    r = run_bass_kernel_spmd(nc, [arrays], core_ids=[0])
    return r.results[0]["out"]
```

```python
import math
from contextlib import ExitStack

import numpy as np
import concourse.bass as bass
from concourse import mybir

P = 128
DM, SEQ, CTX, DEPTH = 1024, 256, 256, 2
GRID_W = 64
HA, HB, KVB, DH = 4, 8, 2, 64
NE, NG, EPG, TOPK, DE = 16, 4, 4, 2, 512
EPS, NEG = 1e-6, -1e30
ROPE_BASE = 10000.0
KC = DM // P
TT = (SEQ + CTX) // P
LT = SEQ // P
TOK = SEQ + CTX
D_IN = 2304
N_ADA = 6 * DM // 512
TILE = 64
MAXW = TOK // P
SLOTCOLS = 4096
SCALE = DH ** -0.5

C_ID, C_TRI, C_MB, C_ROPE = 0, 128, 256, 512
C_DEC, C_DECG, C_THR = 768, 784, 788
C_BEF = C_THR + MAXW
C_ALL = C_BEF + NE * NE


def constants():
    c = np.zeros((P, C_ALL), np.float32)
    r = np.arange(P)
    c[:, C_ID:C_ID + P] = np.eye(P)
    c[:, C_TRI:C_TRI + P] = r[:, None] < r[None, :]
    c[:, C_MB:C_MB + P] = np.where(r[None, :] <= r[:, None], 0.0, NEG)
    c[:, C_MB + P:C_MB + 2 * P] = np.where(r[None, :] >= r[:, None], 0.0, NEG)
    n_freq = DH // 4
    inv = (1.0 / (ROPE_BASE ** (np.arange(n_freq, dtype=np.float32) / np.float32(n_freq)))).astype(np.float32)
    pos = np.arange(SEQ)
    ang = np.stack([pos // GRID_W, pos % GRID_W], -1).astype(np.float32)[:, :, None] * inv
    cos, sin = np.cos(ang), np.sin(ang)
    full_cos = np.stack([cos, cos], 2).reshape(LT, P, DH)
    full_sin = np.stack([-sin, sin], 2).reshape(LT, P, DH)
    for t in range(LT):
        c[:, C_ROPE + 128 * t:C_ROPE + 128 * t + 64] = full_cos[t]
        c[:, C_ROPE + 128 * t + 64:C_ROPE + 128 * t + 128] = full_sin[t]
    c[:, C_DEC:C_DEC + NE] = EPG - np.arange(NE) % EPG
    c[:, C_DECG:C_DECG + NG] = NG - np.arange(NG)
    c[:, C_THR] = TILE
    c[:, C_THR + 1:C_BEF] = P * np.arange(1, MAXW)
    c[:, C_BEF:C_ALL] = (np.arange(NE)[None, :] < np.arange(NE)[:, None]).reshape(-1)
    return c


class Chain:

    def __init__(self, eng, sem):
        self.eng, self.sem, self.n = eng, sem, 0

    def step(self, ins):
        ins.then_inc(self.sem, 1)
        self.n += 1
        self.eng.wait_ge(self.sem, self.n)


def build(nc, a):
    f32, bf16, i32 = mybir.dt.float32, mybir.dt.bfloat16, mybir.dt.int32
    ALU, ACT, AX = mybir.AluOpType, mybir.ActivationFunctionType, mybir.AxisListType
    ds = bass.ds

    mod_d = nc.dram_tensor("mod_d", [DEPTH, 2, 6 * DM], f32).ap()
    n_rows = [TOPK * TOK, TOPK * SEQ]
    x_d = [nc.dram_tensor(f"x_d{l}", [n_rows[l] + TOK, DM], f32).ap() for l in range(DEPTH)]
    y_d = [nc.dram_tensor(f"y_d{l}", [n_rows[l] + TOK, DM], f32).ap() for l in range(DEPTH)]

    qtiles = [list(range(TT)), list(range(LT))]
    UNITS = ["ka", "va", "kvb", "qa", "qb"]
    UCOL = {"qa": (0, 512), "ka": (512, 512), "va": (1024, 512), "qb": (1536, 512), "kvb": (2048, 256)}
    PROJ = [(l, u, t) for l in range(DEPTH) for u in UNITS
            for t in (range(TT) if u in ("ka", "va", "kvb") else qtiles[l])]
    by_dve = lambda u, t: t < LT and u != "va"
    POST = {True: [s for s in PROJ if by_dve(s[1], s[2])], False: [s for s in PROJ if not by_dve(s[1], s[2])]}
    TR = [s for s in PROJ if s[1] != "va"]
    ATT = [(l, qt, kind, j) for l in range(DEPTH) for qt in qtiles[l] for kind in ("diff", "gqa") for j in (0, 1)]
    WOUT = [(l, t, n) for l in range(DEPTH) for t in qtiles[l] for n in (0, 1)]
    ADA = [(l, n) for l in range(DEPTH) for n in range(N_ADA)]
    first_ada = 4
    heads_in = {"diff": 2, "gqa": 4}

    early = N_ADA + first_ada + 2
    rest = [list(range(first_ada, early)), list(range(early, len(ADA)))]
    ada_at = {n: [] for n in range(len(ATT))}
    for l in range(DEPTH):
        units = [n for n, u in enumerate(ATT) if u[0] == l][:-1]
        for i, x in enumerate(rest[l]):
            ada_at[units[i * len(units) // len(rest[l])]].append(x)

    TU = ["c"]
    for l in range(DEPTH):
        TU += [("mod", l, h) for h in range(1 + l)] + [("hT", l, k) for k in range(KC)]
        TU += [("tr",) + s for s in TR if s[0] == l]
        units = [n for n, u in enumerate(ATT) if u[0] == l]
        for i, n in enumerate(units):
            TU += [("att", n, c) for c in range(heads_in[ATT[n][2]])]
            if i % 4 == 0 and i:
                TU += [("mix", l, ATT[n][1] - 1, h) for h in (0, 1)]
        TU += [("mix", l, qtiles[l][-1], h) for h in (0, 1)]
        TU += [("rt", l, t, h) for t in qtiles[l] for h in (0, 1)]
    tix = {key: i for i, key in enumerate(TU)}

    RS, col = {}, 0
    rs_order = []
    for l in range(DEPTH):
        evs = ([("attn", l, TT, DM)] if l == 0 else [("attn", l, t, 1, DM) for t in range(TT)]) + [("sub", l, qt, HA, 128) for qt in qtiles[l]] + \
              [("ffn", l, t, 1, DM) for t in qtiles[l]]
        if l == DEPTH - 1:
            evs += [("fin", LT, DM)]
        for e in evs:
            RS[e[:-2]] = (col, e[-2], e[-1], len(rs_order))
            rs_order.append(e[:-2])
            col += e[-2]
    n_rs = col

    with ExitStack() as ctx:
        def sb(name, shape, dt=f32):
            return ctx.enter_context(nc.sbuf_tensor(name, shape, dt))

        def sem(name):
            return ctx.enter_context(nc.semaphore(name))

        ring = sb("ring", [P, 6, SLOTCOLS])
        X = sb("X", [P, TT, DM])
        hT = sb("hT", [P, KC, TOK])
        R2 = sb("R2", [P, 9728])
        R3 = sb("R3", [P, 5120])
        modrow = sb("modrow", [P, DEPTH * N_ADA, 128])
        cst = sb("cst", [P, C_ALL])
        wr = sb("wr", [P, KC, NE])
        tmp = sb("tmp", [P, 512])
        subb = sb("subb", [P, DEPTH, 128])
        mc = sb("mc", [P, 4 * KC])
        ng = sb("ng", [P, DEPTH * KC])
        Ac = sb("Ac", [P, 2, KC])
        cs = sb("cs", [P, KC, 2])
        craw = sb("craw", [P, 16])
        cth = sb("cth", [P, 16])
        ssq = sb("ssq", [P, n_rs])
        rstd = sb("rstd", [P, n_rs])
        sinkb = sb("sinkb", [P, DEPTH, HB])
        nsink = sb("nsink", [P, DEPTH, HB])
        broutb = sb("broutb", [P, NE])
        mhalf = sb("mhalf", [P, 4])
        zero_row = sb("zero_row", [P, 64])
        nlam = sb("nlam", [P, DEPTH])
        lsum = sb("lsum", [P, 2 * DEPTH])
        lexp = sb("lexp", [P, 2 * DEPTH])
        rm = sb("rm", [P, 4])
        negm = sb("negm", [P, 4])
        sdif = sb("sdif", [P, 4])
        sexp = sb("sexp", [P, 2, 4])
        sums = sb("sums", [P, 2, 4])
        rec = sb("rec", [P, 2, 4])
        gate = sb("gate", [P, 2, TT])
        row_ix = sb("row_ix", [P, DEPTH, 2, TT], i32)
        ntile = sb("ntile", [P, DEPTH, NE], i32)
        nwide = sb("nwide", [P, DEPTH, NE + 1], i32)
        first_row = sb("first_row", [P, DEPTH, NE + 1], i32)

        kaT = R2[:, 0:2048].rearrange("p (c t) -> p c t", c=4)
        qaT = R2[:, 2048:4096].rearrange("p (c t) -> p c t", c=4)
        qbT = R2[:, 4096:6144].rearrange("p (c t) -> p c t", c=4)
        kbT = R2[:, 6144:7168].rearrange("p (c t) -> p c t", c=2)
        Va = R2[:, 7168:9216].rearrange("p (t n) -> p t n", t=TT)
        Vb = R2[:, 9216:9728].rearrange("p (t n) -> p t n", t=TT)
        xn = R2[:, 2048:6144].rearrange("p (t n) -> p t n", t=TT)
        gA = R2[:, 0:2048].rearrange("p (s n) -> p s n", s=2)
        gF = R2[:, 2048:4096].rearrange("p (s n) -> p s n", s=2)
        Af = R2[:, 4096:6144].rearrange("p (s n) -> p s n", s=2)
        Bf = R2[:, 6144:8192].rearrange("p (s n) -> p s n", s=2)
        nfb = R2[:, 8192:9216]
        yk = [r.rearrange("p (k n) -> p k n", k=2)
              for r in (R2[:, 4096:6144], R2[:, 6144:8192], R3[:, 2048:4096], R2[:, 0:2048])]
        rope_t1, rope_t2 = R3[:, 0:512], R3[:, 512:1024]
        stage = R3[:, 1024:2048].rearrange("p (b n) -> p b n", b=2)
        Pm = R3[:, 0:2048].rearrange("p (b n) -> p b n", b=4)
        PT = R3[:, 2048:4096].rearrange("p (b k q) -> p b k q", b=4, k=4)
        mix = R3[:, 4096:5120]
        hTs = R3[:, 0:1024].rearrange("p (k t) -> p k t", k=KC)
        junk = R3[:, 1024:2048]
        hb = [R3[:, 2048:3072], R3[:, 3072:4096], R3[:, 4096:5120], nfb]
        lamb = R3[:, 0:512].rearrange("p (l i d) -> p l i d", l=DEPTH, i=4)
        lprod = R3[:, 512:768].rearrange("p (l i d) -> p l i d", l=DEPTH, i=2)
        crow = R3[0:32, 768:896]
        xg = R2[:, 0:1536].rearrange("p (b n) -> p b n", b=3)
        y_s = R2[:, 4096:6144].rearrange("p (b n) -> p b n", b=2)
        xT = R3[:, 0:2048].rearrange("p (b j h t) -> p b j h t", b=2, j=4, h=2)
        th, t2, u_s = R3[:, 2048:2560], R3[:, 2560:3072], R3[:, 3072:3584]
        uT = R3[:, 3584:4096].rearrange("p (c t) -> p c t", c=4)
        tri_b = R2[:, 9216:9280].bitcast(bf16)
        one_b = R2[:, 9280:9344].bitcast(bf16)
        mask_b = R2[:, 9344:9376].bitcast(bf16)
        ident = cst[:, C_ID:C_ID + P]

        S = ctx.enter_context(nc.psum_tensor("S", [P, 4, 512], f32))
        T = [ctx.enter_context(nc.psum_tensor(f"T{i}", [P, 512], f32)) for i in range(2)]
        O = ctx.enter_context(nc.psum_tensor("O", [P, 512], f32))
        AUX = ctx.enter_context(nc.psum_tensor("AUX", [P, 512], f32))

        mc_view = mc[:, :].rearrange("p (i x q) -> p x q i", i=2, x=first_ada)

        def mod_view(bank, l):
            n = first_ada // (1 + l)
            return bank[:, 0:128 * n].rearrange("p (x q r) -> p x q r", x=n, q=4)[:, :, :, 0:2]

        def mc_part(l, h):
            n = first_ada // (1 + l)
            return mc_view[:, n * h:n * h + n]

        ut_bank = [S[:, 2, :], AUX]

        slot_full = [sem(f"slot_full{i}") for i in range(6)]
        names = """consts_in x_in small_in router_in bias_in clear_done bank_clear zeros_made tail_zeroed c_ready
            ada_done ada_out mod_stored1 mod_stored2 coeff_ready proj_done post_dve post_act t_full t_free_act
            t_free_dve act_ssq dve_ssq rstd_ready xn_ready scores_done negm_ready exps_done norm_done
            pv_done rows_ready o_out mix_ready wout_done wout_out ga_in ab_in gf_in nfin_in ab_ready h_ready
            logits_done sig_done mask_ready ranks_done counts_ready rows_scattered
            first_fetched0 first_fetched1 more_fetched first_flipped more_flipped
            first_ready more_ready up1_done up3_done tanh_done t2_done ua_done ub_done
            uta_done utb_done ea_done eb_done down_done y_out y_stored y_gathered0 y_gathered1 y_gathered2 y_gathered3 y_scaled comb_done
            dve_self pool_self lam_dot lam_exp fin_ready out_stored""".split()
        s = {n: sem(n) for n in names}
        t_free = [s["t_free_act"], s["t_free_dve"]]

        loads, where, last, count = [], {}, {}, [0] * 6

        def load(key, slot, src):
            count[slot] += 16
            loads.append((key, slot, src, last.get(slot)))
            where[key] = (slot, count[slot])

        def cols(w, c0, n):
            return w[:, c0:c0 + n].rearrange("(k p) n -> p k n", p=P)

        def load_ada(x, slot):
            l, n = ADA[x]
            load(("ada", x), slot, cols(a["w_ada"][l], 512 * n, 512))
            last[slot] = (s["ada_done"], x + 1)

        def load_in(l, u, slot):
            load(("in", l, u), slot, cols(a["w_in"][l], *UCOL[u]))
            t_last = max(i for i, st in enumerate(PROJ) if st[:2] == (l, u))
            last[slot] = (s["proj_done"], t_last + 1)

        def load_out(l, n, slot):
            load(("out", l, n), slot, cols(a["w_out"][l], 512 * n, 512))
            last[slot] = (s["wout_done"], 1 + max(i for i, st in enumerate(WOUT) if st[0] == l))

        def expert_src(l, e, part):
            w = a[("w1", "w3", "w2")[part]]
            if isinstance(e, int):
                one = w[l, e]
            else:
                one = w[l, ds(e, 1)].rearrange("a k n -> (a k) n")
            return one.rearrange("(k p) n -> p k n", p=P)

        def load_expert(l, e, part):
            load(("e", l, e, part), 3 * (e % 2) + part, expert_src(l, e, part))

        for x in range(first_ada):
            load_ada(x, x)
        for u, slot in zip(UNITS, (4, 5, 0, 1, 2)):
            load_in(0, u, slot)
        for i, x in enumerate(rest[0]):
            load_ada(x, 3 + i % 3)
            if i == 2:
                for part in range(3):
                    load_expert(0, 0, part)
        for n in (0, 1):
            load_out(0, n, 3 + (len(rest[0]) + n) % 3)
        loads.append("rows0")
        for part in range(3):
            load_expert(0, 1, part)
        loads.append("experts0")
        for i in range(6):
            count[i] += 16 * (NE // 2 - 1)
            last[i] = None
        for u, slot in zip(UNITS, (0, 1, 2, 3, 4)):
            load_in(1, u, slot)
        load_out(1, 0, 5)
        for i, x in enumerate(rest[1]):
            load_ada(x, i % 4)
        for part in range(3):
            load_expert(1, 0, part)
        load_out(1, 1, 4)
        load_expert(1, 1, 0)
        loads.append("rows1")
        for part in (1, 2):
            load_expert(1, 1, part)
        loads.append("experts1")

        def slot_view(slot, k):
            return ring[:, slot, :].rearrange("p (k n) -> p k n", k=k)

        block = ctx.enter_context(nc.Block())

        @block.sync
        def _(sp):
            def rows(l):
                streams = (0, 1) if l == 0 else (0,)
                sp.wait_ge(s["mod_stored1" if l == 0 else "mod_stored2"], 16 * 4)
                n_att = 1 + max(n for n, u in enumerate(ATT) if u[0] == l)
                sp.wait_ge(s["pv_done"], n_att)
                for i in streams:
                    sp.dma_start(gA[:, i, :], mod_d[l, i, 2 * DM:3 * DM].partition_broadcast(P)).then_inc(s["ga_in"], 16)
                for i in streams:
                    sp.dma_start(Af[:, i, :], mod_d[l, i, 4 * DM:5 * DM].partition_broadcast(P)).then_inc(s["ab_in"], 16)
                    sp.dma_start(Bf[:, i, :], mod_d[l, i, 3 * DM:4 * DM].partition_broadcast(P)).then_inc(s["ab_in"], 16)
                sp.dma_start(nfb, a["norm_ffn"][l].partition_broadcast(P)).then_inc(s["ab_in"], 16)
                for i in streams:
                    sp.dma_start(gF[:, i, :], mod_d[l, i, 5 * DM:6 * DM].partition_broadcast(P)).then_inc(s["gf_in"], 16)

            n_items = sp.alloc_register("sp_items")
            sp.reg_mov(n_items, 0)
            flying = []
            for item in loads:
                if item in ("rows0", "rows1"):
                    rows(int(item[-1]))
                elif item in ("experts0", "experts1"):
                    l = int(item[-1])
                    flying = []
                    sp.wait_ge(s["counts_ready"], l + 1)
                    with sp.Fori(1, NE // 2) as pair:
                        for half in range(2):
                            n = sp.value_load(ntile[0:1, l, ds(2 * pair + (half - 2), 1)], min_val=1, max_val=MAXW)
                            sp.reg_add(n_items, n_items, n)
                            for part, used in enumerate(("up1_done", "up3_done", "down_done")):
                                slot = 3 * half + part
                                sp.wait_ge(s["counts_ready"], l + 1)
                                sp.wait_ge(s[used], n_items)
                                early = (slot - 2) % 6
                                full = where[("e", l, early // 3, early % 3)][1] - (16 if slot < 2 else 0)
                                sp.wait_ge(slot_full[early], 16 * pair + full)
                                dst = slot_view(slot, 4 if part == 2 else 8)
                                sp.dma_start(dst, expert_src(l, 2 * pair + half, part)).then_inc(slot_full[slot], 16)
                    for half in range(2):
                        n = sp.value_load(ntile[0:1, l, NE - 2 + half:NE - 1 + half], min_val=1, max_val=MAXW)
                        sp.reg_add(n_items, n_items, n)
                    if l == 0:
                        sp.wait_ge(s["counts_ready"], l + 1)
                        sp.wait_ge(s["down_done"], n_items)
                        for b in range(TT):
                            sp.wait_ge(s[f"y_gathered{b}"], 32)
                else:
                    key, slot, src, free = item
                    if len(flying) >= 2:
                        sp.wait_ge(*flying[-2])
                    flying.append((slot_full[slot], where[key][1]))
                    if free is not None:
                        sp.wait_ge(*free)
                    k, n = src.shape[1], src.shape[2]
                    dst = ring[:, slot, 0:k * n].rearrange("p (k n) -> p k n", k=k)
                    sp.dma_start(dst, src).then_inc(slot_full[slot], 16)
            sp.wait_ge(s["ab_ready"], 2)
            sp.dma_start(nfb, a["norm_final"].partition_broadcast(P)).then_inc(s["nfin_in"], 16)
            for t in range(LT):
                sp.wait_ge(s["fin_ready"], t + 1)
                sp.dma_start(a["out"][0, t * P:(t + 1) * P, :], X[:, t, :]).then_inc(s["out_stored"], 16)
            sp.wait_ge(s["out_stored"], 16 * LT)

        @block.gpsimd
        def _(pool):
            self_ = Chain(pool, s["pool_self"])
            pool.memset(mhalf[:, :], -0.5)
            pool.memset(zero_row[:, :], 0.0).then_inc(s["zeros_made"], 1)
            pool.wait_ge(s["zeros_made"], 1)
            pool.wait_ge(s["clear_done"], 1)
            src = a["b_ada"].rearrange("l (n q c) -> q (l n) c", q=4, c=128)
            for q in range(4):
                pool.dma_start(modrow[32 * q:32 * q + 2, :, :], src[q].partition_broadcast(2)).then_inc(s["bias_in"], 16)
            def rsqrt(key):
                c0, w, n, i = RS[key]
                self_.step(pool.tensor_scalar(rstd[:, c0:c0 + w], ssq[:, c0:c0 + w], 1.0 / n, EPS, ALU.mult, ALU.add))
                pool.tensor_tensor(rstd[:, c0:c0 + w], rstd[:, c0:c0 + w], mhalf[:, 0:w], ALU.pow).then_inc(s["rstd_ready"], 1)

            def store_mod(l, n0, n1, stored):
                pool.wait_ge(s["ada_out"], l * N_ADA + n1)
                for q in range(4):
                    dst = mod_d[l].rearrange("i (n q c) -> q i n c", q=4, c=128)[q, :, n0:n1, :]
                    pool.dma_start(dst, modrow[32 * q:32 * q + 2, l * N_ADA + n0:l * N_ADA + n1, :]).then_inc(s[stored], 16)

            n_items = pool.alloc_register("pool_items")
            pool.reg_mov(n_items, 0)
            have, stored, n_more = (pool.alloc_register(f"pool_{n}") for n in ("have", "stored", "more"))
            pool.reg_mov(n_more, 0)
            tiles = pool.alloc_register("pool_tiles")
            wide = pool.alloc_register("pool_wide")
            n_ssq = 0
            for l in range(DEPTH):
                if l:
                    for t in range(TT):
                        n_ssq += 1
                        pool.wait_ge(s["act_ssq"], n_ssq)
                        rsqrt(("attn", l, t))
                else:
                    n_ssq += TT
                    pool.wait_ge(s["act_ssq"], n_ssq)
                    rsqrt(("attn", l))
                    for m in range(DEPTH):
                        pool.dma_start(x_d[m][n_rows[m]:n_rows[m] + P, :].rearrange("p (a c) -> p a c", c=64),
                                       zero_row[:, :].rearrange("p (a c) -> p a c", a=1).to_broadcast([P, DM // 64, 64])
                                       ).then_inc(s["tail_zeroed"], 16)
                for i, qt in enumerate(qtiles[l]):
                    pool.wait_ge(s["dve_ssq"], 1 + i + (0 if l == 0 else len(qtiles[0])))
                    rsqrt(("sub", l, qt))
                if l == 0:
                    store_mod(0, first_ada, N_ADA, "mod_stored1")
                else:
                    store_mod(1, first_ada, N_ADA, "mod_stored2")
                for t in qtiles[l]:
                    n_ssq += 1
                    pool.wait_ge(s["act_ssq"], n_ssq)
                    rsqrt(("ffn", l, t))
                pool.wait_ge(s["rows_ready"], l + 1)
                for t in qtiles[l]:
                    for k in range(2):
                        pool.indirect_dma_start(
                            out=x_d[l], out_offset=bass.IndirectOffsetOnAxis(ap=row_ix[:, l, k, t:t + 1], axis=0),
                            in_=hb[t], in_offset=None).then_inc(s["rows_scattered"], 16)
                pool.wait_ge(s["tail_zeroed"], 16 * DEPTH)
                pool.wait_ge(s["counts_ready"], l + 1)
                pool.wait_ge(s["rows_scattered"], 32 * (len(qtiles[0]) + (len(qtiles[1]) if l else 0)))

                def fetch(row, buf, free, count):
                    pool.wait_ge(s["counts_ready"], l + 1)
                    pool.wait_ge(s[free], count)
                    pool.dma_start(xg[:, buf, :], x_d[l][ds(row, TILE), :].rearrange("t (h d) -> (t h) d", h=2)
                                   ).then_inc(s[("first_fetched0", "first_fetched1", "more_fetched")[buf]], 16)

                def fetch_more(row):
                    fetch(row, 2, "more_flipped", n_more)
                    pool.reg_add(n_more, n_more, 1)

                def row_of(e):
                    return pool.value_load(first_row[0:1, l, e], min_val=0, max_val=n_rows[l])

                def load_wide(e):
                    pool.reg_mov(wide, pool.value_load(nwide[0:1, l, e], min_val=0, max_val=MAXW))

                firsts = (NE + 1) * l
                pool.reg_mov(have, firsts)
                fetch(0, 0, "first_flipped", have)
                load_wide(slice(0, 1))
                with pool.If_ne(wide, 0):
                    fetch_more(TILE)
                with pool.Fori(0, NE // 2) as pair:
                    for half in range(2):
                        pool.reg_mov(have, 2 * pair + (half + firsts))
                        row = row_of(ds(2 * pair + (half + 1), 1))
                        fetch(row, 1 - half, "first_flipped", have)
                        load_wide(ds(2 * pair + (half + 1), 1))
                        with pool.If_ne(wide, 0):
                            fetch_more(row + TILE)
                        n = pool.value_load(ntile[0:1, l, ds(2 * pair + half, 1)], min_val=1, max_val=MAXW)
                        own_row = row_of(ds(2 * pair + half, 1))
                        pool.reg_add(n_items, n_items, n)
                        pool.reg_mov(tiles, n)
                        with pool.If_ne(tiles, 1), pool.Fori(1, n) as t:
                            for b in range(2):
                                fetch_more(own_row + P * t + TILE * b)
                g = pool.snap(n_items, min_val=1, max_val=64)
                pool.reg_mov(stored, 32 * g)
                pool.wait_ge(s["counts_ready"], l + 1)
                pool.wait_ge(s["y_stored"], stored)
                for t in qtiles[l]:
                    for k in range(2):
                        pool.indirect_dma_start(
                            out=yk[t][:, k, :], out_offset=None, in_=y_d[l][0:TOPK * P * len(qtiles[l]), :],
                            in_offset=bass.IndirectOffsetOnAxis(ap=row_ix[:, l, k, t:t + 1], axis=0)
                        ).then_inc(s[f"y_gathered{t}"], 16)
            n_ssq += LT
            pool.wait_ge(s["act_ssq"], n_ssq)
            rsqrt(("fin",))

        @block.scalar
        def _(act):
            act.dma_start(cst[:, :], a["consts"]).then_inc(s["consts_in"], 16)
            act.dma_start(crow[0:8, :], a["c"][0].rearrange("(r c) -> r c", c=128)).then_inc(s["consts_in"], 16)
            act.dma_start(crow[8:16, :], a["c_ctx"].rearrange("(r c) -> r c", c=128)).then_inc(s["consts_in"], 16)
            act.dma_start(crow[16:32, :], a["norm_attn"].rearrange("l (r c) -> (l r) c", c=128)).then_inc(s["consts_in"], 16)
            for t in range(TT):
                src = a["x"] if t < LT else a["ctx"]
                act.dma_start(X[:, t, :], src[0, (t % LT) * P:(t % LT + 1) * P, :]).then_inc(s["x_in"], 16)
            act.dma_start(lamb.rearrange("p l i d -> p (l i d)"),
                          a["lambda_qk"].rearrange("l i d -> (l i d)").partition_broadcast(P)).then_inc(s["small_in"], 16)
            act.dma_start(sinkb[:, :, :].rearrange("p l h -> p (l h)"),
                          a["sink"].rearrange("l h -> (l h)").partition_broadcast(P)).then_inc(s["small_in"], 16)
            act.dma_start(subb[:, :, :].rearrange("p l d -> p (l d)"),
                          a["subln"].rearrange("l d -> (l d)").partition_broadcast(P)).then_inc(s["small_in"], 16)
            act.dma_start(broutb[:, :], a["b_router"].partition_broadcast(P)).then_inc(s["small_in"], 16)
            act.dma_start(wr[:, :, :], a["w_router"].rearrange("(k p) n -> p k n", p=P)).then_inc(s["router_in"], 16)

            def full(key):
                act.wait_ge(s["t_full"], tix[key] + 1)
                return T[0]

            def mine(key):
                return tix[key] % 2 == 0

            def copy(out, in_):
                return act.activation(out, in_, ACT.Copy)

            full("c")
            copy(craw[:, :], T[0][:, 0:16])
            copy(ng[:, :], T[0][:, 16:32])
            act.activation(cth[:, :], T[0][:, 0:16], ACT.Tanh, scale=0.5).then_inc(s["t_free_act"], 1)

            squares = [0]

            def square_sum(t, key, c):
                c0 = RS[key][0]
                if squares[0]:
                    act.wait_ge(s["act_ssq"], squares[0])
                squares[0] += 1
                act.activation(junk, X[:, t, :], ACT.Square, accum_out=ssq[:, c0 + c:c0 + c + 1]).then_inc(s["act_ssq"], 1)

            n_items, n_more = act.alloc_register("act_items"), act.alloc_register("act_more")
            act.reg_mov(n_items, 0)
            act.reg_mov(n_more, 0)
            tiles = act.alloc_register("act_tiles")
            wide, narrow, next_first, before, down = (act.alloc_register(f"act_{n}")
                                                      for n in ("wide", "own_wide", "next_first", "before", "down"))
            for l in range(DEPTH):
                if l == 0:
                    act.wait_ge(s["x_in"], 16 * TT)
                for t in range(TT):
                    if l and t < TT:
                        act.wait_ge(s["comb_done"], t + 1)
                    square_sum(t, ("attn", l) if l == 0 else ("attn", l, t), t if l == 0 else 0)
                for h in range(1 + l):
                    if mine(("mod", l, h)):
                        full(("mod", l, h))
                        copy(mc_part(l, h), mod_view(T[0], l)).then_inc(s["t_free_act"], 1)
                act.wait_ge(s["coeff_ready"], l + 1)
                for k in range(KC):
                    if mine(("hT", l, k)):
                        full(("hT", l, k))
                        for i in range(2):
                            ins = act.activation(hT[:, k, i * 256:(i + 1) * 256], T[0][:, i * 256:(i + 1) * 256],
                                                 ACT.Identity, bias=mc[:, 16 * i + k:16 * i + k + 1],
                                                 scale=Ac[:, i, k:k + 1])
                        ins.then_inc(s["t_free_act"], 1)
                if l == 0:
                    act.wait_ge(s["lam_dot"], 1)
                    act.activation(lexp[:, :], lsum[:, :], ACT.Exp).then_inc(s["lam_exp"], 1)

                def post(i):
                    _, u, t = PROJ[i]
                    if by_dve(u, t):
                        return
                    act.wait_ge(s["proj_done"], i + 1)
                    if u == "va":
                        copy(Va[:, t, :], S[:, i % 4, :]).then_inc(s["post_act"], 1)
                        return
                    j = TR.index(PROJ[i])
                    if j >= 2:
                        act.wait_ge(s["t_full"], tix[("tr",) + TR[j - 2]] + 1)
                    if u == "kvb":
                        src = S[:, i % 4, 0:128].rearrange("p (v o d) -> p v o d", v=2, o=1).to_broadcast([P, 2, 2, 64])
                        copy(stage[:, j % 2, 0:256].rearrange("p (v o d) -> p v o d", v=2, o=2), src)
                        copy(Vb[:, t, :], S[:, i % 4, 128:256]).then_inc(s["post_act"], 1)
                    else:
                        copy(stage[:, j % 2, :], S[:, i % 4, :]).then_inc(s["post_act"], 1)

                def take(key, dst, src_cols, c):
                    full(key)
                    src = T[0][:, 0:src_cols].rearrange("p (c t) -> p c t", c=c)
                    copy(dst, src).then_inc(s["t_free_act"], 1)

                idx = [i for i, st in enumerate(PROJ) if st[0] == l]
                for i in idx + [None]:
                    if i is not None:
                        post(i)
                    prev = (i - 1) if i is not None else idx[-1]
                    if prev >= idx[0] and PROJ[prev][1] != "va" and mine(("tr",) + PROJ[prev]):
                        _, u, t = PROJ[prev]
                        dst = {"ka": kaT, "qa": qaT, "qb": qbT, "kvb": kbT}[u]
                        c = 2 if u == "kvb" else 4
                        take(("tr",) + PROJ[prev], dst[:, :, t * P:(t + 1) * P], c * P, c)

                units = [n for n, u in enumerate(ATT) if u[0] == l]
                for i, n in enumerate(units):
                    _, qt, kind, j = ATT[n]
                    k0 = 0 if qt < LT else SEQ
                    if not i:
                        act.wait_ge(s["t_full"], max(tix[("tr",) + st] for st in TR if st[0] == l) + 1)
                    for b in range(4):
                        if b % 2 == 0:
                            act.wait_ge(s["negm_ready"], 2 * n + b // 2 + 1)
                            if kind == "gqa":
                                act.activation(sexp[:, n % 2, b:b + 2], sdif[:, b:b + 2], ACT.Exp)
                        if i:
                            c = b // 2 if ATT[n - 1][2] == "diff" else b
                            act.wait_ge(s["t_full"], tix[("att", n - 1, c)] + 1)
                        ins = act.activation(Pm[:, b, 0:TOK - k0], S[:, b, 0:TOK - k0], ACT.Exp, bias=negm[:, b:b + 1],
                                             scale=SCALE, accum_out=sums[:, n % 2, b:b + 1])
                        if b % 2:
                            ins.then_inc(s["exps_done"], 1)
                    nk = (TOK - k0) // P
                    for c in range(heads_in[kind]):
                        if mine(("att", n, c)):
                            take(("att", n, c), PT[:, c, 0:nk, :], nk * P, nk)
                    done = [qt - 1] if i % 4 == 0 and i else []
                    if i == len(units) - 1:
                        done.append(qt)
                    for q in done:
                        for h in (0, 1):
                            if mine(("mix", l, q, h)):
                                take(("mix", l, q, h), hT[:, 4 * h:4 * h + 4, q * P:(q + 1) * P], 512, 4)

                base = 0 if l == 0 else len(qtiles[0])
                w0 = WOUT.index((l, 0, 0))
                for i, t in enumerate(qtiles[l]):
                    act.wait_ge(s["wout_out"], w0 + 2 * i + 2)
                    square_sum(t, ("ffn", l, t), 0)
                    for h in (0, 1):
                        if mine(("rt", l, t, h)):
                            take(("rt", l, t, h), hTs[:, 4 * h:4 * h + 4, :], 512, 4)
                nt = len(qtiles[l])
                act.wait_ge(s["logits_done"], base + nt)
                act.activation(junk[:, 0:nt * NE], AUX[:, 0:nt * NE], ACT.Tanh, scale=0.5).then_inc(s["sig_done"], 1)

                firsts = (NE + 1) * l

                def take_tokens(buf, part, bank, flipped, count, ready):
                    act.wait_ge(s["counts_ready"], l + 1)
                    act.wait_ge(s[flipped], count)
                    copy(xT[:, buf, :, :, 64 * part:64 * part + 64],
                         bank[:, :].rearrange("p (j t h) -> p j h t", j=4, h=2)).then_inc(s[ready], 1)

                def take_more(buf, part):
                    act.reg_add(n_more, n_more, 1)
                    take_tokens(buf, part, T[1], "more_flipped", n_more, "more_ready")

                def load_wide(e):
                    act.reg_mov(wide, act.value_load(nwide[0:1, l, e], min_val=0, max_val=MAXW))

                def item(half, row, is_wide, pair, first):
                    g = act.snap(n_items, min_val=0, max_val=64)
                    width = 512 if is_wide else 256
                    act.wait_ge(s["up1_done"], g + 1)
                    act.activation(th[:, 0:width], S[:, 0, 0:width], ACT.Tanh, scale=0.5).then_inc(s["tanh_done"], 1)
                    if first:
                        act.reg_mov(next_first, 2 * pair + (firsts + half + 2))
                        take_tokens(1 - half, 0, O, "first_flipped", next_first, "first_ready")
                        load_wide(ds(2 * pair + (half + 1), 1))
                        with act.If_ne(wide, 0):
                            take_more(1 - half, 1)
                    act.reg_mov(before, 32 * act.snap(n_items, min_val=0, max_val=64))
                    act.reg_mov(down, act.snap(n_items, min_val=0, max_val=64) + 1)
                    act.wait_ge(s["counts_ready"], l + 1)
                    act.wait_ge(s["down_done"], down)
                    if not first:
                        act.wait_ge(s["y_stored"], before)
                    if is_wide:
                        copy(y_s[:, half, 0:512], S[:, 3, :])
                        copy(y_s[:, half, 512:1024], T[0][:, :]).then_inc(s["y_out"], 1)
                    else:
                        copy(y_s[:, half, 0:512], S[:, 3, :]).then_inc(s["y_out"], 1)
                    g = act.snap(n_items, min_val=0, max_val=64)
                    act.wait_ge(s["y_stored"], 32 * g)
                    act.wait_ge(s["y_out"], g + 2)
                    for h in range(2):
                        dst = y_d[l][ds(row, P if is_wide else TILE), 512 * h:512 * h + 512]
                        src = y_s[:, half, 512 * h:512 * h + 512] if is_wide else y_s[64 * h:64 * h + 64, half, 0:512]
                        act.dma_start(dst, src).then_inc(s["y_stored"], 16)
                    act.reg_add(n_items, n_items, 1)

                take_tokens(0, 0, O, "first_flipped", firsts + 1, "first_ready")
                load_wide(slice(0, 1))
                with act.If_ne(wide, 0):
                    take_more(0, 1)
                if l == 0:
                    copy(sexp[:, 0, 0:1], sexp[:, 0, 0:1]).then_inc(s["y_out"], 1)
                with act.Fori(0, NE // 2) as pair:
                    for half in range(2):
                        n = act.value_load(ntile[0:1, l, ds(2 * pair + half, 1)], min_val=1, max_val=MAXW)
                        row0 = act.value_load(first_row[0:1, l, ds(2 * pair + half, 1)], min_val=0, max_val=TOPK * P * nt)
                        act.reg_mov(tiles, n)
                        load_wide(ds(2 * pair + half, 1))
                        act.reg_mov(narrow, act.snap(wide, min_val=0, max_val=MAXW))
                        with act.If_eq(narrow, 0):
                            item(half, row0, False, pair, True)
                        with act.If_ne(narrow, 0):
                            item(half, row0, True, pair, True)
                            with act.If_ne(tiles, 1), act.Fori(1, n) as t:
                                for b in range(2):
                                    take_more(half, b)
                                item(half, row0 + t * P, True, pair, False)
                act.wait_ge(s["counts_ready"], l + 1)
                for t in qtiles[l]:
                    act.wait_ge(s[f"y_gathered{t}"], 32 * (l + 1))
                    act.activation(yk[t][:, 0, :], yk[t][:, 0, :], ACT.Copy, scale=gate[:, 0, t:t + 1]).then_inc(s["y_scaled"], 1)
            base = len(qtiles[0])
            for t in range(LT):
                act.wait_ge(s["comb_done"], base + t + 1)
                square_sum(t, ("fin",), t)

        @block.vector
        def _(dve):
            ch = Chain(dve, s["dve_self"])

            def full(key):
                dve.wait_ge(s["t_full"], tix[key] + 1)
                return T[1]

            def mine(key):
                return tix[key] % 2 == 1

            def bc(ap, shape):
                return ap.to_broadcast(shape)

            dve.memset(nwide[:, :, :], 0)
            dve.memset(first_row[:, :, :], 0)
            dve.memset(modrow[:, :, :], 0.0).then_inc(s["clear_done"], 1)
            dve.memset(AUX[:, :], 0.0).then_inc(s["bank_clear"], 1)
            dve.wait_ge(s["consts_in"], 64)
            dve.wait_ge(s["t_free_act"], 1)
            ch.step(dve.scalar_tensor_tensor(cth[:, :], cth[:, :], 1.0, craw[:, :], ALU.add, ALU.mult))
            dve.tensor_scalar(cs[:, :, :], cth[:, :].rearrange("p (i k) -> p k i", i=2), 0.5, None, ALU.mult).then_inc(s["c_ready"], 1)

            def ada_out(x):
                dve.wait_ge(s["ada_done"], x + 1)
                dve.tensor_tensor(modrow[:, x, :], modrow[:, x, :], AUX[:, 0:128], ALU.add).then_inc(s["ada_out"], 1)

            dve.wait_ge(s["bias_in"], 16 * 4)
            for x in range(2):
                ada_out(x)

            n_items = dve.alloc_register("dve_items")
            dve.reg_mov(n_items, 0)
            wide = dve.alloc_register("dve_wide")
            for l in range(DEPTH):
                base = 0 if l == 0 else len(qtiles[0])
                nt = len(qtiles[l])
                def normed(t, c, ev):
                    dve.wait_ge(s["rstd_ready"], ev + 1)
                    dve.tensor_scalar(xn[:, t, :], X[:, t, :], rstd[:, c:c + 1], None, ALU.mult).then_inc(s["xn_ready"], 1)

                if l == 0:
                    c0, _, _, ev = RS[("attn", l)]
                    for t in range(TT):
                        normed(t, c0 + t, ev)
                if l == 0:
                    for x in range(2, first_ada):
                        ada_out(x)
                for h in range(1 + l):
                    if mine(("mod", l, h)):
                        full(("mod", l, h))
                        dve.tensor_copy(mc_part(l, h), mod_view(T[1], l)).then_inc(s["t_free_dve"], 1)
                for h in range(1 + l):
                    k = tix[("mod", l, h)]
                    dve.wait_ge(t_free[k % 2], k // 2 + 1)
                for i in range(2):
                    ins = dve.scalar_tensor_tensor(Ac[:, i, :], mc[:, 16 * i + 8:16 * i + 16], 1.0, ng[:, KC * l:KC * l + KC], ALU.add, ALU.mult)
                ins.then_inc(s["coeff_ready"], 1)
                dve.wait_ge(s["coeff_ready"], l + 1)
                for k in range(KC):
                    if mine(("hT", l, k)):
                        full(("hT", l, k))
                        for i in range(2):
                            ins = dve.tensor_scalar(hT[:, k, i * 256:(i + 1) * 256], T[1][:, i * 256:(i + 1) * 256],
                                                    Ac[:, i, k:k + 1], mc[:, 16 * i + k:16 * i + k + 1], ALU.mult, ALU.add)
                        ins.then_inc(s["t_free_dve"], 1)
                if l == 0:
                    dve.wait_ge(s["small_in"], 64)
                    ch.step(dve.tensor_tensor(lprod, lamb[:, :, 0::2, :], lamb[:, :, 1::2, :], ALU.mult))
                    dve.tensor_reduce(lsum[:, :].rearrange("p (l i) -> p l i", l=DEPTH), lprod, AX.X, ALU.add).then_inc(s["lam_dot"], 1)
                    dve.tensor_scalar(nsink[:, :, :], sinkb[:, :, :], -1.0, None, ALU.mult)
                    for m in range(DEPTH):
                        lam_init = 0.8 - 0.6 * math.exp(-0.3 * m)
                        dve.tensor_scalar(subb[:, m, :], subb[:, m, :], 1.0 - lam_init, None, ALU.mult)
                    dve.wait_ge(s["lam_exp"], 1)
                    for m in range(DEPTH):
                        lam_init = 0.8 - 0.6 * math.exp(-0.3 * m)
                        ch.step(dve.tensor_tensor(nlam[:, m:m + 1], lexp[:, 2 * m + 1:2 * m + 2], lexp[:, 2 * m:2 * m + 1], ALU.subtract))
                        ch.step(dve.tensor_scalar(nlam[:, m:m + 1], nlam[:, m:m + 1], -lam_init, None, ALU.add))

                def rope(src, heads, t, outs):
                    n = heads * 64
                    v = lambda ap: ap[:, 0:n].rearrange("p (h x b f) -> p h x b f", h=heads, x=2, b=2)
                    tab = cst[:, C_ROPE + 128 * t:C_ROPE + 128 * t + 128]
                    cosv = tab[:, 0:64].rearrange("p (o d) -> p o d", o=1)
                    sinv = tab[:, 64:128].rearrange("p (o x b f) -> p o x b f", o=1, x=2, b=2)
                    dve.tensor_tensor(rope_t1[:, 0:n].rearrange("p (h d) -> p h d", h=heads),
                                      src[:, 0:n].rearrange("p (h d) -> p h d", h=heads), bc(cosv, [P, heads, 64]), ALU.mult)
                    for b in range(2):
                        ins = dve.tensor_tensor(v(rope_t2)[:, :, :, b, :], v(src)[:, :, :, 1 - b, :],
                                                bc(sinv[:, :, :, b, :], [P, heads, 2, 16]), ALU.mult)
                    ch.step(ins)
                    for out in outs:
                        ins = dve.tensor_tensor(out, rope_t1[:, 0:n].rearrange("p (h d) -> p h d", h=heads),
                                                rope_t2[:, 0:n].rearrange("p (h d) -> p h d", h=heads), ALU.add)
                    return ins

                def post(i):
                    _, u, t = PROJ[i]
                    if not by_dve(u, t):
                        return
                    dve.wait_ge(s["proj_done"], i + 1)
                    j = TR.index(PROJ[i])
                    if j >= 2:
                        dve.wait_ge(s["t_full"], tix[("tr",) + TR[j - 2]] + 1)
                    src = S[:, i % 4, :]
                    if u == "kvb":
                        dve.tensor_copy(Vb[:, t, :], src[:, 128:256])
                        st = stage[:, j % 2, 0:256].rearrange("p (v o d) -> p v o d", v=2, o=2)
                        ch.step(rope(src, 2, t, [st[:, :, 0, :], st[:, :, 1, :]]))
                    else:
                        ch.step(rope(src, 8, t, [stage[:, j % 2, :].rearrange("p (h d) -> p h d", h=8)]))
                    dve.tensor_scalar(sdif[:, 0:1], nlam[:, 0:1], 1.0, None, ALU.mult).then_inc(s["post_dve"], 1)

                def take(key, dst, src_cols, c):
                    full(key)
                    dve.tensor_copy(dst, T[1][:, 0:src_cols].rearrange("p (c t) -> p c t", c=c)).then_inc(s["t_free_dve"], 1)

                idx = [i for i, st in enumerate(PROJ) if st[0] == l]
                for i in idx + [None]:
                    if i is not None:
                        post(i)
                    prev = (i - 1) if i is not None else idx[-1]
                    if prev >= idx[0] and PROJ[prev][1] != "va" and mine(("tr",) + PROJ[prev]):
                        _, u, t = PROJ[prev]
                        dst = {"ka": kaT, "qa": qaT, "qb": qbT, "kvb": kbT}[u]
                        c = 2 if u == "kvb" else 4
                        take(("tr",) + PROJ[prev], dst[:, :, t * P:(t + 1) * P], c * P, c)

                units = [n for n, u in enumerate(ATT) if u[0] == l]

                def row_max(n, pairs=(0, 1)):
                    _, qt, kind, j = ATT[n]
                    k0 = 0 if qt < LT else SEQ
                    for pair in pairs:
                        r = slice(2 * pair, 2 * pair + 2)
                        dve.wait_ge(s["scores_done"], 2 * n + pair + 1)
                        ch.step(dve.tensor_reduce(rm[:, r], S[:, r, 0:TOK - k0], AX.X, ALU.max))
                        if kind == "diff":
                            dve.tensor_scalar(negm[:, r], rm[:, r], -SCALE, None, ALU.mult).then_inc(s["negm_ready"], 1)
                        else:
                            heads = slice(4 * j + 2 * pair, 4 * j + 2 * pair + 2)
                            ch.step(dve.scalar_tensor_tensor(negm[:, r], rm[:, r], -SCALE, nsink[:, l, heads], ALU.mult, ALU.min))
                            dve.tensor_tensor(sdif[:, r], negm[:, r], sinkb[:, l, heads], ALU.add).then_inc(s["negm_ready"], 1)

                row_max(units[0])
                for i, n in enumerate(units):
                    _, qt, kind, j = ATT[n]
                    nkey = TOK if qt < LT else CTX
                    dve.wait_ge(s["exps_done"], 2 * n + 2)
                    sm, rc = sums[:, n % 2, :], rec[:, n % 2, :]
                    if kind == "gqa":
                        ch.step(dve.tensor_tensor(sm, sm, sexp[:, n % 2, :], ALU.add))
                    ch.step(dve.reciprocal(rc, sm))
                    if kind == "diff":
                        ch.step(dve.tensor_scalar(rec[:, n % 2, 1::2], rec[:, n % 2, 1::2], nlam[:, l:l + 1], None, ALU.mult))
                        for h in range(2):
                            ch.step(dve.tensor_scalar(Pm[:, 2 * h, 0:nkey], Pm[:, 2 * h, 0:nkey], rc[:, 2 * h:2 * h + 1], None, ALU.mult))
                            dve.scalar_tensor_tensor(Pm[:, 2 * h, 0:nkey], Pm[:, 2 * h + 1, 0:nkey], rc[:, 2 * h + 1:2 * h + 2],
                                                     Pm[:, 2 * h, 0:nkey], ALU.mult, ALU.add).then_inc(s["norm_done"], 1)
                    if i + 1 < len(units):
                        row_max(n + 1, (0,))
                    nk = nkey // P
                    own = [c for c in range(heads_in[kind]) if mine(("att", n, c))]
                    for c in own:
                        take(("att", n, c), PT[:, c, 0:nk, :], nk * P, nk)
                        if c == own[0] and i + 1 < len(units):
                            row_max(n + 1, (1,))
                    dve.wait_ge(s["pv_done"], n + 1)
                    if kind == "diff":
                        if j == 0 and i:
                            dve.wait_ge(s["t_full"], tix[("mix", l, qt - 1, 1)] + 1)
                        dve.tensor_copy(mix[:, 256 * j:256 * j + 256], O[:, 0:256]).then_inc(s["o_out"], 1)
                        if j == 1:
                            dve.wait_ge(s["o_out"], n + 1)
                            ch.step(dve.tensor_tensor(tmp[:, :], mix[:, 0:512], mix[:, 0:512], ALU.mult))
                            c0 = RS[("sub", l, qt)][0]
                            dve.tensor_reduce(ssq[:, c0:c0 + HA], tmp[:, :].rearrange("p (h d) -> p h d", h=HA), AX.X,
                                              ALU.add).then_inc(s["dve_ssq"], 1)
                    else:
                        dve.tensor_tensor(mix[:, 512 + 256 * j:768 + 256 * j].rearrange("p (h d) -> p h d", h=4),
                                          O[:, 0:256].rearrange("p (h d) -> p h d", h=4),
                                          bc(rc.rearrange("p (h o) -> p h o", o=1), [P, 4, 64]), ALU.mult).then_inc(s["o_out"], 1)
                        if j == 1:
                            c0, _, _, ev = RS[("sub", l, qt)]
                            dve.wait_ge(s["rstd_ready"], ev + 1)
                            mv = mix[:, 0:512].rearrange("p (h d) -> p h d", h=HA)
                            ch.step(dve.tensor_tensor(mv, mv, bc(rstd[:, c0:c0 + HA].rearrange("p (h o) -> p h o", o=1), [P, HA, 128]), ALU.mult))
                            dve.tensor_tensor(mv, mv, bc(subb[:, l, :].rearrange("p (o d) -> p o d", o=1), [P, HA, 128]),
                                              ALU.mult).then_inc(s["mix_ready"], 1)
                    for x in ada_at[n]:
                        ada_out(x)
                    done = [qt - 1] if i % 4 == 0 and i else []
                    if i == len(units) - 1:
                        done.append(qt)
                    for q in done:
                        for h in (0, 1):
                            if mine(("mix", l, q, h)):
                                take(("mix", l, q, h), hT[:, 4 * h:4 * h + 4, q * P:(q + 1) * P], 512, 4)

                streams = 2 if l == 0 else 1
                dve.wait_ge(s["ga_in"], 32 if l == 0 else 48)
                w0 = WOUT.index((l, 0, 0))

                def residual(t):
                    for n in range(2):
                        w = WOUT.index((l, t, n))
                        if w:
                            dve.wait_ge(s["wout_out"], w)
                        dve.wait_ge(s["wout_done"], w + 1)
                        ch.step(dve.tensor_tensor(tmp[:, :], S[:, w % 4, :], gA[:, t // LT, n * 512:(n + 1) * 512], ALU.mult))
                        xs = X[:, t, n * 512:(n + 1) * 512]
                        dve.tensor_tensor(xs, xs, tmp[:, :], ALU.add).then_inc(s["wout_out"], 1)

                def ffn_input(i, t):
                    c0, _, _, ev = RS[("ffn", l, t)]
                    dve.wait_ge(s["rstd_ready"], ev + 1)
                    for h in (0, 1):
                        r = slice(512 * h, 512 * h + 512)
                        ch.step(dve.scalar_tensor_tensor(hb[t][:, r], X[:, t, r], rstd[:, c0:c0 + 1], Af[:, t // LT, r], ALU.mult, ALU.mult))
                        dve.tensor_tensor(hb[t][:, r], hb[t][:, r], Bf[:, t // LT, r], ALU.add).then_inc(s["h_ready"], 1)

                def take_rt(t):
                    for h in (0, 1):
                        if mine(("rt", l, t, h)):
                            take(("rt", l, t, h), hTs[:, 4 * h:4 * h + 4, :], 512, 4)

                residual(0)
                dve.wait_ge(s["ab_in"], 80 if l == 0 else 80 + 48)
                for i in range(streams):
                    ins = dve.scalar_tensor_tensor(Af[:, i, :], Af[:, i, :], 1.0, nfb, ALU.add, ALU.mult)
                    if i < streams - 1:
                        ch.step(ins)
                ins.then_inc(s["ab_ready"], 1)
                dve.wait_ge(s["ab_ready"], l + 1)
                for i, t in enumerate(qtiles[l]):
                    ffn_input(i, t)
                    take_rt(t)
                    if i + 1 < nt:
                        residual(t + 1)

                W = nt * NE
                R = [junk[:, 64 * i:64 * i + W] for i in range(14)]
                g4 = lambda ap: ap.rearrange("p (a e) -> p a e", e=EPG)
                G = [junk[:, 896 + 16 * i:896 + 16 * i + nt * NG] for i in range(8)]
                ch.step(dve.tensor_copy(tri_b, cst[:, C_TRI:C_TRI + P]))
                ch.step(dve.memset(one_b, 1.0))
                dve.wait_ge(s["sig_done"], l + 1)
                sg, sbv, e1, k1, o1, s2 = R[1], R[2], R[3], R[4], R[5], R[6]
                A4 = [P, nt * NG, EPG]
                dec = bc(cst[:, C_DEC:C_DEC + EPG].rearrange("p (o e) -> p o e", o=1), A4)
                up = lambda ap: bc(ap.rearrange("p (a o) -> p a o", o=1), A4)
                ch.step(dve.tensor_scalar(sg, R[0], 0.5, 0.5, ALU.mult, ALU.add))
                ch.step(dve.tensor_tensor(sbv.rearrange("p (t e) -> p t e", e=NE), sg.rearrange("p (t e) -> p t e", e=NE),
                                          bc(broutb[:, :].rearrange("p (o e) -> p o e", o=1), [P, nt, NE]), ALU.add))

                def best(vals, top, onehot, dec_, up_, view, top_view):
                    ch.step(dve.tensor_reduce(top, view(vals), AX.X, ALU.max))
                    ch.step(dve.tensor_tensor(view(e1), view(vals), up_(top), ALU.is_equal))
                    ch.step(dve.tensor_tensor(view(e1), view(e1), dec_, ALU.mult))
                    ch.step(dve.tensor_reduce(top_view, view(e1), AX.X, ALU.max))
                    ch.step(dve.tensor_tensor(view(onehot), view(e1), up_(top_view), ALU.is_equal))

                best(sbv, G[0], o1, dec, up, g4, G[1])
                ch.step(dve.scalar_tensor_tensor(s2, o1, -3e38, sbv, ALU.mult, ALU.add))
                o2 = k1
                best(s2, G[2], o2, dec, up, g4, G[3])
                ch.step(dve.tensor_tensor(G[4], G[0], G[2], ALU.add))
                tg = lambda ap: ap.rearrange("p (t g) -> p t g", g=NG)
                G3 = [P, nt, NG]
                upg = lambda ap: bc(ap.rearrange("p (t o) -> p t o", o=1), G3)
                gm, gk = G[5][:, 0:nt], G[6][:, 0:nt]
                decg = bc(cst[:, C_DECG:C_DECG + NG].rearrange("p (o g) -> p o g", o=1), G3)
                ch.step(dve.tensor_reduce(gm, tg(G[4]), AX.X, ALU.max))
                ch.step(dve.tensor_tensor(tg(G[1]), tg(G[4]), upg(gm), ALU.is_equal))
                ch.step(dve.tensor_tensor(tg(G[1]), tg(G[1]), decg, ALU.mult))
                ch.step(dve.tensor_reduce(gk, tg(G[1]), AX.X, ALU.max))
                ch.step(dve.tensor_tensor(tg(G[1]), tg(G[1]), upg(gk), ALU.is_equal))
                ch.step(dve.tensor_tensor(g4(o1), g4(o1), up(G[1]), ALU.mult))
                ch.step(dve.tensor_tensor(g4(o2), g4(o2), up(G[1]), ALU.mult))
                dve.tensor_tensor(mask_b[:, 0:W], o1, o2, ALU.add).then_inc(s["mask_ready"], 1)
                te = lambda ap: ap.rearrange("p (t e) -> p t e", e=NE)
                dve.wait_ge(s["ranks_done"], l + 1)
                cnt = AUX[:, 256:256 + NE]
                rank = AUX[:, 128:128 + W].rearrange("p (t e) -> p t e", e=NE)

                def places(start, out):
                    ch.step(dve.tensor_tensor(te(R[9]), rank, bc(start.rearrange("p (o e) -> p o e", o=1), [P, nt, NE]), ALU.add))
                    for k, oh in enumerate((o1, o2)):
                        ch.step(dve.tensor_tensor(R[10 + k], R[9], oh, ALU.mult))
                    for k in range(2):
                        ch.step(dve.tensor_reduce(G[k][:, 0:nt], te(R[10 + k]), AX.X, ALU.add))
                    for k in range(2):
                        ins = dve.tensor_copy(out[:, l, k, 0:nt], G[k][:, 0:nt])
                    return ins

                before = tmp[:, 0:NE * NE].rearrange("p (e f) -> p e f", e=NE)
                ch.step(dve.tensor_tensor(before, bc(cnt.rearrange("p (o f) -> p o f", o=1), [P, NE, NE]),
                                          cst[:, C_BEF:C_ALL].rearrange("p (e f) -> p e f", e=NE), ALU.mult))
                ch.step(dve.tensor_reduce(R[13][:, 0:NE], before, AX.X, ALU.add))
                places(R[13][:, 0:NE], row_ix).then_inc(s["rows_ready"], 1)
                ch.step(dve.tensor_copy(first_row[:, l, 0:NE], R[13][:, 0:NE]))
                for k, oh in enumerate((o1, o2)):
                    ch.step(dve.tensor_tensor(R[7 + k], sg, oh, ALU.mult))
                    ch.step(dve.tensor_reduce(gate[:, k, 0:nt], te(R[7 + k]), AX.X, ALU.add))
                den = G[7][:, 0:nt]
                ch.step(dve.tensor_tensor(den, gate[:, 0, 0:nt], gate[:, 1, 0:nt], ALU.add))
                ch.step(dve.reciprocal(den, den))
                for k in range(2):
                    ch.step(dve.tensor_tensor(gate[:, k, 0:nt], gate[:, k, 0:nt], den, ALU.mult))
                big = tmp[:, 0:NE * MAXW].rearrange("p (e j) -> p e j", e=NE)
                ch.step(dve.tensor_tensor(big, bc(cnt.rearrange("p (e o) -> p e o", o=1), [P, NE, MAXW]),
                                          bc(cst[:, C_THR:C_BEF].rearrange("p (o j) -> p o j", o=1), [P, NE, MAXW]), ALU.is_gt))
                ch.step(dve.tensor_reduce(R[12][:, 0:NE], big, AX.X, ALU.add))
                ch.step(dve.tensor_copy(nwide[:, l, 0:NE], R[12][:, 0:NE]))
                dve.tensor_scalar(ntile[:, l, :], R[12][:, 0:NE], 1.0, None, ALU.max).then_inc(s["counts_ready"], 1)
                dve.wait_ge(s["counts_ready"], l + 1)

                def item(is_wide):
                    g = dve.snap(n_items, min_val=0, max_val=64)
                    part = 256 if is_wide else 128
                    dve.wait_ge(s["tanh_done"], g + 1)
                    dve.scalar_tensor_tensor(t2[:, 0:2 * part], th[:, 0:2 * part], 1.0, S[:, 0, 0:2 * part],
                                             ALU.add, ALU.mult).then_inc(s["t2_done"], 1)
                    dve.wait_ge(s["t2_done"], g + 1)
                    dve.wait_ge(s["up3_done"], g + 1)
                    for c, name in enumerate(("ua_done", "ub_done")):
                        r = slice(part * c, part * c + part)
                        dve.scalar_tensor_tensor(u_s[:, r], t2[:, r], 0.5, S[:, 1, r], ALU.mult, ALU.mult).then_inc(s[name], 1)
                    nc_ = part // 128
                    for c, (flipped, done) in enumerate((("uta_done", "ea_done"), ("utb_done", "eb_done"))):
                        dve.wait_ge(s[flipped], g + 1)
                        dve.tensor_copy(uT[:, nc_ * c:nc_ * c + nc_, :],
                                        ut_bank[c][:, 0:part].rearrange("p (c t) -> p c t", c=nc_)).then_inc(s[done], 1)
                    dve.reg_add(n_items, n_items, 1)

                with dve.Fori(0, NE) as e:
                    n = dve.value_load(ntile[0:1, l, ds(e, 1)], min_val=1, max_val=MAXW)
                    dve.reg_mov(wide, dve.value_load(nwide[0:1, l, ds(e, 1)], min_val=0, max_val=MAXW))
                    with dve.If_eq(wide, 0):
                        item(False)
                    with dve.If_ne(wide, 0), dve.Fori(0, n):
                        item(True)

                dve.wait_ge(s["gf_in"], 32 if l == 0 else 48)
                for t in qtiles[l]:
                    dve.wait_ge(s[f"y_gathered{t}"], 32 * (l + 1))
                    dve.wait_ge(s["y_scaled"], base + t + 1)
                    y0, y1 = yk[t][:, 0, :], yk[t][:, 1, :]
                    ch.step(dve.scalar_tensor_tensor(y0, y1, gate[:, 1, t:t + 1], y0, ALU.mult, ALU.add))
                    ch.step(dve.tensor_tensor(y0, y0, gF[:, t // LT, :], ALU.mult))
                    dve.tensor_tensor(X[:, t, :], X[:, t, :], y0, ALU.add).then_inc(s["comb_done"], 1)
                    if l == 0 and t >= LT:
                        for u in ([0] if t < TT - 1 else [1, 2, 3]):
                            dve.wait_ge(s["comb_done"], t if u == 0 else t + 1)
                            c0, _, _, ev = RS[("attn", 1, u)]
                            normed(u, c0, ev)
            c0, _, _, ev = RS[("fin",)]
            dve.wait_ge(s["rstd_ready"], ev + 1)
            dve.wait_ge(s["nfin_in"], 16)
            for t in range(LT):
                dve.scalar_tensor_tensor(X[:, t, :], X[:, t, :], rstd[:, c0 + t:c0 + t + 1], nfb, ALU.mult, ALU.mult).then_inc(s["fin_ready"], 1)

        @block.tensor
        def _(pe):
            def weights(key):
                slot, n = where[key]
                pe.wait_ge(slot_full[slot], n)
                return slot

            def bank(key):
                k = tix[key]
                if k >= 2:
                    pe.wait_ge(t_free[k % 2], k // 2)
                return T[k % 2]

            def taken(key):
                k = tix[key]
                pe.wait_ge(t_free[k % 2], k // 2 + 1)

            def transposes(key, srcs):
                b, at = bank(key), 0
                for src in srcs:
                    rows = src.shape[0]
                    ins = pe.transpose(b[0:src.shape[1], at:at + rows], src, cst[0:rows, C_ID:C_ID + rows])
                    at += rows
                ins.then_inc(s["t_full"], 1)

            pe.wait_ge(s["consts_in"], 64)
            transposes("c", [crow])
            pe.wait_ge(s["c_ready"], 1)
            pe.wait_ge(s["bank_clear"], 1)

            def ada(x):
                slot = weights(("ada", x))
                if x:
                    pe.wait_ge(s["ada_out"], x)
                w = slot_view(slot, KC)
                for k in range(KC):
                    for q in range(4):
                        ins = pe.matmul(AUX[32 * q:32 * q + 2, 0:128], cs[:, k, :], w[:, k, 128 * q:128 * q + 128],
                                        start=(k == 0), stop=(k == KC - 1))
                ins.then_inc(s["ada_done"], 1)

            for x in range(first_ada):
                ada(x)

            n_items = pe.alloc_register("pe_items")
            pe.reg_mov(n_items, 0)
            n_more, have, emptied, last_y = (pe.alloc_register(f"pe_{n}") for n in ("more", "have", "emptied", "last_y"))
            pe.reg_mov(n_more, 0)
            tiles = pe.alloc_register("pe_tiles")
            wide, own_wide, now = (pe.alloc_register(f"pe_{n}") for n in ("wide", "own_wide", "now"))
            for l in range(DEPTH):
                nt = len(qtiles[l])
                base = 0 if l == 0 else len(qtiles[0])
                pe.wait_ge(s["ada_out"], l * N_ADA + first_ada)
                step = first_ada // (1 + l)
                for h in range(1 + l):
                    transposes(("mod", l, h), [modrow[:, l * N_ADA + x, :] for x in range(h * step, (h + 1) * step)])
                pe.wait_ge(s["xn_ready"], TT * (l + 1))
                for k in range(KC):
                    transposes(("hT", l, k), [xn[:, t, k * P:(k + 1) * P] for t in range(TT)])
                taken(("hT", l, KC - 2))
                taken(("hT", l, KC - 1))

                def posted(i):
                    eng = by_dve(*PROJ[i][1:])
                    pe.wait_ge(s["post_dve" if eng else "post_act"], POST[eng].index(PROJ[i]) + 1)

                def tr(st):
                    posted(PROJ.index(st))
                    j = TR.index(st)
                    n = 2 if st[1] == "kvb" else 4
                    transposes(("tr",) + st, [stage[:, j % 2, c * P:(c + 1) * P] for c in range(n)])

                idx = [i for i, st in enumerate(PROJ) if st[0] == l]
                for i in idx:
                    _, u, t = PROJ[i]
                    slot = weights(("in", l, u))
                    width = UCOL[u][1]
                    w = ring[:, slot, 0:KC * width].rearrange("p (k n) -> p k n", k=KC)
                    if i - 4 >= idx[0]:
                        posted(i - 4)
                    for k in range(KC):
                        ins = pe.matmul(S[:, i % 4, 0:width], hT[:, k, t * P:(t + 1) * P], w[:, k, :],
                                        start=(k == 0), stop=(k == KC - 1))
                    ins.then_inc(s["proj_done"], 1)
                    if i > idx[0] and PROJ[i - 1][1] != "va":
                        tr(PROJ[i - 1])
                tr(PROJ[idx[-1]])

                trs = sorted(tix[("tr",) + st] for st in TR if st[0] == l)[-2:]
                for k in trs:
                    pe.wait_ge(t_free[k % 2], k // 2 + 1)
                for eng in (True, False):
                    pe.wait_ge(s["post_dve" if eng else "post_act"], len([st for st in POST[eng] if st[0] <= l]))
                units = [n for n, u in enumerate(ATT) if u[0] == l]

                def scores(n):
                    _, qt, kind, j = ATT[n]
                    k0 = 0 if qt < LT else SEQ
                    nkey = TOK - k0
                    q = slice(qt * P, (qt + 1) * P)
                    biased = kind == "gqa" and qt < LT
                    for pair in (0, 1):
                        if n > units[0]:
                            pe.wait_ge(s["exps_done"], 2 * n - 1 + pair)
                        for b in (2 * pair, 2 * pair + 1):
                            r = slice(64 * (b % 2), 64 * (b % 2) + 64)
                            if kind == "diff":
                                c = 2 * j + b // 2
                                lhs, rhs = qaT[r, c, q], kaT[r, c, k0:TOK]
                            else:
                                lhs, rhs = qbT[r, 2 * j + b // 2, q], kbT[r, j, k0:TOK]
                            ins = pe.matmul(S[:, b, 0:nkey], lhs, rhs, start=True, stop=not biased)
                        if biased:
                            blk = (1 - qt) * P
                            for b in (2 * pair, 2 * pair + 1):
                                ins = pe.matmul(S[:, b, blk:blk + P], ident, cst[:, C_MB + P * qt:C_MB + P * qt + P],
                                                start=False, stop=True)
                        ins.then_inc(s["scores_done"], 1)

                def heads(n):
                    _, qt, kind, j = ATT[n]
                    t0 = 0 if qt < LT else LT
                    nk = TT - t0
                    nh = heads_in[kind]

                    def flip(c):
                        if kind == "diff":
                            pe.wait_ge(s["norm_done"], 2 * diffs[n] + c + 1)
                        else:
                            pe.wait_ge(s["exps_done"], 2 * n + 1 + c // 2)
                        row = 2 * c if kind == "diff" else c
                        transposes(("att", n, c), [Pm[:, row, kb * P:(kb + 1) * P] for kb in range(nk)])

                    def product(c):
                        taken(("att", n, c))
                        if c == 0 and n:
                            pe.wait_ge(s["o_out"], n)
                        for kb in range(nk):
                            if kind == "diff":
                                h = 2 * j + c
                                out, v = O[:, 128 * c:128 * c + 128], Va[:, t0 + kb, 128 * h:128 * h + 128]
                            else:
                                out, v = O[:, 64 * c:64 * c + 64], Vb[:, t0 + kb, 64 * j:64 * j + 64]
                            ins = pe.matmul(out, PT[:, c, kb, :], v, start=(kb == 0), stop=(kb == nk - 1))
                        return ins

                    flip(0)
                    for c in range(nh):
                        if c + 1 < nh:
                            flip(c + 1)
                        ins = product(c)
                    ins.then_inc(s["pv_done"], 1)

                diffs, d = {}, 0
                for n, u in enumerate(ATT):
                    diffs[n] = d
                    d += u[2] == "diff"

                def mixT(qt):
                    pe.wait_ge(s["mix_ready"], base + qt + 1)
                    for h in (0, 1):
                        transposes(("mix", l, qt, h), [mix[:, (4 * h + c) * P:(4 * h + c + 1) * P] for c in range(4)])

                scores(units[0])
                for i, n in enumerate(units):
                    if i + 1 < len(units):
                        scores(n + 1)
                    heads(n)
                    for x in ada_at[n]:
                        ada(x)
                    if i % 4 == 0 and i:
                        mixT(ATT[n][1] - 1)
                mixT(qtiles[l][-1])

                slots = [weights(("out", l, n)) for n in (0, 1)]

                def out_proj(t):
                    for n in range(2):
                        w = WOUT.index((l, t, n))
                        if t == qtiles[l][0] and n == 0:
                            pe.wait_ge(s["exps_done"], 2 * units[-1] + 2)
                        if w - 4 >= WOUT.index((l, 0, 0)):
                            pe.wait_ge(s["wout_out"], w - 3)
                        if n == 0:
                            taken(("mix", l, t, 0))
                            taken(("mix", l, t, 1))
                        wv = slot_view(slots[n], KC)
                        for k in range(KC):
                            ins = pe.matmul(S[:, w % 4, :], hT[:, k, t * P:(t + 1) * P], wv[:, k, :],
                                            start=(k == 0), stop=(k == KC - 1))
                        ins.then_inc(s["wout_done"], 1)

                def logits(i, t):
                    for h in (0, 1):
                        pe.wait_ge(s["h_ready"], 2 * (base + i) + h + 1)
                        transposes(("rt", l, t, h), [hb[t][:, (4 * h + c) * P:(4 * h + c + 1) * P] for c in range(4)])
                    for k in range(KC):
                        if k % 4 == 0:
                            taken(("rt", l, t, k // 4))
                        ins = pe.matmul(AUX[:, t * NE:(t + 1) * NE], hTs[:, k, :], wr[:, k, :], start=(k == 0), stop=(k == KC - 1))
                    ins.then_inc(s["logits_done"], 1)

                pe.wait_ge(s["ada_out"], rest[l][-1] + 1)
                if l == 0:
                    pe.wait_ge(s["router_in"], 16)
                out_proj(0)
                for i, t in enumerate(qtiles[l]):
                    if i + 1 < nt:
                        out_proj(t + 1)
                    logits(i, t)

                pe.wait_ge(s["mask_ready"], l + 1)
                pe.wait_ge(s["sig_done"], l + 1)
                for t in range(nt):
                    for p_ in range(t + 1):
                        pe.matmul(AUX[:, 128 + t * NE:128 + (t + 1) * NE], tri_b if p_ == t else one_b,
                                  mask_b[:, p_ * NE:(p_ + 1) * NE], start=(p_ == 0), stop=(p_ == t))
                for p_ in range(nt):
                    ins = pe.matmul(AUX[:, 256:256 + NE], one_b, mask_b[:, p_ * NE:(p_ + 1) * NE],
                                    start=(p_ == 0), stop=(p_ == nt - 1))
                ins.then_inc(s["ranks_done"], 1)

                firsts = (NE + 1) * l

                def flip_tokens(buf, bank, fetched, count, flipped):
                    pe.wait_ge(s[fetched], count)
                    for j in range(4):
                        ins = pe.transpose(bank[:, j * P:(j + 1) * P], xg[:, buf, j * P:(j + 1) * P], ident)
                    ins.then_inc(s[flipped], 1)

                def flip_more():
                    pe.reg_mov(emptied, pe.snap(n_more, min_val=0, max_val=64))
                    pe.reg_add(n_more, n_more, 1)
                    pe.reg_mov(have, 16 * pe.snap(n_more, min_val=0, max_val=64))
                    pe.wait_ge(s["counts_ready"], l + 1)
                    pe.wait_ge(s["more_ready"], emptied)
                    flip_tokens(2, T[1], "more_fetched", have, "more_flipped")

                def load_wide(e):
                    pe.reg_mov(wide, pe.value_load(nwide[0:1, l, e], min_val=0, max_val=MAXW))

                def item(half, pair, is_wide, first):
                    part = [slot_view(3 * half + i, 4 if i == 2 else 8) for i in range(3)]
                    full0 = [where[("e", l, half, i)][1] for i in range(3)]
                    g = pe.snap(n_items, min_val=0, max_val=64)
                    pe.reg_mov(have, 2 * pair + (firsts + half + 1))
                    pe.wait_ge(s["counts_ready"], l + 1)
                    pe.wait_ge(s["first_ready"], have)
                    if is_wide:
                        pe.wait_ge(s["more_ready"], n_more)
                    for i, done in ((0, "up1_done"), (1, "up3_done")):
                        if first:
                            pe.wait_ge(slot_full[3 * half + i], 16 * pair + full0[i])
                        for k in range(KC):
                            if is_wide:
                                ins = pe.matmul(S[:, i, :], xT[:, half, k % 4, k // 4, :], part[i][:, k, :],
                                                start=(k == 0), stop=(k == KC - 1))
                                continue
                            for h in range(2):
                                ins = pe.matmul(S[64 * h:64 * h + 64, i, 0:256], xT[:, half, k % 4, k // 4, 0:64],
                                                part[i][:, k, h * 256:h * 256 + 256], start=(k == 0), stop=(k == KC - 1))
                        ins.then_inc(s[done], 1)
                    if first:
                        gone = (NE // 2 + 1 if half else NE // 2) * l
                        flip_tokens(1 - half, O, f"first_fetched{1 - half}", 16 * pair + 16 * (gone + 1 + half), "first_flipped")
                        load_wide(ds(2 * pair + (half + 1), 1))
                        with pe.If_ne(wide, 0):
                            flip_more()
                    g = pe.snap(n_items, min_val=0, max_val=64)
                    pe.reg_mov(now, g + 1)
                    nc_ = 2 if is_wide else 1
                    for c, (made, done) in enumerate((("ua_done", "uta_done"), ("ub_done", "utb_done"))):
                        pe.wait_ge(s["counts_ready"], l + 1)
                        pe.wait_ge(s[made], now)
                        for b in range(nc_):
                            at = (nc_ * c + b) * P
                            ins = pe.transpose(ut_bank[c][:, b * P:(b + 1) * P], u_s[:, at:at + P], ident)
                        ins.then_inc(s[done], 1)
                    pe.wait_ge(s["counts_ready"], l + 1)
                    pe.wait_ge(s["ea_done"], now)
                    pe.wait_ge(s["y_out"], now)
                    if first:
                        pe.wait_ge(slot_full[3 * half + 2], 16 * pair + full0[2])
                    for c in range(2 if not is_wide else 4):
                        if c == (2 if is_wide else 1):
                            pe.wait_ge(s["eb_done"], now)
                        if is_wide:
                            for h, bank in enumerate((S[:, 3, :], T[0][:, :])):
                                ins = pe.matmul(bank, uT[:, c, :], part[2][:, c, h * 512:h * 512 + 512],
                                                start=(c == 0), stop=(c == 3))
                            continue
                        for hf in range(2):
                            for h in range(2):
                                ins = pe.matmul(S[64 * h:64 * h + 64, 3, :], uT[:, c, 64 * hf:64 * hf + 64],
                                                part[2][:, 2 * hf + c, h * 512:h * 512 + 512],
                                                start=(c == 0 and hf == 0), stop=(c == 1 and hf == 1))
                    ins.then_inc(s["down_done"], 1)
                    pe.reg_add(n_items, n_items, 1)

                flip_tokens(0, O, "first_fetched0", 16 * ((NE // 2 + 1) * l + 1), "first_flipped")
                pe.wait_ge(s["counts_ready"], l + 1)
                load_wide(slice(0, 1))
                with pe.If_ne(wide, 0):
                    flip_more()
                with pe.Fori(0, NE // 2) as pair:
                    for half in range(2):
                        n = pe.value_load(ntile[0:1, l, ds(2 * pair + half, 1)], min_val=1, max_val=MAXW)
                        pe.reg_mov(tiles, n)
                        pe.reg_mov(own_wide, pe.value_load(nwide[0:1, l, ds(2 * pair + half, 1)], min_val=0, max_val=MAXW))
                        with pe.If_eq(own_wide, 0):
                            item(half, pair, False, True)
                        with pe.If_ne(own_wide, 0):
                            item(half, pair, True, True)
                            with pe.If_ne(tiles, 1), pe.Fori(1, n):
                                for b in range(2):
                                    flip_more()
                                item(half, pair, True, False)
                g = pe.snap(n_items, min_val=1, max_val=64)
                pe.reg_mov(last_y, g + 1)
                pe.wait_ge(s["counts_ready"], l + 1)
                pe.wait_ge(s["first_ready"], firsts + NE + 1)
                pe.wait_ge(s["y_out"], last_y)


_INS = ["x", "c", "ctx", "c_ctx", "w_ada", "b_ada", "norm_attn", "norm_ffn", "w_in", "w_out", "lambda_qk",
        "subln", "sink", "w_router", "b_router", "w1", "w3", "w2", "norm_final"]


def kernel(**inputs):
    import concourse.bacc as bacc
    from concourse.bass_utils import run_bass_kernel_spmd

    nc = bacc.Bacc("TRN2", target_bir_lowering=False, num_devices=1)
    arrays = {f"in_{n}": np.ascontiguousarray(inputs[n]) for n in _INS}
    arrays["in_consts"] = constants()
    aps = {n[3:]: nc.dram_tensor(n, v.shape, mybir.dt.from_np(v.dtype), kind="ExternalInput").ap()
           for n, v in arrays.items()}
    aps["out"] = nc.dram_tensor("out", (1, SEQ, DM), mybir.dt.float32, kind="ExternalOutput").ap()
    build(nc, aps)
    r = run_bass_kernel_spmd(nc, [arrays], core_ids=[0])
    return r.results[0]["out"]
```
